# Optimizing a Trainium2 kernel written in Bass

```python
import math
import jax, jax.numpy as jnp
from jax import lax
import numpy as np

D_MODEL = 2048
BATCH = 1
SEQ = 256
DEPTH = 1

HEAD_DIM = 64
N_MIXERS = 4
HEADS_PER_MIXER = 8
GROUP_WIDTH = HEADS_PER_MIXER * HEAD_DIM
MIX_WIDTH = N_MIXERS * GROUP_WIDTH
N_HEADS_TOTAL = N_MIXERS * HEADS_PER_MIXER
SCALE = HEAD_DIM ** -0.5

REL_BUCKETS = 32
REL_MAX_DIST = 2048

DILATED_CONFIGS = ((128, 1), (512, 4), (2048, 16))

SWA_WINDOW = 128
SWA_KV_HEADS = 2

MOBA_BLOCK = 256
MOBA_TOPK = 3

NSA_KV_HEADS = 2
NSA_CMP_BLOCK = 32
NSA_CMP_STRIDE = 16
NSA_CMP_HIDDEN = 128
NSA_SLC_BLOCK = 64
NSA_SLC_TOPN = 16
NSA_WINDOW = 512

BAND_BLOCK = 128
QUERY_CHUNK = 64

N_EXPERTS = 16
N_EXPERT_GROUPS = 4
TOPK_GROUPS = 1
TOPK_EXPERTS = 2
D_EXPERT = 512

NORM_EPS = 1e-6
NEG_INF = -1e30

KV_B = SWA_KV_HEADS * HEAD_DIM
KV_D = NSA_KV_HEADS * HEAD_DIM
IN_SIZES = (GROUP_WIDTH, GROUP_WIDTH, GROUP_WIDTH,
            GROUP_WIDTH, KV_B, KV_B,
            GROUP_WIDTH, GROUP_WIDTH, GROUP_WIDTH,
            GROUP_WIDTH, KV_D, KV_D, KV_D, KV_D, KV_D, KV_D, HEADS_PER_MIXER * 3)
IN_COLS = sum(IN_SIZES)


def rmsnorm(x, g):
    xf = x.astype(jnp.float32)
    ms = jnp.mean(xf * xf, axis=-1, keepdims=True)
    return (xf * lax.rsqrt(ms + NORM_EPS)).astype(x.dtype) * g

def t5_bucket(dist):
    dist = jnp.maximum(dist, 0)
    max_exact = REL_BUCKETS // 2
    large = max_exact + (jnp.log(jnp.maximum(dist, 1).astype(jnp.float32) / max_exact)
                         / math.log(REL_MAX_DIST / max_exact) * (REL_BUCKETS - max_exact)).astype(jnp.int32)
    large = jnp.minimum(large, REL_BUCKETS - 1)
    return jnp.where(dist < max_exact, dist, large)

def masked_softmax(s, mask, sink=None):
    s = jnp.where(mask, s, NEG_INF)
    m = jnp.max(s, axis=-1, keepdims=True)
    if sink is not None:
        m = jnp.maximum(m, sink)
    e = jnp.where(mask, jnp.exp(s - m), 0.0)
    den = jnp.sum(e, axis=-1, keepdims=True)
    if sink is not None:
        den = den + jnp.exp(sink - m)
    den = jnp.maximum(den, jnp.finfo(jnp.float32).tiny)
    return e / den, (m + jnp.log(den))[..., 0]

def banded_attention(q, k, v, max_dist, tab, dist_scale, sink=None):
    b, hk, g, L, hd = q.shape
    nblk = -(-L // BAND_BLOCK)
    Lp = nblk * BAND_BLOCK
    nprev = -(-max_dist // BAND_BLOCK)
    nk = (nprev + 1) * BAND_BLOCK
    q = jnp.pad(q, ((0, 0), (0, 0), (0, 0), (0, Lp - L), (0, 0)))
    pad_kv = ((0, 0), (0, 0), (nprev * BAND_BLOCK, Lp - L), (0, 0))
    k = jnp.pad(k, pad_kv)
    v = jnp.pad(v, pad_kv)
    kidx = np.arange(nblk)[:, None] * BAND_BLOCK + np.arange(nk)[None, :]
    kb = k[:, :, kidx]
    vb = v[:, :, kidx]
    qb = q.reshape(b, hk, g, nblk, BAND_BLOCK, hd)
    rel = np.arange(BAND_BLOCK)[:, None] + nprev * BAND_BLOCK - np.arange(nk)[None, :]
    kpos = np.arange(nblk)[:, None, None] * BAND_BLOCK - nprev * BAND_BLOCK + np.arange(nk)[None, None, :]
    mask = (rel >= 0) & (rel <= max_dist) & (kpos >= 0)
    bias = tab.astype(jnp.float32)[:, :, t5_bucket(jnp.asarray(rel * dist_scale))]
    s = jnp.einsum('bhgnqd,bhnkd->bhgnqk', qb, kb).astype(jnp.float32) * SCALE + bias[None, :, :, None]
    if sink is not None:
        sink = sink.astype(jnp.float32)[None, :, :, None, None, None]
    p, lse = masked_softmax(s, mask, sink)
    o = jnp.einsum('bhgnqk,bhnkd->bhgnqd', p.astype(v.dtype), vb).reshape(b, hk, g, Lp, hd)[:, :, :, :L]
    return o, lse.reshape(b, hk, g, Lp)[:, :, :, :L]

def dilated_attention(q, k, v, tab):
    b, h, s, hd = q.shape
    outs, lses = [], []
    for window, r in DILATED_CONFIGS:
        def strided(t):
            return t.reshape(b, h, s // r, r, hd).transpose(0, 3, 1, 2, 4).reshape(b * r, h, s // r, hd)
        o, lse = banded_attention(strided(q)[:, :, None], strided(k), strided(v), window // r, tab[:, None], r)
        outs.append(o[:, :, 0].reshape(b, r, h, s // r, hd).transpose(0, 2, 3, 1, 4).reshape(b, h, s, hd))
        lses.append(lse[:, :, 0].reshape(b, r, h, s // r).transpose(0, 2, 3, 1).reshape(b, h, s))
    w = jax.nn.softmax(jnp.stack(lses, axis=0), axis=0)
    o = w[0][..., None] * outs[0] + w[1][..., None] * outs[1] + w[2][..., None] * outs[2]
    return o.astype(q.dtype)

def moba_attention(q, k, v, tab):
    b, h, s, hd = q.shape
    nb = -(-s // MOBA_BLOCK)
    sp = nb * MOBA_BLOCK
    pad = ((0, 0), (0, 0), (0, sp - s), (0, 0))
    q, k, v = jnp.pad(q, pad), jnp.pad(k, pad), jnp.pad(v, pad)
    kb = k.reshape(b, h, nb, MOBA_BLOCK, hd)
    vb = v.reshape(b, h, nb, MOBA_BLOCK, hd)
    kmean = jnp.mean(kb, axis=-2)
    nch = sp // QUERY_CHUNK
    qc = jnp.moveaxis(q.reshape(b, h, nch, QUERY_CHUNK, hd), 2, 0)
    starts = jnp.arange(nch, dtype=jnp.int32) * QUERY_CHUNK
    ksel = min(MOBA_TOPK, nb)
    bi = jnp.arange(b)[:, None, None, None]
    hi = jnp.arange(h)[None, :, None, None]
    tabf = tab.astype(jnp.float32)

    def chunk(args):
        qi, start = args
        pos = start + jnp.arange(QUERY_CHUNK, dtype=jnp.int32)
        cur = start // MOBA_BLOCK
        gate = jnp.einsum('bhqd,bhnd->bhqn', qi, kmean).astype(jnp.float32)
        gate = jnp.where(jnp.arange(nb) < cur, gate, NEG_INF)
        _, sel = lax.top_k(gate, ksel)
        ks = kb[bi, hi, sel]
        vs = vb[bi, hi, sel]
        s_sel = jnp.einsum('bhqd,bhqnkd->bhqnk', qi, ks).reshape(b, h, QUERY_CHUNK, ksel * MOBA_BLOCK)
        kpos_sel = (sel[..., None] * MOBA_BLOCK + jnp.arange(MOBA_BLOCK)).reshape(b, h, QUERY_CHUNK, ksel * MOBA_BLOCK)
        mask_sel = jnp.repeat(sel < cur, MOBA_BLOCK, axis=-1)
        ko = lax.dynamic_index_in_dim(kb, cur, axis=2, keepdims=False)
        vo = lax.dynamic_index_in_dim(vb, cur, axis=2, keepdims=False)
        s_own = jnp.einsum('bhqd,bhkd->bhqk', qi, ko)
        kpos_own = cur * MOBA_BLOCK + jnp.arange(MOBA_BLOCK, dtype=jnp.int32)
        shp = (b, h, QUERY_CHUNK, MOBA_BLOCK)
        mask_own = jnp.broadcast_to(kpos_own[None, :] <= pos[:, None], shp)
        kpos = jnp.concatenate([kpos_sel, jnp.broadcast_to(kpos_own, shp)], axis=-1)
        mask = jnp.concatenate([mask_sel, mask_own], axis=-1)
        bias = tabf[hi, t5_bucket(pos[:, None] - kpos)]
        sc = jnp.concatenate([s_sel, s_own], axis=-1).astype(jnp.float32) * SCALE + bias
        p, _ = masked_softmax(sc, mask)
        p = p.astype(v.dtype)
        o = (jnp.einsum('bhqnk,bhqnkd->bhqd', p[..., :ksel * MOBA_BLOCK].reshape(b, h, QUERY_CHUNK, ksel, MOBA_BLOCK), vs)
             + jnp.einsum('bhqk,bhkd->bhqd', p[..., ksel * MOBA_BLOCK:], vo))
        return o

    o = lax.map(chunk, (qc, starts))
    return jnp.moveaxis(o, 0, 2).reshape(b, h, sp, hd)[:, :, :s]

def nsa_attention(q, k_cmp, v_cmp, k_slc, v_slc, k_win, v_win, gates, pe_k, pe_v, w1k, w2k, w1v, w2v, tab):
    b, hk, g, s, hd = q.shape
    n_cmp = (s - NSA_CMP_BLOCK) // NSA_CMP_STRIDE + 1
    cidx = np.arange(n_cmp)[:, None] * NSA_CMP_STRIDE + np.arange(NSA_CMP_BLOCK)[None, :]

    def compress(t, pe, w1, w2):
        blk = (t[:, :, cidx] + pe).reshape(b, hk, n_cmp, NSA_CMP_BLOCK * hd)
        return jax.nn.gelu(blk @ w1) @ w2

    kc = compress(k_cmp, pe_k, w1k, w2k)
    vc = compress(v_cmp, pe_v, w1v, w2v)
    pos = np.arange(s)
    mask_c = (np.arange(n_cmp) * NSA_CMP_STRIDE + NSA_CMP_BLOCK - 1)[None, :] <= pos[:, None]
    s_c = jnp.einsum('bhgqd,bhnd->bhgqn', q, kc).astype(jnp.float32) * SCALE
    p_c, _ = masked_softmax(s_c, mask_c)
    o_cmp = jnp.einsum('bhgqn,bhnd->bhgqd', p_c.astype(vc.dtype), vc)
    n_slc = s // NSA_SLC_BLOCK
    c_start = np.arange(n_cmp) * NSA_CMP_STRIDE
    j_start = np.arange(n_slc) * NSA_SLC_BLOCK
    overlap = ((c_start[:, None] < j_start[None, :] + NSA_SLC_BLOCK)
               & (c_start[:, None] + NSA_CMP_BLOCK > j_start[None, :])).astype(np.float32)
    imp = jnp.einsum('bhgqn,nj->bhqj', p_c, jnp.asarray(overlap))
    cur = pos // NSA_SLC_BLOCK
    jj = np.arange(n_slc)[None, :]
    forced = (jj == 0) | (jj == cur[:, None]) | (jj == cur[:, None] - 1)
    imp = jnp.where(forced, -NEG_INF, jnp.where(jj <= cur[:, None], imp, NEG_INF))
    n_sel = min(NSA_SLC_TOPN, n_slc)
    _, sel = lax.top_k(imp, n_sel)
    ksb = k_slc.reshape(b, hk, n_slc, NSA_SLC_BLOCK, hd)
    vsb = v_slc.reshape(b, hk, n_slc, NSA_SLC_BLOCK, hd)
    nch = s // QUERY_CHUNK
    qc = jnp.moveaxis(q.reshape(b, hk, g, nch, QUERY_CHUNK, hd), 3, 0)
    selc = jnp.moveaxis(sel.reshape(b, hk, nch, QUERY_CHUNK, n_sel), 2, 0)
    starts = jnp.arange(nch, dtype=jnp.int32) * QUERY_CHUNK
    bi = jnp.arange(b)[:, None, None, None]
    hi = jnp.arange(hk)[None, :, None, None]
    tab_t = tab.astype(jnp.float32).transpose(0, 2, 1)

    def chunk(args):
        qi, si, start = args
        pos_q = start + jnp.arange(QUERY_CHUNK, dtype=jnp.int32)
        kk = ksb[bi, hi, si]
        vv = vsb[bi, hi, si]
        nkeys = n_sel * NSA_SLC_BLOCK
        sc = jnp.einsum('bhgqd,bhqnkd->bhgqnk', qi, kk).reshape(b, hk, g, QUERY_CHUNK, nkeys).astype(jnp.float32) * SCALE
        kpos = (si[..., None] * NSA_SLC_BLOCK + jnp.arange(NSA_SLC_BLOCK)).reshape(b, hk, QUERY_CHUNK, nkeys)
        mask = (kpos <= pos_q[:, None])[:, :, None]
        bias = jnp.moveaxis(tab_t[hi, t5_bucket(pos_q[:, None] - kpos)], -1, 2)
        p, _ = masked_softmax(sc + bias, mask)
        return jnp.einsum('bhgqnk,bhqnkd->bhgqd',
                          p.reshape(b, hk, g, QUERY_CHUNK, n_sel, NSA_SLC_BLOCK).astype(vv.dtype), vv)

    o_slc = jnp.moveaxis(lax.map(chunk, (qc, selc, starts)), 0, 3).reshape(b, hk, g, s, hd)
    o_win, _ = banded_attention(q, k_win, v_win, NSA_WINDOW - 1, tab, 1)
    gates = gates.astype(q.dtype)
    return gates[..., 0:1] * o_cmp + gates[..., 1:2] * o_slc + gates[..., 2:3] * o_win

def _heads(t, n):
    b, s, _ = t.shape
    return t.reshape(b, s, n, HEAD_DIM).transpose(0, 2, 1, 3)

def _seq(o):
    b, n, s, d = o.shape
    return o.transpose(0, 2, 1, 3).reshape(b, s, n * d)

def token_mixer(h, w_in_l, rel_bias, sink_l, pe_k, pe_v, w1k, w2k, w1v, w2v, mix_g, w_out_l):
    b, s, _ = h.shape
    H = HEADS_PER_MIXER
    proj = h @ w_in_l
    offs = [int(o) for o in np.cumsum(IN_SIZES)[:-1]]
    (q_a, k_a, v_a, q_b, k_b, v_b, q_c, k_c, v_c,
     q_d, k_dc, v_dc, k_ds, v_ds, k_dw, v_dw, g_d) = jnp.split(proj, offs, axis=-1)
    tabs = [rel_bias[:, i * H:(i + 1) * H].T for i in range(N_MIXERS)]
    o_a = dilated_attention(_heads(q_a, H), _heads(k_a, H), _heads(v_a, H), tabs[0])
    gb = H // SWA_KV_HEADS
    o_b, _ = banded_attention(_heads(q_b, H).reshape(b, SWA_KV_HEADS, gb, s, HEAD_DIM),
                              _heads(k_b, SWA_KV_HEADS), _heads(v_b, SWA_KV_HEADS),
                              SWA_WINDOW - 1, tabs[1].reshape(SWA_KV_HEADS, gb, REL_BUCKETS), 1,
                              sink_l.reshape(SWA_KV_HEADS, gb))
    o_b = o_b.reshape(b, H, s, HEAD_DIM)
    o_c = moba_attention(_heads(q_c, H), _heads(k_c, H), _heads(v_c, H), tabs[2])
    gd = H // NSA_KV_HEADS
    gates = jax.nn.sigmoid(g_d.reshape(b, s, H, 3)).transpose(0, 2, 1, 3).reshape(b, NSA_KV_HEADS, gd, s, 3)
    kvh = lambda t: _heads(t, NSA_KV_HEADS)
    o_d = nsa_attention(_heads(q_d, H).reshape(b, NSA_KV_HEADS, gd, s, HEAD_DIM),
                        kvh(k_dc), kvh(v_dc), kvh(k_ds), kvh(v_ds), kvh(k_dw), kvh(v_dw), gates,
                        pe_k, pe_v, w1k, w2k, w1v, w2v, tabs[3].reshape(NSA_KV_HEADS, gd, REL_BUCKETS))
    o_d = o_d.reshape(b, H, s, HEAD_DIM)
    outs = [rmsnorm(_seq(o), mix_g[i]) for i, o in enumerate((o_a, o_b, o_c, o_d))]
    return jnp.concatenate(outs, axis=-1) @ w_out_l

def moe_ffn(h, router_w, router_bias, w_gate, w_up, w_down):
    b, s, d = h.shape
    t = h.reshape(b * s, d)
    aff = jax.nn.sigmoid((t @ router_w).astype(jnp.float32))
    score = aff + router_bias.astype(jnp.float32)
    per_group = N_EXPERTS // N_EXPERT_GROUPS
    group_score = lax.top_k(score.reshape(-1, N_EXPERT_GROUPS, per_group), 2)[0].sum(-1)
    _, gsel = lax.top_k(group_score, TOPK_GROUPS)
    gmask = jnp.any(jnp.arange(N_EXPERT_GROUPS)[None, None, :] == gsel[..., None], axis=1)
    emask = jnp.repeat(gmask, per_group, axis=-1)
    _, esel = lax.top_k(jnp.where(emask, score, NEG_INF), TOPK_EXPERTS)
    w = jnp.take_along_axis(aff, esel, axis=-1)
    w = w / jnp.sum(w, axis=-1, keepdims=True)
    combine = jnp.sum((esel[..., None] == jnp.arange(N_EXPERTS)) * w[..., None], axis=1).astype(t.dtype)
    y = jnp.zeros_like(t)
    for e in range(N_EXPERTS):
        he = jax.nn.silu(t @ w_gate[e]) * (t @ w_up[e])
        y = y + combine[:, e:e + 1] * (he @ w_down[e])
    return y.reshape(b, s, d)

def first_inputs(seed: int = 0) -> dict:
    key = jax.random.key(seed)
    ks = jax.random.split(key, 24)
    f32 = jnp.float32

    def nrm(k, shape, sc):
        return jax.random.normal(k, shape, f32) * sc

    D, E, F = D_MODEL, N_EXPERTS, D_EXPERT
    cin = NSA_CMP_BLOCK * HEAD_DIM
    return {
        "x": nrm(ks[0], (BATCH, SEQ, D), 1.0),
        "c": nrm(ks[1], (BATCH, D), 1.0),
        "rel_bias": nrm(ks[2], (REL_BUCKETS, N_HEADS_TOTAL), 0.5),
        "router_w": nrm(ks[3], (D, E), D ** -0.5),
        "router_bias": nrm(ks[4], (E,), 0.01),
        "norm1_g": 1.0 + nrm(ks[5], (DEPTH, D), 0.02),
        "norm2_g": 1.0 + nrm(ks[6], (DEPTH, D), 0.02),
        "ada_w": nrm(ks[7], (DEPTH, D, 6 * D), 0.3 * D ** -0.5),
        "ada_b": nrm(ks[8], (DEPTH, 6 * D), 0.02),
        "w_in": nrm(ks[9], (DEPTH, D, IN_COLS), D ** -0.5),
        "nsa_pe_k": nrm(ks[10], (DEPTH, NSA_CMP_BLOCK, HEAD_DIM), 0.5),
        "nsa_pe_v": nrm(ks[11], (DEPTH, NSA_CMP_BLOCK, HEAD_DIM), 0.5),
        "nsa_cmp_w1_k": nrm(ks[12], (DEPTH, cin, NSA_CMP_HIDDEN), cin ** -0.5),
        "nsa_cmp_w2_k": nrm(ks[13], (DEPTH, NSA_CMP_HIDDEN, HEAD_DIM), NSA_CMP_HIDDEN ** -0.5),
        "nsa_cmp_w1_v": nrm(ks[14], (DEPTH, cin, NSA_CMP_HIDDEN), cin ** -0.5),
        "nsa_cmp_w2_v": nrm(ks[15], (DEPTH, NSA_CMP_HIDDEN, HEAD_DIM), NSA_CMP_HIDDEN ** -0.5),
        "sinks": nrm(ks[16], (DEPTH, HEADS_PER_MIXER), 0.5),
        "mix_norm_g": 1.0 + nrm(ks[17], (DEPTH, N_MIXERS, GROUP_WIDTH), 0.02),
        "w_out": nrm(ks[18], (DEPTH, MIX_WIDTH, D), MIX_WIDTH ** -0.5),
        "exp_w_gate": nrm(ks[19], (DEPTH, E, D, F), D ** -0.5),
        "exp_w_up": nrm(ks[20], (DEPTH, E, D, F), D ** -0.5),
        "exp_w_down": nrm(ks[21], (DEPTH, E, F, D), F ** -0.5),
        "final_g": 1.0 + nrm(ks[22], (D,), 0.02),
    }

def first_block(x, c, rel_bias, router_w, router_bias, norm1_g, norm2_g, ada_w, ada_b, w_in,
              nsa_pe_k, nsa_pe_v, nsa_cmp_w1_k, nsa_cmp_w2_k, nsa_cmp_w1_v, nsa_cmp_w2_v,
              sinks, mix_norm_g, w_out, exp_w_gate, exp_w_up, exp_w_down, final_g):
    c_act = jax.nn.silu(c)
    for l in range(DEPTH):
        mod = c_act @ ada_w[l] + ada_b[l]
        sh1, sc1, g1, sh2, sc2, g2 = jnp.split(mod, 6, axis=-1)
        h = rmsnorm(x, norm1_g[l]) * (1.0 + sc1[:, None]) + sh1[:, None]
        x = x + g1[:, None] * token_mixer(h, w_in[l], rel_bias, sinks[l], nsa_pe_k[l], nsa_pe_v[l],
                                          nsa_cmp_w1_k[l], nsa_cmp_w2_k[l], nsa_cmp_w1_v[l], nsa_cmp_w2_v[l],
                                          mix_norm_g[l], w_out[l])
        h = rmsnorm(x, norm2_g[l]) * (1.0 + sc2[:, None]) + sh2[:, None]
        x = x + g2[:, None] * moe_ffn(h, router_w, router_bias, exp_w_gate[l], exp_w_up[l], exp_w_down[l])
    return rmsnorm(x, final_g)


D_HYENA = D_MODEL // 2
HYENA_GROUPS = 8
HYENA_ORDER = 2
HYENA_SHORT = 3
FILTER_EMB = 33
FILTER_ORDER = 64
FAST_DECAY = 0.3
SLOW_DECAY = 1.5
DECAY_TARGET = 1e-2
MOD_SHIFT = 0.0
N_DIR = 2
D_SGU = D_MODEL // 2
SGU_HEADS = 8
SGU_HEAD_DIM = D_SGU // SGU_HEADS
CHUNK = 128
N_BRANCH = 2
D_FF = -(-8 * D_MODEL // (3 * 256)) * 256
D_IN = 3 * D_HYENA + 2 * D_SGU + N_BRANCH * D_MODEL
EPS = 1e-6


F32 = jnp.float32

def _rmsnorm(x, g):
    x32 = x.astype(F32)
    y = x32 * lax.rsqrt(jnp.mean(x32 * x32, axis=-1, keepdims=True) + EPS)
    return (y * g.astype(F32)).astype(x.dtype)

def _layernorm(x, g, b):
    x32 = x.astype(F32)
    mu = jnp.mean(x32, axis=-1, keepdims=True)
    var = jnp.mean(jnp.square(x32 - mu), axis=-1, keepdims=True)
    y = (x32 - mu) * lax.rsqrt(var + EPS)
    return (y * g.astype(F32) + b.astype(F32)).astype(x.dtype)

def _hyena_filters(L, w1, b1, w2, b2, w3, b3, freq, w4):
    t = jnp.linspace(0.0, 1.0, L, dtype=F32)[:, None]
    bands = (FILTER_EMB - 1) // 2
    w = 2.0 * math.pi * jnp.arange(L, dtype=F32)[:, None] / L
    f = jnp.linspace(1e-4, bands - 1, bands, dtype=F32)[None, :]
    z = jnp.concatenate([t, jnp.cos(f * w), -jnp.sin(f * w)], axis=-1)
    fr = freq.astype(F32)
    h = jnp.sin(fr * (z @ w1.astype(F32) + b1.astype(F32)))
    h = jnp.sin(fr * (h @ w2.astype(F32) + b2.astype(F32)))
    h = jnp.sin(fr * (h @ w3.astype(F32) + b3.astype(F32)))
    h = (h @ w4.astype(F32)).reshape(L, N_DIR, HYENA_ORDER, D_HYENA)
    max_decay = math.log(DECAY_TARGET) / FAST_DECAY
    min_decay = math.log(DECAY_TARGET) / SLOW_DECAY
    deltas = jnp.linspace(min_decay, max_decay, D_HYENA, dtype=F32)
    decay = jnp.exp(-t * jnp.abs(deltas))
    h = h * (decay + MOD_SHIFT)[:, None, None, :]
    h_fwd, h_bwd = h[:, 0], h[:, 1]
    k = jnp.concatenate([h_fwd, jnp.zeros((1, HYENA_ORDER, D_HYENA), F32), h_bwd[:0:-1]], axis=0)
    k = k / jnp.sum(jnp.abs(k), axis=0, keepdims=True)
    return jnp.fft.rfft(k, axis=0)

def _long_conv(z, k_f, bias):
    L = z.shape[1]
    zf = jnp.fft.rfft(z, n=2 * L, axis=1)
    y = jnp.fft.irfft(zf * k_f[None], n=2 * L, axis=1)[:, :L]
    return y + z * bias.astype(F32)

def _hyena_mixer(p, conv_w, conv_b, k_f, bias):
    pp = jnp.pad(p, ((0, 0), (1, 1), (0, 0)))
    p = pp[:, :-2] * conv_w[0] + pp[:, 1:-1] * conv_w[1] + pp[:, 2:] * conv_w[2] + conv_b
    v, x1, x2 = jnp.split(p, 3, axis=-1)
    z = v.astype(F32)
    z = x1.astype(F32) * _long_conv(z, k_f[:, 0], bias[0])
    z = x2.astype(F32) * _long_conv(z, k_f[:, 1], bias[1])
    return z.astype(p.dtype)

def _sgu_mixer(p, ln_g, ln_b, w_s, b_s):
    B, L, _ = p.shape
    u, v = jnp.split(jax.nn.gelu(p, approximate=False), 2, axis=-1)
    v = _layernorm(v, ln_g, ln_b)
    v = v.reshape(B, L // CHUNK, CHUNK, SGU_HEADS, SGU_HEAD_DIM)
    s = jnp.einsum('hpq,bnqhc->bnphc', w_s, v) + b_s.T[None, None, :, :, None]
    return u * s.reshape(B, L, D_SGU)

def second_inputs(seed: int = 0) -> dict:
    key = jax.random.key(seed)
    ks = jax.random.split(key, 32)

    def nrm(k, shape, scale):
        return jax.random.normal(k, shape, F32) * scale

    return {
        "x": nrm(ks[0], (BATCH, SEQ, D_MODEL), 1.0),
        "norm_mix_g": 1.0 + nrm(ks[1], (DEPTH, D_MODEL), 0.01),
        "w_in": nrm(ks[2], (DEPTH, D_MODEL, D_IN), D_MODEL ** -0.5),
        "short_conv_w": nrm(ks[3], (DEPTH, HYENA_SHORT, 3 * D_HYENA), HYENA_SHORT ** -0.5),
        "short_conv_b": nrm(ks[4], (DEPTH, 3 * D_HYENA), 0.02),
        "filt_w1": nrm(ks[5], (DEPTH, FILTER_EMB, FILTER_ORDER), FILTER_EMB ** -0.5),
        "filt_b1": nrm(ks[6], (DEPTH, FILTER_ORDER), 0.1),
        "filt_w2": nrm(ks[7], (DEPTH, FILTER_ORDER, FILTER_ORDER), FILTER_ORDER ** -0.5),
        "filt_b2": nrm(ks[8], (DEPTH, FILTER_ORDER), 0.1),
        "filt_w3": nrm(ks[9], (DEPTH, FILTER_ORDER, FILTER_ORDER), FILTER_ORDER ** -0.5),
        "filt_b3": nrm(ks[10], (DEPTH, FILTER_ORDER), 0.1),
        "filt_freq": 1.0 + nrm(ks[11], (DEPTH, FILTER_ORDER), 0.01),
        "filt_w4": nrm(ks[12], (DEPTH, FILTER_ORDER, N_DIR * HYENA_ORDER * D_HYENA), FILTER_ORDER ** -0.5),
        "hyena_bias": nrm(ks[13], (DEPTH, HYENA_ORDER, D_HYENA), 0.5),
        "sgu_ln_g": 1.0 + nrm(ks[14], (DEPTH, D_SGU), 0.01),
        "sgu_ln_b": nrm(ks[15], (DEPTH, D_SGU), 0.02),
        "sgu_w_s": nrm(ks[16], (DEPTH, SGU_HEADS, CHUNK, CHUNK), CHUNK ** -0.5),
        "sgu_b_s": 1.0 + nrm(ks[17], (DEPTH, SGU_HEADS, CHUNK), 0.01),
        "w_branch_hyena": nrm(ks[18], (DEPTH, D_HYENA, D_MODEL), D_HYENA ** -0.5),
        "w_branch_sgu": nrm(ks[19], (DEPTH, D_SGU, D_MODEL), D_SGU ** -0.5),
        "w_out": nrm(ks[20], (DEPTH, D_MODEL, D_MODEL), D_MODEL ** -0.5),
        "norm_ffn_g": 1.0 + nrm(ks[21], (DEPTH, D_MODEL), 0.01),
        "w_ffn_in": nrm(ks[22], (DEPTH, D_MODEL, 2 * D_FF), D_MODEL ** -0.5),
        "w_ffn_out": nrm(ks[23], (DEPTH, D_FF, D_MODEL), D_FF ** -0.5),
        "norm_final_g": 1.0 + nrm(ks[24], (D_MODEL,), 0.01),
    }

def second_block(x, norm_mix_g, w_in, short_conv_w, short_conv_b, filt_w1, filt_b1, filt_w2, filt_b2,
              filt_w3, filt_b3, filt_freq, filt_w4, hyena_bias, sgu_ln_g, sgu_ln_b, sgu_w_s, sgu_b_s,
              w_branch_hyena, w_branch_sgu, w_out, norm_ffn_g, w_ffn_in, w_ffn_out, norm_final_g):
    L = x.shape[1]
    split_pts = [3 * D_HYENA, 3 * D_HYENA + 2 * D_SGU, 3 * D_HYENA + 2 * D_SGU + D_MODEL]
    for l in range(DEPTH):
        h = _rmsnorm(x, norm_mix_g[l])
        proj = jnp.einsum('bsd,de->bse', h, w_in[l])
        p_hy, p_sgu, g_hy, g_sgu = jnp.split(proj, split_pts, axis=-1)
        k_f = _hyena_filters(L, filt_w1[l], filt_b1[l], filt_w2[l], filt_b2[l],
                             filt_w3[l], filt_b3[l], filt_freq[l], filt_w4[l])
        y_hy = _hyena_mixer(p_hy, short_conv_w[l], short_conv_b[l], k_f, hyena_bias[l])
        y_sgu = _sgu_mixer(p_sgu, sgu_ln_g[l], sgu_ln_b[l], sgu_w_s[l], sgu_b_s[l])
        merged = (jax.nn.sigmoid(g_hy) * jnp.einsum('bsc,cd->bsd', y_hy, w_branch_hyena[l])
                  + jax.nn.sigmoid(g_sgu) * jnp.einsum('bsc,cd->bsd', y_sgu, w_branch_sgu[l]))
        x = x + jnp.einsum('bsd,de->bse', merged, w_out[l])
        h = _rmsnorm(x, norm_ffn_g[l])
        gate, up = jnp.split(jnp.einsum('bsd,df->bsf', h, w_ffn_in[l]), 2, axis=-1)
        x = x + jnp.einsum('bsf,fd->bsd', jax.nn.silu(gate) * up, w_ffn_out[l])
    return _rmsnorm(x, norm_final_g)


_first_inputs = second_inputs


def second_inputs(seed=0):
    import zlib

    import numpy as np

    out = dict(_first_inputs(seed))
    spreads = {}
    factors = {'norm_mix_g': 7.605,
     'short_conv_b': 8.0,
     'filt_b1': 7.577,
     'filt_b2': 7.815,
     'filt_b3': 6.134,
     'filt_freq': 8.0,
     'sgu_ln_g': 8.0,
     'sgu_ln_b': 8.0,
     'sgu_b_s': 8.0,
     'norm_ffn_g': 8.0,
     'norm_final_g': 5.662}
    for name, (base, spread) in spreads.items():
        noise = np.random.default_rng([zlib.crc32(name.encode()), seed]).standard_normal(out[name].shape)
        drawn = base * np.exp(spread * noise) if base else spread * noise
        out[name] = __import__('jax').numpy.asarray(drawn.astype(out[name].dtype))
    for name, factor in factors.items():
        out[name] = (out[name] * factor).astype(out[name].dtype)
    return out


_narrow_inputs = second_inputs


def second_inputs(seed=0):

    out = dict(_narrow_inputs(seed))
    wider = {'sgu_ln_g': 12.0,
     'sgu_ln_b': 8.08,
     'sgu_b_s': 12.0,
     'norm_ffn_g': 9.07,
     'norm_final_g': 6.37}
    for name, times in wider.items():
        mean = out[name].mean()
        out[name] = (mean + times * (out[name] - mean)).astype(out[name].dtype)
    return out


def setup_inputs(seed=0):
    out = dict(first_inputs(seed))
    for name, value in second_inputs(seed + 1).items():
        if name != "x":
            out[name + "_2"] = value
    return out


def reference(
    x, c, rel_bias, router_w, router_bias, norm1_g, norm2_g, ada_w, ada_b, w_in, nsa_pe_k,
    nsa_pe_v, nsa_cmp_w1_k, nsa_cmp_w2_k, nsa_cmp_w1_v, nsa_cmp_w2_v, sinks, mix_norm_g, w_out,
    exp_w_gate, exp_w_up, exp_w_down, final_g, norm_mix_g_2, w_in_2, short_conv_w_2,
    short_conv_b_2, filt_w1_2, filt_b1_2, filt_w2_2, filt_b2_2, filt_w3_2, filt_b3_2,
    filt_freq_2, filt_w4_2, hyena_bias_2, sgu_ln_g_2, sgu_ln_b_2, sgu_w_s_2, sgu_b_s_2,
    w_branch_hyena_2, w_branch_sgu_2, w_out_2, norm_ffn_g_2, w_ffn_in_2, w_ffn_out_2,
    norm_final_g_2,
):
    x = first_block(
        x, c, rel_bias, router_w, router_bias, norm1_g, norm2_g, ada_w, ada_b, w_in, nsa_pe_k,
        nsa_pe_v, nsa_cmp_w1_k, nsa_cmp_w2_k, nsa_cmp_w1_v, nsa_cmp_w2_v, sinks, mix_norm_g,
        w_out, exp_w_gate, exp_w_up, exp_w_down, final_g,
    )
    return second_block(
        x, norm_mix_g_2, w_in_2, short_conv_w_2, short_conv_b_2, filt_w1_2, filt_b1_2,
        filt_w2_2, filt_b2_2, filt_w3_2, filt_b3_2, filt_freq_2, filt_w4_2, hyena_bias_2,
        sgu_ln_g_2, sgu_ln_b_2, sgu_w_s_2, sgu_b_s_2, w_branch_hyena_2, w_branch_sgu_2, w_out_2,
        norm_ffn_g_2, w_ffn_in_2, w_ffn_out_2, norm_final_g_2,
    )


_drawn_inputs = setup_inputs


def setup_inputs(seed=0):
    import zlib

    import numpy as np

    out = dict(_drawn_inputs(seed))
    spreads = {}
    factors = {'norm1_g': 5.647, 'nsa_pe_k': 2.715, 'sinks': 8.0, 'mix_norm_g': 7.234, 'norm2_g': 4.425}
    for name, (base, spread) in spreads.items():
        noise = np.random.default_rng([zlib.crc32(name.encode()), seed]).standard_normal(out[name].shape)
        drawn = base * np.exp(spread * noise) if base else spread * noise
        out[name] = __import__('jax').numpy.asarray(drawn.astype(out[name].dtype))
    for name, factor in factors.items():
        out[name] = (out[name] * factor).astype(out[name].dtype)
    return out
```

```python
import math
from contextlib import ExitStack

import numpy as np
import concourse.bass as bass
from concourse import mybir

F32 = mybir.dt.float32
F32R = mybir.dt.float32r
ACT = mybir.ActivationFunctionType
ALU = mybir.AluOpType
AX = mybir.AxisListType.X

P = 128
T = 256
TH = T // P
D = 2048
DC = D // P
HD = 64
NH = 8
UNIT = 2048
HALF = UNIT // 2
ARENA = 14400
SLOTS = 4
SCALE = HD ** -0.5
EPS = 1e-6
NEG = -1e30
TINY = float(np.finfo(np.float32).tiny)
N_EXP = 16
N_CMP = 15
DF = 5632
CH = 1024
MAGIC = 1.5 * 2 ** 23
PI_IN = 3.1415925
TWO_PI = (6.28125, 0.0019350051879882812, 3.0199159819e-07)

ADA_UNITS = 6 * DC
PHASES = [
    ("a_q", 4), ("a_k", 4), ("a_v", 4), ("c_q", 4), ("c_k", 4), ("c_v", 4), ("small", 8), ("b_q", 4),
    ("d_q", 4), ("mix_out", 16), ("moe", 12 * N_EXP), ("hyena", 24), ("sgu_u", 8), ("sgu_v", 8),
    ("gate_hy", 16), ("branch_hy", 8), ("gate_sgu", 16), ("branch_sgu", 8), ("out2", 16),
    ("ffn_in0", 32), ("ffn_down0", 16), ("ffn_in1", 32), ("ffn_down1", 16), ("ffn_in2", 24), ("ffn_down2", 12),
]
NORMS = [("h1", 16), ("mixA", 4), ("mixC", 4), ("mixB", 4), ("mixD", 4), ("hm", 16), ("x1", 0), ("h2", 16), ("hf", 16), ("y", 0)]


def norm_count(name, kind, n):
    for other, tiles in NORMS:
        if other == name:
            return n
        n += {"sq": 2, "ms": 1, "rt": 1, "xh": 2 * (tiles > 0), "t": tiles // 2, "f": tiles // 4, "hi": tiles // 4,
              "lo": tiles // 4}[kind]


FFN_TILES = (16, 16, 12)
BASE, UNITS = {}, 0
for _name, _n in PHASES:
    BASE[_name] = UNITS
    UNITS += _n
SIZE = dict(PHASES)

COLS, NCOLS = {}, 0
for _name, _n in [("norm1", 16), ("norm2", 16), ("mixg", 16), ("normmix2", 16), ("normffn2", 16),
                  ("ada_b", 96), ("conv_w", 72), ("conv_b", 24), ("fb", 3), ("ffreq", 1)]:
    COLS[_name] = NCOLS
    NCOLS += _n

TAB_ID, TAB_TRI, TAB_CADD, TAB_C01, TAB_FLIP, NTAB = 0, 128, 144, 176, 208, 336


def t5_buckets(dist):
    f = np.float32
    large = 16 + (np.log(np.maximum(dist, 1).astype(f) / f(16)) / f(math.log(2048 / 16)) * f(16)).astype(np.int32)
    return np.where(dist < 16, dist, np.minimum(large, 31))


def shape_tables():
    f = np.float32
    tab = np.zeros((P, NTAB), f)
    tab[:, TAB_ID:TAB_ID + P] = np.eye(P)
    tab[:, TAB_TRI:TAB_TRI + 16] = (np.arange(4)[None, :] < np.arange(4)[:, None]).reshape(1, 16)
    tab[:, TAB_FLIP:TAB_FLIP + P] = np.eye(P)[::-1]
    pos = np.arange(P)[:, None, None] + P * np.arange(TH)[None, :, None]
    seen = (np.arange(16)[None, None, :] * 16 + 31 <= pos) & (np.arange(16) < N_CMP)
    tab[:, TAB_CADD:TAB_CADD + 32] = np.where(seen, 0.0, NEG).reshape(P, 32)
    tab[:, TAB_C01:TAB_C01 + 32] = seen.reshape(P, 32)
    dist = 255 - np.arange(384)
    ok = dist >= 0
    onehot = np.zeros((36, 384), f)
    onehot[t5_buckets(np.maximum(dist, 0))[ok], np.arange(384)[ok]] = 1.0
    times = ok * ((dist <= 128).astype(int) + (dist % 4 == 0) + (dist % 16 == 0))
    onehot[32] = np.where(times > 0, np.log(np.maximum(times, 1)), NEG)
    onehot[33] = np.where(ok & (dist <= 127), 0.0, NEG)
    onehot[34] = onehot[35] = np.where(ok, 0.0, NEG)
    owner = np.zeros((4, 32), f)
    for m in range(4):
        owner[m, 8 * m:8 * m + 8] = 1.0
    n = np.arange(T, dtype=np.float64)
    ang = 2 * math.pi * np.outer(n, n) / (2 * T)
    cos, sin = np.cos(ang), -np.sin(ang)
    alt = (-1.0) ** n
    zs = sin.copy(); zs[:, 0] = alt
    c0 = cos[:, :P].copy(); c0[:, 0] = alt
    ic = cos * 2 / (2 * T); ic[0] = 1 / (2 * T)
    inv_s = sin * 2 / (2 * T); inv_s[0] = alt / (2 * T)
    rows = lambda m: m.reshape(TH, P, -1).transpose(1, 0, 2).reshape(P, -1).astype(f)
    dft_k = np.concatenate([rows(cos), rows(sin), rows(c0)], 1)
    dft_z = np.concatenate([rows(cos), rows(zs), rows(ic), rows(inv_s)], 1)
    t = (np.arange(T, dtype=f) * f(1 / f(T - 1))).astype(f)
    w = f(2 * math.pi) * np.arange(T, dtype=f) / f(T)
    s = np.arange(16, dtype=f) / f(15)
    fr = (f(1e-4) * (f(1) - s) + f(15) * s).astype(f)
    fw = (fr[:, None] * w[None, :]).astype(f).astype(np.float64)
    zt = np.concatenate([t[None], np.cos(fw), -np.sin(fw)], 0).astype(f)
    lo, hi = math.log(1e-2) / 1.5, math.log(1e-2) / 0.3
    dl = np.abs(np.linspace(lo, hi, CH, dtype=f))
    decay = np.exp(-(t[:, None] * dl[None]).astype(f).astype(np.float64)).astype(f)
    decay = decay.reshape(TH, P, 2, 512).transpose(2, 1, 0, 3)
    decay = np.concatenate([decay, decay]).reshape(4, P, 1024)
    return dict(tab=tab, onehot=onehot, owner=owner, dft_k=dft_k, dft_z=dft_z, zt=zt, decay=decay)


class Chain:

    def __init__(self, engine, sem):
        self.engine, self.sem, self.n, self.off = engine, sem, 0, 0

    def __call__(self, instruction):
        self.n += 1
        instruction.then_inc(self.sem, 1)
        self.engine.wait_ge(self.sem, self.n + self.off)

    def enter(self, i, per):
        self.start, self.per, self.off = self.n, per, i * per

    def leave(self, times):
        assert self.n - self.start == self.per, (self.n - self.start, self.per)
        self.n, self.off = self.n + self.per * (times - 1), 0


def two_blocks(nc, d, out):
    with ExitStack() as ctx:
        def sb(name, shape, dt=F32):
            return ctx.enter_context(nc.sbuf_tensor(name, shape, dt))

        raw = sb("raw", [P, SLOTS, UNIT])
        w_hi = sb("w_hi", [P, 4, HALF], F32R)
        w_lo = sb("w_lo", [P, 4, HALF], F32R)
        x = sb("x", [P, TH, D])
        h_hi = sb("h_hi", [P, DC, T], F32R)
        h_lo = sb("h_lo", [P, DC, T], F32R)
        r_hi = sb("r_hi", [P, 16, T], F32R)
        r_lo = sb("r_lo", [P, 16, T], F32R)
        n_hi = sb("n_hi", [P, DC, 24], F32R)
        n_lo = sb("n_lo", [P, DC, 24], F32R)
        cols = sb("cols", [P, NCOLS])
        tab = sb("tab", [P, NTAB])
        ones = sb("ones", [P, P])
        mod = sb("mod", [P, 6 * DC])
        gain = sb("gain", [P, DC])
        stat = sb("stat", [P, 160])
        gates = sb("gates", [P, TH, 24])
        comb = sb("comb", [P, TH, N_EXP])
        arena = sb("arena", [P, ARENA])

        def at(off, *shape, parts=P):
            assert off + int(np.prod(shape)) <= ARENA
            v = arena[0:parts, off:off + int(np.prod(shape))]
            if len(shape) == 2:
                v = v.rearrange("p (a b) -> p a b", a=shape[0])
            if len(shape) == 3:
                v = v.rearrange("p (a b c) -> p a b c", a=shape[0], b=shape[1])
            return v

        ident = tab[:, TAB_ID:TAB_ID + P]
        flip = tab[:, TAB_FLIP:TAB_FLIP + P]

        def col(name, n=1):
            return cols[:, COLS[name]:COLS[name] + n]

        c_row = x[:, 1, :]
        mod_sums = stat[:, 144:148]

        ps = ctx.enter_context(nc.psum_tensor("ps", [P, 8, 512], F32))

        brow = nc.dram_tensor("bias_rows", (32, 384), F32, kind="Internal").ap()
        kf_dram = nc.dram_tensor("filters", (4, P, 5 * 512), F32, kind="Internal").ap()

        sems = {}

        def sem(name):
            if name not in sems:
                sems[name] = ctx.enter_context(nc.semaphore(name))
            return sems[name]

        landed = [sem(f"landed{s}") for s in range(SLOTS)]
        ada_done, hi_ready, lo_ready, half_done = sem("ada_done"), sem("hi_ready"), sem("lo_ready"), sem("half_done")
        mod_ready = sem("mod_ready")

        F_DFT, F_ZT, F_W1, F_W2, F_W3 = 0, 1280, 1536, 1600, 1664
        F_A, F_T, F_R, F_H = 1792, 2048, 2304, 2560
        F_W4, F_DEC, F_HB, F_TAPS, F_ABS, F_RN, F_KO = 2816, 3840, 4864, 5376, 7424, 9472, 9984
        F_RELB, F_ONEH, F_BOUT = 12544, 12576, 12960
        qT, kT, v_a = at(0, 8, T, parts=64), at(2048, 8, T, parts=64), at(4096, TH, 512)
        smk, smv = at(2048, 5, 2, T), at(4608, 3, 2, P)
        toep = at(5376, 8, T)
        mix = at(7424, TH, 512)
        prob, pT = at(9216, 2, 384), at(9984, 2, 384)
        blocks = at(10752, 2, 16 * 30)
        hidc, kc, vc = at(11712, 2, 30), at(11772, 2, N_CMP, parts=64), at(11808, 2, HD, parts=N_CMP)
        cs, cp = at(11936, 8, 2, 16), at(12192, 8, 2, 16)
        cpT = at(12448, 512)
        mixf = at(12960, 4, T)
        mix_junk = at(12960, TH, 512)
        w1v, w2c, peT = at(5376, 16, P), at(13984, 2, HD), at(14112, 2, 32, parts=64)
        w1k = at(0, 16, P)
        xhat, hf = at(0, TH, D), at(4096, DC, T)
        row = at(8192, D)
        diag = at(10240, 2, P)
        acc = at(0, TH, D)
        g_act, hid = at(10496, 2, T), at(11008, 2, T)
        ro = 12000
        cvT = at(0, 24, T)
        seq = at(6144, 3, TH, CH)

        def seq_pair(n):
            c = 2 * n
            return seq[:, c // 8, :, (c % 8) * P:(c % 8 + 2) * P].rearrange("p h (c n) -> p c h n", c=2)

        def bank_pair(n):
            return ps[:, n % 4, :].rearrange("p (c h n) -> p c h n", c=2, h=2)

        kf, dftz = at(0, 5, 512), at(2560, 4, 2, T)
        prods = at(4608, 2, 512)
        yr = at(12288, 4, 512)
        uT, vg, ln_row = at(0, 8, T), at(2048, TH, CH), at(4096, 2, CH)
        wsT, bs = at(6144, 8, P), at(7168, 8, P)
        yf = at(8192, 2, T)
        sg1, sg2 = at(0, DC, T), at(4096, DC, T)
        mf = at(8192, 2, T)

        block = ctx.enter_context(nc.Block())

        def group_base(phase):
            return BASE[phase] // SLOTS

        def run_groups(engine, phase, body, per_iter=1, before=None, after=None):
            gb, n = group_base(phase), SIZE[phase] // SLOTS // per_iter
            final = BASE[phase] + SIZE[phase] == UNITS
            body_n = n - final
            if body_n == 1:
                body(gb, 0, False)
            elif body_n > 1:
                with engine.Fori(0, body_n) as i:
                    if before:
                        before(i)
                    body(gb + per_iter * i, i, False)
                if after:
                    after(body_n)
            if final:
                if before:
                    before(0)
                body(gb + per_iter * (n - 1), n - 1, True)
                if after:
                    after(1)

        @block.sync
        def _(sp):
            first = 0
            for s in range(SLOTS):
                sp.dma_start(raw[:, s, :], d["stream"][s]).then_inc(landed[s], 16)
            sp_units = d["stream"]
            with sp.Fori(1, ADA_UNITS // SLOTS) as g:
                for s in range(SLOTS):
                    sp.wait_ge(ada_done, 4 * g + s - 3)
                    sp.dma_start(raw[:, s, :], sp_units[bass.ds(4 * g + s, 1)].rearrange("a p n -> (a p) n"))\
                        .then_inc(landed[s], 16)
            for s in range(SLOTS):
                sp.wait_ge(ada_done, ADA_UNITS - 3 + s)
                sp.dma_start(raw[:, s, :], sp_units[ADA_UNITS + s]).then_inc(landed[s], 16)
            with sp.Fori(1, UNITS // SLOTS) as g:
                for s in range(SLOTS):
                    sp.wait_ge(lo_ready, 8 * g + 2 * s - 6)
                    sp.dma_start(raw[:, s, :],
                                 sp_units[bass.ds(ADA_UNITS + 4 * g + s, 1)].rearrange("a p n -> (a p) n"))\
                        .then_inc(landed[s], 16)
            sp.wait_ge(sem("y_ready"), 2)
            sp.dma_start(out.rearrange("b (h p) n -> p (b h) n", p=P), x[:, :, :]).then_inc(sem("y_stored"), 16)
            sp.wait_ge(sem("y_stored"), 16)

        @block.gpsimd
        def _(pool):
            def load(name, *pairs):
                for dst, src in pairs:
                    pool.dma_start(dst, src).then_inc(sem(name), 16)

            load("ld_small", (cols[:, :], d["cols"]), (tab[:, :], d["tab"]))
            pool.memset(ones[:, :], 1.0).then_inc(sem("ones_set"), 1)
            load("ld_bias", (at(F_RELB, 32, parts=32), d["rel_bias"]), (arena[32:36, F_RELB:F_RELB + 32], d["owner"]),
                 (at(F_ONEH, 384, parts=36), d["onehot"]))
            load("ld_filt", (at(F_DFT, 1280), d["dft_k"]), (at(F_ZT, T, parts=33), d["zt"]),
                 (at(F_W1, 64, parts=33), d["filt_w1"]), (at(F_W2, 64, parts=64), d["filt_w2"]),
                 (at(F_W3, 64, parts=64), d["filt_w3"]))
            load("ld_c", (c_row, d["c_row"].partition_broadcast(P)))
            pool.wait_ge(sem("bias_rows_out"), 1)
            pool.dma_start(brow, at(F_BOUT, 384, parts=32)).then_inc(sem("brow_stored"), 16)
            with pool.Fori(0, 4) as b:
                load("ld_block", (at(F_W4, 1024, parts=64), d["filt_w4"][bass.ds(b, 1)].rearrange("a p n -> (a p) n")),
                     (at(F_DEC, 1024), d["decay"][bass.ds(b, 1)].rearrange("a p n -> (a p) n")),
                     (at(F_HB, 512), d["hyena_bias"][bass.ds(b, 1)].rearrange("a n -> (a n)").partition_broadcast(P)))
                pool.wait_ge(sem("spectrum_out"), 5 * b + 5)
                pool.dma_start(kf_dram[bass.ds(b, 1)].rearrange("a p n -> (a p) n"), at(F_KO, 2560))\
                    .then_inc(sem("kf_stored"), 16)
                pool.wait_ge(sem("kf_stored"), 16 * b + 16)
            pool.wait_ge(sem("brow_stored"), 16)
            pool.wait_ge(sem("kf_stored"), 64)
            load("ld_narrow", (at(12960, DC, 24), d["w_gate_nsa"]))
            pool.wait_ge(mod_ready, ADA_UNITS // 4)
            load("ld_x", (x[:, :, :], d["x"].rearrange("(h p) n -> p h n", p=P)))
            pool.wait_ge(sem("norm_lo"), norm_count("h1", "lo", 4))

            def toeplitz(m):
                src = bass.AP(tensor=brow.tensor, offset=8 * m * 384, ap=[[1, P], [384, 8], [1, T]])
                load("ld_toep", (toep, src))

            toeplitz(0)
            load("ld_sink", (stat[:, 32:40], d["sinks"].partition_broadcast(P)))
            pool.wait_ge(sem("att_out"), 16 * 1)
            toeplitz(2)
            pool.wait_ge(sem("att_out"), 16 * 2)
            load("ld_cmp", (w1k, d["w1k"]), (w1v, d["w1v"]), (w2c, d["w2kv"]), (peT, d["pe"]))
            pool.wait_ge(sem("cmp_hidden"), 2)
            toeplitz(1)
            pool.wait_ge(sem("att_out"), 16 * 3)
            toeplitz(3)
            pool.wait_ge(sem("norm_lo"), norm_count("hm", "lo", 4))
            load("ld_router", (at(ro, DC, 16), d["router_w"]), (at(ro + 256, 16), d["router_bias"].partition_broadcast(P)))
            pool.wait_ge(sem("x_moe"), 2)
            load("ld_rowg", (row, d["final_g"].partition_broadcast(P)))
            pool.wait_ge(sem("seq_t"), 12)
            load("ld_dftz", (at(2560, 2048), d["dft_z"]))
            for b in range(4):
                if b:
                    pool.wait_ge(sem("spec_ready"), 4 * b)
                load("ld_kf", (at(0, 2560), kf_dram[b]))
            pool.wait_ge(sem("yhy_split"), 8)
            load("ld_sgu", (at(4096, CH), d["ln_g"].partition_broadcast(P)), (at(5120, CH), d["ln_b"].partition_broadcast(P)),
                 (wsT, d["w_s"]), (at(7168, 1024, parts=1), d["b_s"]))
            pool.wait_ge(sem("cols_added"), 2 + 8)
            load("ld_rowf", (row, d["norm_final_g"].partition_broadcast(P)))

        @block.scalar
        def _(act):
            def hi(g, k):
                s, static = (k // 2) % SLOTS, isinstance(g, int)
                if k % 2 == 0:
                    act.wait_ge(landed[s], 16 * (ADA_UNITS // SLOTS + 1) + 16 * (g + k // 8))
                if not (static and 8 * g + k < 4):
                    act.wait_ge(half_done, 8 * g + (k - 3))
                act.activation(w_hi[:, k % 4, :], raw[:, s, (k % 2) * HALF:(k % 2 + 1) * HALF], ACT.Copy)\
                    .then_inc(hi_ready, 1)

            def phase(name, step=None, per_iter=1):
                def body(g, i, final):
                    for k in range(8 * per_iter):
                        if not (final and k + 3 >= 8 * per_iter):
                            hi(g, k + 3)
                        if step:
                            step(g, i, k)
                run_groups(act, name, body, per_iter)

            def done(g, k):
                act.wait_ge(half_done, 8 * g + (k + 1))

            def copy(dst, src):
                return act.activation(dst, src, ACT.Copy)

            act.wait_ge(sem("ld_c"), 16)
            act.activation(c_row, c_row, ACT.Silu).then_inc(sem("c_ready"), 1)
            for n in range(3):
                act.wait_ge(sem("sin_arg"), n + 1)
                act.activation(at(F_H, T, parts=64), at(F_R, T, parts=64), ACT.Sin).then_inc(sem("sin_out"), 1)
            with act.Fori(0, 4) as b:
                for n in range(4):
                    act.wait_ge(sem("taps_ready"), 4 * b + n + 1)
                    act.activation(at(F_ABS + 512 * n, 512), at(F_TAPS + 512 * n, 512), ACT.Abs).then_inc(sem("abs_ready"), 1)

            def norm(name, ready, width=D, src=x, spread=True, dst=h_hi, tiles=DC, f=hf, junk=xhat, first=0):
                act.wait_ge(sem(ready[0]), ready[1])
                for h in range(TH):
                    act.activation(junk[:, h, 0:width], src[:, h, 0:width], ACT.Square,
                                   accum_out=stat[:, h:h + 1]).then_inc(sem("norm_sq"), 1)
                act.wait_ge(sem("norm_ms"), norm_count(name, "ms", 1))
                act.activation(stat[:, 4:6], stat[:, 2:4], ACT.Sqrt).then_inc(sem("norm_rt"), 1)
                if spread:
                    for c in range(0, tiles, 4):
                        act.wait_ge(sem("norm_f"), norm_count(name, "f", c // 4 + 1))
                        copy(dst[:, first + c:first + c + 4, :], f[:, c:c + 4, :]).then_inc(sem("norm_hi"), 1)

            act.wait_ge(sem("ld_x"), 16)
            norm("h1", ("kf_stored", 64))
            act.wait_ge(sem("ld_narrow"), 16)
            copy(n_hi[:, :, :], at(12960, DC, 24)).then_inc(sem("narrow_hi"), 1)
            for k in range(3):
                hi(0, k)

            def heads_out(dst, sem_name):
                def step(g, i, k):
                    if k % 2 == 0:
                        return
                    done(g, k)
                    s = k // 2
                    copy(dst[:, 2 * s, :], ps[0:64, s, 0:T]).then_inc(sem(sem_name), 1)
                    copy(dst[:, 2 * s + 1, :], ps[64:128, s, 0:T]).then_inc(sem(sem_name), 1)
                return step

            def values_out(sem_name):
                def step(g, i, k):
                    if k == 7:
                        done(g, k)
                        for h in range(TH):
                            copy(v_a[:, h, :], ps[:, 4 + h, :]).then_inc(sem(sem_name), 1)
                return step

            def exps(first, n, sink):
                for t in range(n + 1):
                    if t < n:
                        a = first + t
                        act.wait_ge(sem("att_max"), a + 1)
                        if a >= 2:
                            act.wait_ge(sem("att_t"), a - 1)
                        if sink:
                            act.activation(stat[:, 128 + 2 * (t % 4):130 + 2 * (t % 4)], stat[:, 8 + 2 * (t % 2):10 + 2 * (t % 2)],
                                           ACT.Exp, bias=stat[:, 32 + t:33 + t]).then_inc(sem("sink_exp"), 1)
                        for h, (lo, w) in enumerate(((0, 128), (128, 256))):
                            act.activation(prob[:, t % 2, lo:lo + w], ps[:, t % 2, lo:lo + w], ACT.Exp,
                                           scale=SCALE, bias=stat[:, 8 + 2 * (t % 2) + h:9 + 2 * (t % 2) + h],
                                           accum_out=stat[:, 120 + 2 * (t % 4) + h:121 + 2 * (t % 4) + h]).then_inc(sem("att_p"), 1)
                    if t >= 1:
                        a = first + t - 1
                        act.wait_ge(sem("att_t"), a + 1)
                        if a >= 2:
                            act.wait_ge(sem("att_pv"), a - 1)
                        copy(pT[:, (t - 1) % 2, :], ps[:, 2 + (t - 1) % 2, 0:384]).then_inc(sem("att_pt"), 1)

            phase("a_q", heads_out(qT, "q_out"))
            phase("a_k", heads_out(kT, "k_out"))
            phase("a_v", values_out("v_out"))
            exps(0, 8, False)
            norm("mixA", ("att_out", 16), 512, mix, True, r_hi, 4, mixf, mix_junk, 0)
            phase("c_q", heads_out(qT, "q_out"))
            phase("c_k", heads_out(kT, "k_out"))
            phase("c_v", values_out("v_out"))
            exps(8, 8, False)
            norm("mixC", ("att_out", 32), 512, mix, True, r_hi, 4, mixf, mix_junk, 8)

            def small_out(g, i, k):
                if k % 2 == 0:
                    return
                u = k // 2
                done(g, k)
                if u < 5:
                    copy(smk[0:64, u, 0, :], ps[0:64, u % 4, 0:T]).then_inc(sem("small_out"), 1)
                    copy(smk[0:64, u, 1, :], ps[64:128, u % 4, 0:T]).then_inc(sem("small_out"), 1)
                elif u == 7:
                    for h in range(TH):
                        copy(smv[:, :, h, :], ps[:, 4 + h, 0:3 * P].rearrange("p (a b) -> p a b", a=3))\
                            .then_inc(sem("small_out"), 1)
            phase("small", small_out, per_iter=2)
            act.wait_ge(sem("gate_sum"), 1)
            act.activation(gates[:, :, :], ps[:, 6:8, 0:24], ACT.Sigmoid).then_inc(sem("gates_ready"), 1)
            for n in range(2):
                act.wait_ge(sem("cmp_hidden"), n + 1)
                act.activation(hidc[:, n, :], ps[:, n, 0:30], ACT.Gelu_apprx_tanh).then_inc(sem("hid_act"), 1)
            act.wait_ge(sem("cmp_kv"), 1)
            copy(kc, ps[0:64, 2, 0:30].rearrange("p (a b) -> p a b", a=2)).then_inc(sem("kc_ready"), 1)
            copy(vc, ps[0:N_CMP, 3, 0:128].rearrange("p (a b) -> p a b", a=2)).then_inc(sem("kc_ready"), 1)
            phase("b_q", heads_out(qT, "q_out"))
            exps(16, 8, True)
            norm("mixB", ("att_out", 48), 512, mix, True, r_hi, 4, mixf, mix_junk, 4)
            phase("d_q", heads_out(qT, "q_out"))
            act.wait_ge(sem("cmp_max"), 1)
            act.activation(cp[:, :, :, 0:N_CMP], cs[:, :, :, 0:N_CMP], ACT.Exp).then_inc(sem("cmp_exp"), 1)
            for r in range(4):
                act.wait_ge(sem("cmp_t"), r + 1)
                if r >= 1:
                    act.wait_ge(sem("cmp_pv"), r)
                copy(cpT[0:N_CMP, :], ps[0:N_CMP, 6, :]).then_inc(sem("cmp_pt"), 1)
            exps(24, 16, False)
            norm("mixD", ("att_out", 82), 512, mix, True, r_hi, 4, mixf, mix_junk, 12)
            phase("mix_out")
            norm("hm", ("cols_added", 2 + 4))
            act.wait_ge(sem("ld_router"), 32)
            copy(n_hi[:, :, 0:16], at(ro, DC, 16)).then_inc(sem("router_hi"), 1)
            act.wait_ge(sem("logits"), 1)
            act.activation(at(ro + 272, TH, 16), ps[:, 6:8, 0:16], ACT.Sigmoid).then_inc(sem("affinity"), 1)

            def expert_step(g, i, k):
                u = k // 2
                if u >= 8 or k % 4 == 0 or k % 4 == 2:
                    return
                f = u // 2
                if k % 4 == 1:
                    done(g, k)
                    act.wait_ge(sem("moe_pair"), 4 * i + f + 1)
                    act.activation(g_act[:, f % 2, :], ps[:, u % 4, 0:T], ACT.Silu).then_inc(sem("moe_silu"), 1)
                else:
                    act.wait_ge(sem("moe_pair"), 4 * i + f + 3)
                    copy(r_hi[:, f, :], hid[:, f % 2, :]).then_inc(sem("moe_hi"), 1)
            phase("moe", expert_step, per_iter=3)
            norm("x1", ("x_moe", 2), spread=False)
            norm("h2", ("x1_done", 2))

            phase("hyena")
            for n in range(1, 12, 2):
                act.wait_ge(sem("seq_t"), n + 1)
                copy(seq_pair(n), bank_pair(n)).then_inc(sem("seq_odd"), 1)
            for c in range(8):
                act.wait_ge(sem("yhy_t"), c + 1)
                copy(r_hi[:, c, :], ps[:, c % 4, 0:T]).then_inc(sem("yhy_hi"), 1)

            def gelu_u(g, i, k):
                if k % 2:
                    done(g, k)
                    act.activation(uT[:, bass.ds(4 * i + k // 2, 1), :],
                                   ps[:, k // 2:k // 2 + 1, 0:T], ACT.Gelu)\
                        .then_inc(sem("u_out"), 1)
            phase("sgu_u", gelu_u)

            def gelu_v(g, i, k):
                if k % 8 == 7:
                    cb = k // 8
                    done(g, k)
                    for h in range(TH):
                        act.activation(vg[:, h, cb * 512:(cb + 1) * 512], ps[:, 4 + 2 * cb + h, :], ACT.Gelu)\
                            .then_inc(sem("v_gelu"), 1)
            phase("sgu_v", gelu_v, per_iter=2)
            act.wait_ge(sem("ln_var"), 1)
            act.activation(stat[:, 4:6], stat[:, 2:4], ACT.Sqrt).then_inc(sem("ln_rt"), 1)
            for h in range(8):
                act.wait_ge(sem("ysgu_f"), h + 1)
                copy(r_hi[:, 8 + h, :], yf[:, h % 2, :]).then_inc(sem("ysgu_hi"), 1)

            def sigmoid(dst, name):
                def step(g, i, k):
                    if k % 2:
                        done(g, k)
                        act.activation(dst[:, bass.ds(4 * i + k // 2, 1), :], ps[:, k // 2:k // 2 + 1, 0:T], ACT.Sigmoid)\
                            .then_inc(sem(name), 1)
                return step
            phase("gate_hy", sigmoid(sg1, "sg1_out"))
            phase("branch_hy")
            phase("gate_sgu", sigmoid(sg2, "sg2_out"))

            def merged_hi(g, i, k):
                act.wait_ge(sem("merged_f"), 8 * i + k + 5)
                copy(h_hi[:, bass.ds(8 * i + k, 1), :], mf[:, k % 2:k % 2 + 1, :]).then_inc(sem("merged_hi"), 1)
            phase("branch_sgu", merged_hi)
            phase("out2")
            norm("hf", ("cols_added", 2 + 8))

            for part in range(3):
                def ffn_step(g, i, k, part=part):
                    n0 = sum(FFN_TILES[:part])
                    f = k // 4
                    if k % 4 == 1:
                        done(g, k)
                        act.wait_ge(sem("ffn_pair"), 2 * i + (n0 + f + 1))
                        act.activation(g_act[:, f, :], ps[:, k // 2, 0:T], ACT.Silu).then_inc(sem("ffn_silu"), 1)
                    elif k % 4 == 3:
                        act.wait_ge(sem("ffn_pair"), 2 * i + (n0 + f + 3))
                        copy(r_hi[:, bass.ds(2 * i + f, 1), :], hid[:, f:f + 1, :]).then_inc(sem("ffn_hi"), 1)
                phase(f"ffn_in{part}", ffn_step)
                phase(f"ffn_down{part}")
            norm("y", ("cols_added", 2 + 20), spread=False)

        @block.vector
        def _(dve):
            ch = Chain(dve, sem("dve_chain"))

            def lo(g, k):
                s = (k // 2) % SLOTS
                dve.wait_ge(hi_ready, 8 * g + (k + 1))
                dve.tensor_tensor(w_lo[:, k % 4, :], raw[:, s, (k % 2) * HALF:(k % 2 + 1) * HALF],
                                  w_hi[:, k % 4, :].bitcast(F32), ALU.subtract).then_inc(lo_ready, 1)

            def phase(name, step=None, per_iter=1, links=0):
                def body(g, i, final):
                    for k in range(8 * per_iter):
                        if not (final and k + 3 >= 8 * per_iter):
                            lo(g, k + 3)
                        if step:
                            step(g, i, k)
                before = (lambda i: ch.enter(i, links)) if links else None
                run_groups(dve, name, body, per_iter, before, ch.leave if links else None)

            def done(g, k):
                dve.wait_ge(half_done, 8 * g + (k + 1))

            for name, n in (("moe_pair", 2), ("ffn_pair", 2), ("down_out", 2), ("cols_added", 2),
                            ("conv_out", 4), ("bhy_out", 4), ("merged_f", 4), ("u_out", 4), ("sg1_out", 4), ("sg2_out", 4)):
                dve.sem_inc(sem(name), n)

            def modulation(g):
                if not (isinstance(g, int) and g == 0):
                    dve.wait_ge(mod_ready, g)
                for s in range(SLOTS):
                    dve.wait_ge(landed[s], 16 * g + 16)
                    dve.tensor_tensor_reduce(raw[:, s, :], raw[:, s, :], c_row, 1.0, 0.0, ALU.mult, ALU.add, mod_sums[:, s:s + 1])\
                        .then_inc(ada_done, 1)
                dve.wait_ge(ada_done, 4 * g + 4)
                dve.tensor_tensor(mod[:, bass.ds(4 * g, 4)], mod_sums, cols[:, bass.ds(4 * g + COLS["ada_b"], 4)], ALU.add)\
                    .then_inc(mod_ready, 1)

            dve.wait_ge(sem("bias_mm"), 1)
            dve.tensor_scalar(at(F_BOUT, 384, parts=32), ps[0:32, 4, 0:384], 1 / SCALE, None, ALU.mult)\
                .then_inc(sem("bias_rows_out"), 1)
            a, tt, r = (at(o, T, parts=64) for o in (F_A, F_T, F_R))
            dve.wait_ge(sem("ld_small"), 32)
            for n in range(3):
                dve.wait_ge(sem("mlp_mm"), n + 1)
                ch(dve.tensor_scalar(a, ps[0:64, 5, 0:T], cols[0:64, COLS["fb"] + n:COLS["fb"] + n + 1],
                                     cols[0:64, COLS["ffreq"]:COLS["ffreq"] + 1], ALU.add, ALU.mult))
                ch(dve.tensor_scalar(tt, a, 1 / (2 * math.pi), MAGIC, ALU.mult, ALU.add))
                ch(dve.tensor_scalar(tt, tt, MAGIC, None, ALU.subtract))
                for part in TWO_PI:
                    ch(dve.scalar_tensor_tensor(a, tt, -part, a, ALU.mult, ALU.add))
                if n:
                    dve.wait_ge(sem("sin_out"), n)
                dve.tensor_scalar(r, a, PI_IN, -PI_IN, ALU.min, ALU.max).then_inc(sem("sin_arg"), 1)
                if n == 0:
                    dve.wait_ge(sem("c_ready"), 1)
                modulation(n)
            modulation(3)
            with dve.Fori(0, 4) as b:
                ch.enter(b, 2)
                modulation(5 * b + 4)
                dve.wait_ge(sem("ld_block"), 48 * b + 48)
                for n in range(4):
                    dve.wait_ge(sem("taps_mm"), 4 * b + n + 1)
                    ins = dve.tensor_tensor(at(F_TAPS + 512 * n, 512), ps[:, n, :], at(F_DEC + 512 * (n // 2), 512), ALU.mult)
                    if n == 1:
                        ch(ins)
                        ins = dve.memset(arena[0:1, F_TAPS + 512:F_TAPS + 1024], 0.0)
                    ins.then_inc(sem("taps_ready"), 1)
                modulation(5 * b + 5)
                dve.wait_ge(sem("taps_ready"), 4 * b + 4)
                dve.wait_ge(sem("norm_mm"), b + 1)
                ch(dve.reciprocal(at(F_RN, 512), ps[:, 4, :]))
                for t in range(TH):
                    for op, o in ((ALU.add, 0), (ALU.subtract, 1024)):
                        dve.tensor_tensor(at(F_ABS + o + 512 * t, 512), at(F_TAPS + 1024 * t, 512),
                                          at(F_TAPS + 1024 * t + 512, 512), op).then_inc(sem("parity_ready"), 1)
                modulation(5 * b + 6)
                for n in range(5):
                    if n == 3:
                        modulation(5 * b + 7)
                    dve.wait_ge(sem("spectrum_mm"), 5 * b + n + 1)
                    dve.tensor_tensor(at(F_KO + 512 * n, 512), ps[:, (0, 1, 2, 3, 5)[n], :], at(F_RN, 512), ALU.mult)\
                        .then_inc(sem("spectrum_out" if n in (2, 3) else "spectrum_cos"), 1)
                dve.wait_ge(sem("spectrum_cos"), 3 * b + 3)
                for n in (0, 1, 4):
                    o = at(F_KO + 512 * n, 512)
                    dve.tensor_tensor(o, o, at(F_HB, 512), ALU.add).then_inc(sem("spectrum_out"), 1)
                modulation(5 * b + 8)
            ch.leave(4)
            dve.wait_ge(mod_ready, ADA_UNITS // 4)

            def norm(name, width=D, src=x, spread=True, dst=(h_hi, h_lo), tiles=DC, f=hf, xh=xhat, first=0, gain=None, bias=None):
                dve.wait_ge(sem("norm_sq"), norm_count(name, "sq", 2))
                dve.tensor_scalar(stat[:, 2:4], stat[:, 0:2], 1.0 / width, EPS, ALU.mult, ALU.add).then_inc(sem("norm_ms"), 1)
                dve.wait_ge(sem("norm_rt"), norm_count(name, "rt", 1))
                ch(dve.reciprocal(stat[:, 6:8], stat[:, 4:6]))
                if not spread:
                    return
                for h in range(TH):
                    dve.tensor_scalar(xh[:, h, 0:width], src[:, h, 0:width], stat[:, 6 + h:7 + h], None, ALU.mult)\
                        .then_inc(sem("norm_xh"), 1)

                def low(c):
                    dve.wait_ge(sem("norm_hi"), norm_count(name, "hi", c // 4 + 1))
                    dve.tensor_tensor(dst[1][:, first + c:first + c + 4, :], f[:, c:c + 4, :],
                                      dst[0][:, first + c:first + c + 4, :].bitcast(F32), ALU.subtract)\
                        .then_inc(sem("norm_lo"), 1)
                for c in range(tiles):
                    if c % 2 == 0:
                        dve.wait_ge(sem("norm_t"), norm_count(name, "t", c // 2 + 1))
                    src_ps = ps[:, (c // 2) % 4, (c % 2) * T:(c % 2 + 1) * T]
                    if bias is None:
                        ins = dve.tensor_scalar(f[:, c, :], src_ps, gain[:, c:c + 1], None, ALU.mult)
                    else:
                        ins = dve.tensor_scalar(f[:, c, :], src_ps, gain[:, c:c + 1], bias[:, c:c + 1], ALU.mult, ALU.add)
                    if c % 4 == 3:
                        ins.then_inc(sem("norm_f"), 1)
                        dve.wait_ge(sem("norm_f"), norm_count(name, "f", c // 4 + 1))
                        if c >= 7:
                            low(c - 7)
                low(tiles - 4)

            def gated_norm_gain(section, name):
                ch(dve.scalar_tensor_tensor(gain[:, :], mod[:, section * DC:(section + 1) * DC], 1.0, col(name, DC),
                                            ALU.add, ALU.mult))

            gated_norm_gain(1, "norm1")
            norm("h1", gain=gain, bias=mod[:, 0:DC])
            dve.wait_ge(sem("narrow_hi"), 1)
            dve.tensor_tensor(n_lo[:, :, :], at(12960, DC, 24), n_hi[:, :, :].bitcast(F32), ALU.subtract)\
                .then_inc(sem("narrow_lo"), 1)
            for k in range(3):
                lo(0, k)

            def scores(first, n, sink, out_of):
                for t in range(n + 2):
                    a = first + t
                    if t < n:
                        b = t % 2
                        dve.wait_ge(sem("att_s"), a + 1)
                        if a >= 2:
                            dve.wait_ge(sem("att_p"), 2 * (a - 1))
                        m = stat[:, 8 + 2 * b:10 + 2 * b]
                        dve.tensor_reduce(m[:, 0:1], ps[:, b, 0:128], AX, ALU.max, negate=True)
                        ch(dve.tensor_reduce(m[:, 1:2], ps[:, b, 128:384], AX, ALU.max, negate=True))
                        if sink:
                            ins = dve.tensor_scalar(m, m, SCALE, stat[:, 40 + t:41 + t], ALU.mult, ALU.min)
                        else:
                            ins = dve.tensor_scalar(m, m, SCALE, None, ALU.mult)
                        ins.then_inc(sem("att_max"), 1)
                    if t >= 2:
                        a, b = a - 2, t % 2
                        dve.wait_ge(sem("att_pv"), a + 1)
                        four = (t - 2) % 4
                        den = rden = stat[:, 120 + 2 * four:122 + 2 * four]
                        if sink:
                            dve.wait_ge(sem("sink_exp"), t - 1)
                            ch(dve.tensor_tensor(den, den, stat[:, 128 + 2 * four:130 + 2 * four], ALU.add))
                        ch(dve.reciprocal(rden, den))
                        out_of(a, t - 2, b, rden)

            def head_out(a, h, b, rden):
                for half in range(TH):
                    dve.tensor_scalar(mix[:, half, h * HD:(h + 1) * HD], ps[:, 4 + b, half * HD:(half + 1) * HD],
                                      rden[:, half:half + 1], None, ALU.mult).then_inc(sem("att_out"), 1)

            phase("a_q")
            phase("a_k")
            phase("a_v")
            scores(0, 8, False, head_out)

            def mixer_norm(m, name, count):
                dve.wait_ge(sem("att_out"), count)
                norm(name, 512, mix, True, (r_hi, r_lo), 4, mixf, mix, 4 * m, gain=col("mixg", 16)[:, 4 * m:4 * m + 4])
            mixer_norm(0, "mixA", 16)
            phase("c_q")
            phase("c_k")
            phase("c_v")
            scores(8, 8, False, head_out)
            mixer_norm(2, "mixC", 32)
            phase("small", per_iter=2)
            dve.wait_ge(sem("ld_cmp"), 64)
            dve.wait_ge(sem("small_out"), 12)
            for n in range(2):
                for par in range(2):
                    for part in range(2):
                        src = smk[0:64, 1 + n, :, 16 * part:16 * part + 240].rearrange("p g (n b) -> p b g n", b=16)
                        dst = blocks[64 * par:64 * par + 64, n, 240 * part:240 * part + 240]\
                            .rearrange("p (r g n) -> p r g n", r=8, g=2)
                        pe_v = peT[:, n, 16 * part:16 * part + 16].rearrange("p (r q) -> p q r", q=2)[:, par, :]
                        dve.tensor_tensor(dst, src[:, par:16:2, :, :],
                                          pe_v.unsqueeze(2).unsqueeze(3).broadcast_to([64, 8, 2, N_CMP]), ALU.add)\
                            .then_inc(sem("blocks_ready"), 1)
            dve.wait_ge(sem("ld_sink"), 16)
            ch(dve.tensor_scalar(stat[:, 40:48], stat[:, 32:40], -1.0, None, ALU.mult))
            phase("b_q")
            scores(16, 8, True, head_out)
            mixer_norm(1, "mixB", 48)
            phase("d_q")
            dve.wait_ge(sem("cmp_s"), 1)
            v15 = lambda v: v[:, :, :, 0:N_CMP]
            add, keep = (tab[:, o:o + 32].rearrange("p (a b) -> p a b", a=2)[:, :, 0:N_CMP].unsqueeze(1)
                         .broadcast_to([P, 8, 2, N_CMP]) for o in (TAB_CADD, TAB_C01))
            ch(dve.tensor_scalar(v15(cs), v15(ps[:, 7, 0:256].rearrange("p (a b c) -> p a b c", a=8, b=2)), SCALE, None, ALU.mult))
            ch(dve.tensor_tensor(v15(cs), v15(cs), add, ALU.add))
            cm, cden = stat[:, 48:64], stat[:, 64:80]
            ch(dve.tensor_reduce(cm.rearrange("p (a b) -> p a b", a=8), v15(cs), AX, ALU.max, negate=True))
            bc = cm.rearrange("p (a b) -> p a b", a=8).unsqueeze(3).broadcast_to([P, 8, 2, N_CMP])
            dve.tensor_tensor(v15(cs), v15(cs), bc, ALU.add).then_inc(sem("cmp_max"), 1)
            dve.wait_ge(sem("cmp_exp"), 1)
            dve.tensor_tensor(v15(cp), v15(cp), keep, ALU.mult).then_inc(sem("cmp_p"), 1)
            dve.wait_ge(sem("cmp_p"), 1)
            ch(dve.tensor_reduce(cden.rearrange("p (a b) -> p a b", a=8), v15(cp), AX, ALU.add))
            ch(dve.tensor_scalar(cden, cden, TINY, None, ALU.max))
            ch(dve.reciprocal(cden, cden))
            dve.wait_ge(sem("gates_ready"), 1)
            gate = gates[:, :, :].rearrange("p t (h g) -> p g h t", g=3)
            ch(dve.tensor_tensor(cden.rearrange("p (a b) -> p a b", a=8), cden.rearrange("p (a b) -> p a b", a=8),
                                 gate[:, 0], ALU.mult))
            for q in range(2):
                dve.wait_ge(sem("cmp_pv"), 2 * q + 2)
                w = cden.rearrange("p (a b) -> p a b", a=8)[:, 4 * q:4 * q + 4, :].unsqueeze(3).broadcast_to([P, 4, 2, HD])
                dve.tensor_tensor(mix[:, :, 256 * q:256 * q + 256].rearrange("p t (h n) -> p h t n", h=4),
                                  ps[:, 4 + q, :].rearrange("p (h t n) -> p h t n", h=4, t=2), w, ALU.mult)\
                    .then_inc(sem("att_out"), 1)

            def nsa_out(a, n, b, rden):
                h, branch = n % 8, 1 + n // 8
                for half in range(TH):
                    ch(dve.tensor_tensor(rden[:, half:half + 1], rden[:, half:half + 1],
                                         gates[:, half, 3 * h + branch:3 * h + branch + 1], ALU.mult))
                dve.wait_ge(sem("att_out"), 50 if branch == 1 else 50 + 2 * h + 2)
                for half in range(TH):
                    o = mix[:, half, h * HD:(h + 1) * HD]
                    dve.scalar_tensor_tensor(o, ps[:, 4 + b, half * HD:(half + 1) * HD], rden[:, half:half + 1], o,
                                             ALU.mult, ALU.add).then_inc(sem("att_out"), 1)
            scores(24, 16, False, nsa_out)
            mixer_norm(3, "mixD", 82)

            def gate_row(section, n):
                for c in range(DC):
                    if c >= 2:
                        dve.wait_ge(sem("row_mm"), DC * n + c - 1)
                    dve.tensor_scalar(diag[:, c % 2, :], ident, mod[:, section * DC + c:section * DC + c + 1], None, ALU.mult)\
                        .then_inc(sem("diag_ready"), 1)
                for q in range(4):
                    dve.wait_ge(sem("row_mm"), DC * n + 4 * q + 4)
                    dve.tensor_copy(row[:, q * 512:(q + 1) * 512], ps[:, 4 + q, :]).then_inc(sem("row_ready"), 1)
                dve.wait_ge(sem("row_ready"), 4 * n + 4)

            gate_row(2, 0)

            def add_cols(first, per_cb, gated=False):
                def step(g, i, k):
                    u, r = divmod(k, 2)
                    if not r or u % per_cb != per_cb - 1:
                        return
                    cb = u // per_cb
                    per = 2 if per_cb == 4 else 4
                    done(g, k)
                    for h in range(TH):
                        o = x[:, h, bass.ds(512 * per * i + 512 * cb, 512)] if not isinstance(i, int) else \
                            x[:, h, 512 * (per * i + cb):512 * (per * i + cb) + 512]
                        acc_ps = ps[:, 4 + 2 * (cb % 2) + h, :]
                        if gated:
                            rw = row[:, bass.ds(512 * per * i + 512 * cb, 512)]
                            tmp = at(11000 + 512 * h, 512)
                            ch(dve.tensor_tensor(tmp, acc_ps, rw, ALU.mult))
                            ins = dve.tensor_tensor(o, o, tmp, ALU.add)
                        else:
                            ins = dve.tensor_tensor(o, o, acc_ps, ALU.add)
                        if h:
                            ins.then_inc(sem("cols_added"), 1)
                return step
            phase("mix_out", add_cols(0, 4, True), per_iter=2, links=4)

            gated_norm_gain(4, "norm2")
            norm("hm", gain=gain, bias=mod[:, 3 * DC:4 * DC])
            dve.wait_ge(sem("router_hi"), 1)
            dve.tensor_tensor(n_lo[:, :, 0:16], at(ro, DC, 16), n_hi[:, :, 0:16].bitcast(F32), ALU.subtract)\
                .then_inc(sem("router_lo"), 1)
            dve.memset(acc, 0.0).then_inc(sem("acc_zero"), 1)
            aff, score, beat, tie = at(ro + 272, 32), at(ro + 304, 32), at(ro + 336, 128), at(ro + 464, 128)
            rank, sel = at(ro + 592, 32), at(ro + 624, 32)
            gsc, gbeat, gtie, grank, wsum = at(ro + 656, 8), at(ro + 664, 32), at(ro + 696, 32), at(ro + 728, 8), at(ro + 736, 2)
            dve.wait_ge(sem("affinity"), 1)
            ch(dve.tensor_tensor(score.rearrange("p (h e) -> p h e", h=2), aff.rearrange("p (h e) -> p h e", h=2),
                                 at(ro + 256, 16).unsqueeze(1).broadcast_to([P, 2, 16]), ALU.add))
            tri = tab[:, TAB_TRI:TAB_TRI + 16].rearrange("p (a b) -> p a b", a=4)

            def ranks(s, wins, ties, out_rank, n):
                s3 = s.rearrange("p (g e) -> p g e", e=4)
                w4, t4 = (v.rearrange("p (g e j) -> p g e j", e=4, j=4) for v in (wins, ties))
                sj, se = s3.unsqueeze(2).broadcast_to([P, n, 4, 4]), s3.unsqueeze(3).broadcast_to([P, n, 4, 4])
                ch(dve.tensor_tensor(w4, sj, se, ALU.is_gt))
                ch(dve.tensor_tensor(t4, sj, se, ALU.is_equal))
                ch(dve.tensor_tensor(t4, t4, tri.unsqueeze(1).broadcast_to([P, n, 4, 4]), ALU.mult))
                ch(dve.tensor_tensor(wins, wins, ties, ALU.add))
                ch(dve.tensor_reduce(out_rank.rearrange("p (g e) -> p g e", e=4), w4, AX, ALU.add))

            ranks(score, beat, tie, rank, 8)
            ch(dve.tensor_scalar(sel, rank, 1.5, None, ALU.is_lt))
            ch(dve.tensor_tensor(rank, score, sel, ALU.mult))
            ch(dve.tensor_reduce(gsc, rank.rearrange("p (g e) -> p g e", e=4), AX, ALU.add))
            ranks(gsc, gbeat, gtie, grank, 2)
            ch(dve.tensor_scalar(grank, grank, 0.5, None, ALU.is_lt))
            ch(dve.tensor_tensor(sel.rearrange("p (g e) -> p g e", e=4), sel.rearrange("p (g e) -> p g e", e=4),
                                 grank.unsqueeze(2).broadcast_to([P, 8, 4]), ALU.mult))
            ch(dve.tensor_tensor(sel, sel, aff, ALU.mult))
            ch(dve.tensor_reduce(wsum, sel.rearrange("p (h e) -> p h e", h=2), AX, ALU.add))
            ch(dve.reciprocal(wsum, wsum))
            ch(dve.tensor_tensor(comb[:, :, :], sel.rearrange("p (h e) -> p h e", h=2),
                                 wsum.unsqueeze(2).broadcast_to([P, 2, 16]), ALU.mult))
            gate_row(5, 1)
            dve.wait_ge(sem("acc_zero"), 1)

            def expert_step(g, i, k):
                u = k // 2
                if k in (4, 8, 12, 16):
                    f = k // 4 - 1
                    dve.wait_ge(sem("moe_hi"), 4 * i + (f + 1))
                    dve.tensor_tensor(r_lo[:, f, :], hid[:, f % 2, :], r_hi[:, f, :].bitcast(F32), ALU.subtract)\
                        .then_inc(sem("moe_lo"), 1)
                if u < 8 and k % 4 == 3:
                    f = k // 4
                    done(g, k)
                    dve.wait_ge(sem("moe_silu"), 4 * i + (f + 1))
                    dve.tensor_tensor(hid[:, f % 2, :], g_act[:, f % 2, :], ps[:, u % 4, 0:T], ALU.mult)\
                        .then_inc(sem("moe_pair"), 1)
                if u >= 8 and k % 2:
                    cb = u - 8
                    done(g, k)
                    for h in range(TH):
                        o = acc[:, h, cb * 512:(cb + 1) * 512]
                        ins = dve.scalar_tensor_tensor(o, ps[:, 4 + 2 * (cb % 2) + h, :], comb[:, h, bass.ds(i, 1)], o,
                                                       ALU.mult, ALU.add)
                        if h == 0:
                            ch(ins)
                        else:
                            ins.then_inc(sem("down_out"), 1)
                            dve.wait_ge(sem("down_out"), 4 * i + (cb + 3))
            phase("moe", expert_step, per_iter=3, links=4)
            for h in range(TH):
                ch(dve.tensor_tensor(acc[:, h, :], acc[:, h, :], row, ALU.mult))
                dve.tensor_tensor(x[:, h, :], x[:, h, :], acc[:, h, :], ALU.add).then_inc(sem("x_moe"), 1)

            def scaled(name, row_sem, value, done_sem):
                norm(name, spread=False)
                dve.wait_ge(sem(row_sem), value)
                for h in range(TH):
                    dve.scalar_tensor_tensor(x[:, h, :], x[:, h, :], stat[:, 6 + h:7 + h], row, ALU.mult, ALU.mult)\
                        .then_inc(sem(done_sem), 1)
            scaled("x1", "ld_rowg", 16, "x1_done")
            dve.wait_ge(sem("x1_done"), 2)
            norm("h2", gain=col("normmix2", DC))

            def conv_step(g, i, k):
                if k % 2 == 0:
                    return
                s = k // 2
                done(g, k)
                tile = cvT[:, bass.ds(4 * i + s, 1), :].rearrange("p a n -> p (a n)")
                w = [cols[:, bass.ds(4 * i + (s + COLS["conv_w"] + 24 * j), 1)] for j in range(3)]
                b = cols[:, bass.ds(4 * i + (s + COLS["conv_b"]), 1)]
                ch(dve.tensor_scalar(tile, ps[:, s, 0:T], w[1], b, ALU.mult, ALU.add))
                ch(dve.scalar_tensor_tensor(tile[:, 1:T], ps[:, s, 0:T - 1], w[0], tile[:, 1:T], ALU.mult, ALU.add))
                dve.scalar_tensor_tensor(tile[:, 0:T - 1], ps[:, s, 1:T], w[2], tile[:, 0:T - 1], ALU.mult, ALU.add)\
                    .then_inc(sem("conv_out"), 1)
            phase("hyena", conv_step, links=8)
            for n in range(0, 12, 2):
                dve.wait_ge(sem("seq_t"), n + 1)
                dve.tensor_copy(seq_pair(n), bank_pair(n)).then_inc(sem("seq_even"), 1)
            for b in range(4):
                o, q = divmod(b, 2)
                cut = slice(q * 512, (q + 1) * 512)
                dve.wait_ge(sem("ld_kf"), 16 * (b + 1))
                if b:
                    dve.wait_ge(sem("inv_mm"), 2 * b)
                for ft in range(2):
                    re, im = ps[:, ft, :], ps[:, 2 + ft, :]
                    ka, kb, kc_ = kf[:, ft, :], kf[:, 2 + ft, :], kf[:, 4 if ft == 0 else 1, :]
                    dve.wait_ge(sem("spec_mm"), 4 * b + 3 + ft)
                    for (u, v, op, dst, part) in ((ka, kb, ALU.subtract, yr[:, ft, :], prods[:, 0, :]),
                                                  (kb, kc_, ALU.add, yr[:, 2 + ft, :], prods[:, 1, :])):
                        dve.tensor_tensor(dst, re, u, ALU.mult)
                        ch(dve.tensor_tensor(part, im, v, ALU.mult))
                        dve.tensor_tensor(dst, dst, part, op).then_inc(sem("spec_ready"), 1)
                for lt in range(TH):
                    dve.wait_ge(sem("inv_mm"), 2 * b + lt + 1)
                    dve.tensor_tensor(seq[:, 0, lt, cut], ps[:, 4 + lt, :], seq[:, 1 + o, lt, cut], ALU.mult)\
                        .then_inc(sem("conv_step"), 1)
            for c in range(8):
                dve.wait_ge(sem("yhy_hi"), c + 1)
                dve.tensor_tensor(r_lo[:, c, :], ps[:, c % 4, 0:T], r_hi[:, c, :].bitcast(F32), ALU.subtract)\
                    .then_inc(sem("yhy_split"), 1)

            phase("sgu_u")
            phase("sgu_v", per_iter=2)
            dve.wait_ge(sem("v_gelu"), 4)
            for h in range(TH):
                for q in range(2):
                    ch(dve.bn_stats(stat[:, 96 + 12 * h + 6 * q:102 + 12 * h + 6 * q], vg[:, h, q * 512:(q + 1) * 512]))
                ch(dve.bn_aggr(stat[:, 88 + 2 * h:90 + 2 * h], stat[:, 96 + 12 * h:108 + 12 * h]))
            dve.tensor_scalar(stat[:, 2:4], stat[:, 89:92:2], EPS, None, ALU.add).then_inc(sem("ln_var"), 1)
            dve.wait_ge(sem("ln_rt"), 1)
            ch(dve.reciprocal(stat[:, 6:8], stat[:, 4:6]))
            dve.wait_ge(sem("ld_sgu"), 64)
            for h in range(TH):
                ch(dve.tensor_scalar(vg[:, h, :], vg[:, h, :], stat[:, 88 + 2 * h:89 + 2 * h], stat[:, 6 + h:7 + h],
                                     ALU.subtract, ALU.mult))
                ch(dve.tensor_tensor(vg[:, h, :], vg[:, h, :], ln_row[:, 0, :], ALU.mult))
                dve.tensor_tensor(vg[:, h, :], vg[:, h, :], ln_row[:, 1, :], ALU.add).then_inc(sem("v_normed"), 1)
            dve.wait_ge(sem("u_out"), 4 + 8)
            for h in range(8):
                dve.wait_ge(sem("spatial_mm"), h + 1)
                dve.tensor_tensor(yf[:, h % 2, :], uT[:, h, :], ps[:, h % 4, 0:T], ALU.mult).then_inc(sem("ysgu_f"), 1)
                dve.wait_ge(sem("ysgu_hi"), h + 1)
                dve.tensor_tensor(r_lo[:, 8 + h, :], yf[:, h % 2, :], r_hi[:, 8 + h, :].bitcast(F32), ALU.subtract)\
                    .then_inc(sem("ysgu_lo"), 1)

            phase("gate_hy")
            dve.wait_ge(sem("sg1_out"), 4 + 16)

            def branch_step(g, i, k):
                done(g, k)
                t = sg1[:, bass.ds(8 * i + k, 1), :]
                dve.tensor_tensor(t, t, ps[:, k % 4:k % 4 + 1, 0:T], ALU.mult).then_inc(sem("bhy_out"), 1)
            phase("branch_hy", branch_step)
            phase("gate_sgu")
            dve.wait_ge(sem("sg2_out"), 4 + 16)
            dve.wait_ge(sem("bhy_out"), 4 + 16)

            def merge_step(g, i, k):
                done(g, k)
                m = mf[:, k % 2:k % 2 + 1, :]
                ch(dve.tensor_tensor(m, sg2[:, bass.ds(8 * i + k, 1), :], ps[:, k % 4:k % 4 + 1, 0:T], ALU.mult))
                dve.tensor_tensor(m, m, sg1[:, bass.ds(8 * i + k, 1), :], ALU.add).then_inc(sem("merged_f"), 1)
                dve.wait_ge(sem("merged_hi"), 8 * i + (k + 1))
                dve.tensor_tensor(h_lo[:, bass.ds(8 * i + k, 1), :], m, h_hi[:, bass.ds(8 * i + k, 1), :].bitcast(F32),
                                  ALU.subtract).then_inc(sem("merged_lo"), 1)
            phase("branch_sgu", merge_step, links=8)
            phase("out2", add_cols(4, 4), per_iter=2)
            norm("hf", gain=col("normffn2", DC))

            for part in range(3):
                def ffn_step(g, i, k, part=part):
                    n0 = sum(FFN_TILES[:part])
                    if k % 4 == 3:
                        f = k // 4
                        done(g, k)
                        dve.wait_ge(sem("ffn_silu"), 2 * i + (n0 + f + 1))
                        dve.tensor_tensor(hid[:, f, :], g_act[:, f, :], ps[:, k // 2, 0:T], ALU.mult).then_inc(sem("ffn_pair"), 1)
                        dve.wait_ge(sem("ffn_hi"), 2 * i + (n0 + f + 1))
                        dve.tensor_tensor(r_lo[:, bass.ds(2 * i + f, 1), :], hid[:, f:f + 1, :],
                                          r_hi[:, bass.ds(2 * i + f, 1), :].bitcast(F32), ALU.subtract).then_inc(sem("ffn_lo"), 1)
                phase(f"ffn_in{part}", ffn_step)
                per_cb = FFN_TILES[part] // 4
                phase(f"ffn_down{part}", add_cols(8 + 4 * part, per_cb), per_iter=2 if per_cb == 4 else 3)
            scaled("y", "ld_rowf", 16, "y_ready")

        @block.tensor
        def _(pe):
            def mm(o, a, b, start=True, stop=True):
                return pe.matmul(o, a, b, start=start, stop=stop)

            def three(o, a, b, start, stop):
                mm(o, a[0], b[0], start, False)
                mm(o, a[0], b[1], False, False)
                return mm(o, a[1], b[0], False, stop)

            def w(k, lo_col, n):
                return w_hi[:, k % 4, lo_col:lo_col + n], w_lo[:, k % 4, lo_col:lo_col + n]

            H = lambda c, a=0, b=T: (h_hi[:, c, a:b], h_lo[:, c, a:b])
            R = lambda c, a=0, b=T: (r_hi[:, c, a:b], r_lo[:, c, a:b])

            def phase(name, step, per_iter=1):
                def body(g, i, final):
                    for k in range(8 * per_iter):
                        pe.wait_ge(lo_ready, 8 * g + (k + 1))
                        step(g, i, k).then_inc(half_done, 1)
                run_groups(pe, name, body, per_iter)

            def feature_major(k, o, src=H):
                for j in range(8):
                    c = (k % 2) * 8 + j
                    ins = three(o, w(k, j * P, P), src(c), c == 0, c == DC - 1)
                return ins

            def token_major(k, kq, n_kq, bank, src):
                for j in range(2):
                    c = 4 * kq + (k % 2) * 2 + j
                    for h in range(TH):
                        ins = three(ps[:, bank + h, :], src(c, h * P, (h + 1) * P), w(k, j * 512, 512), c == 0, c == 4 * n_kq - 1)
                return ins

            def fm_phase(name, free=None, per=4):
                def step(g, i, k):
                    if k % 2 == 0 and free:
                        free(i, k // 2)
                    return feature_major(k, ps[:, k // 2, 0:T])
                phase(name, step)

            pe.wait_ge(sem("ld_bias"), 48)
            mm(ps[0:32, 4, 0:384], at(F_RELB, 32, parts=36), at(F_ONEH, 384, parts=36)).then_inc(sem("bias_mm"), 1)
            pe.wait_ge(sem("ld_filt"), 80)
            for n, (wo, kk, src) in enumerate(((F_W1, 33, F_ZT), (F_W2, 64, F_H), (F_W3, 64, F_H))):
                if n:
                    pe.wait_ge(sem("sin_out"), n)
                mm(ps[0:64, 5, 0:T], at(wo, 64, parts=kk), at(src, T, parts=kk)).then_inc(sem("mlp_mm"), 1)
            pe.wait_ge(sem("sin_out"), 3)
            pe.wait_ge(sem("ones_set"), 1)
            cosm, sinm = at(F_DFT, 2, T), at(F_DFT + 512, 2, T)
            nyq = at(F_DFT + 1024, 2, P)
            with pe.Fori(0, 4) as b:
                pe.wait_ge(sem("ld_block"), 48 * b + 48)
                for n in range(4):
                    mm(ps[:, n, :], arena[0:64, F_H + (n // 2) * P:F_H + (n // 2 + 1) * P],
                       arena[0:64, F_W4 + (n % 2) * 512:F_W4 + (n % 2 + 1) * 512]).then_inc(sem("taps_mm"), 1)
                for n in range(4):
                    pe.wait_ge(sem("abs_ready"), 4 * b + n + 1)
                    ins = mm(ps[:, 4, :], ones[:, :], at(F_ABS + 512 * n, 512), n == 0, n == 3)
                ins.then_inc(sem("norm_mm"), 1)
                pe.wait_ge(sem("parity_ready"), 4 * b + 4)
                for n, (m, c0, o) in enumerate(((cosm, 0, 0), (cosm, P, 0), (sinm, 0, 1024), (sinm, P, 1024), (nyq, 0, 0))):
                    for t in range(TH):
                        ins = mm(ps[:, (0, 1, 2, 3, 5)[n], :], m[:, t, c0:c0 + P], at(F_ABS + o + 512 * t, 512), t == 0, t == 1)
                    ins.then_inc(sem("spectrum_mm"), 1)
            def turn(name, tiles=DC, xh=xhat):
                pe.wait_ge(sem("norm_xh"), norm_count(name, "xh", 2))
                for p in range(tiles // 2):
                    if p >= 4:
                        pe.wait_ge(sem("norm_f"), norm_count(name, "f", (p - 4) // 2 + 1))
                    for c in range(2):
                        for h in range(TH):
                            ins = pe.transpose(ps[:, p % 4, c * T + h * P:c * T + (h + 1) * P],
                                               xh[:, h, (2 * p + c) * P:(2 * p + c + 1) * P], ident)
                    ins.then_inc(sem("norm_t"), 1)

            turn("h1")
            pe.wait_ge(sem("norm_lo"), norm_count("h1", "lo", 4))
            fm_phase("a_q")
            fm_phase("a_k", lambda i, s: pe.wait_ge(sem("q_out"), 2 * s + 2))
            phase("a_v", lambda g, i, k: token_major(k, k // 2, 4, 4, H))

            def attend(first, n, keys, values):
                for t in range(n + 2):
                    if t < n:
                        a, b = first + t, t % 2
                        if a >= 2:
                            pe.wait_ge(sem("att_p"), 2 * (a - 1))
                        q, kt, bias = qT[:, t % 8, :], keys(t), toep[:, t % 8, :]
                        mm(ps[:, b, 0:128], q[:, 0:P], kt[:, 0:P], True, False)
                        mm(ps[:, b, 0:128], flip, bias[:, P:T], False, True)
                        mm(ps[:, b, 128:384], q[:, P:T], kt, True, False)
                        mm(ps[:, b, 128:384], flip, bias, False, True).then_inc(sem("att_s"), 1)
                    if 1 <= t <= n:
                        a, b = first + t - 1, (t - 1) % 2
                        pe.wait_ge(sem("att_p"), 2 * a + 2)
                        if a >= 2:
                            pe.wait_ge(sem("att_pt"), a - 1)
                        for j in range(3):
                            ins = pe.transpose(ps[:, 2 + b, j * P:(j + 1) * P], prob[:, b, j * P:(j + 1) * P], ident)
                        ins.then_inc(sem("att_t"), 1)
                    if t >= 2:
                        a, b = first + t - 2, t % 2
                        pe.wait_ge(sem("att_pt"), a + 1)
                        if t >= 4:
                            pe.wait_ge(sem("att_out"), out_count(a - 2))
                        v0, v1 = values(t - 2)
                        mm(ps[:, 4 + b, 0:HD], pT[:, b, 0:P], v0)
                        mm(ps[:, 4 + b, HD:2 * HD], pT[:, b, P:2 * P], v0, True, False)
                        mm(ps[:, 4 + b, HD:2 * HD], pT[:, b, 2 * P:3 * P], v1, False, True).then_inc(sem("att_pv"), 1)

            def out_count(a):
                return 2 * a + 2 if a < 24 else 2 * a + 4

            own = (lambda t: kT[:, t, :], lambda t: (v_a[:, 0, t * HD:(t + 1) * HD], v_a[:, 1, t * HD:(t + 1) * HD]))

            def shared(kk, vv):
                return (lambda t: smk[0:64, kk, (t % 8) // 4, :],
                        lambda t: tuple(smv[:, vv, h, ((t % 8) // 4) * HD:((t % 8) // 4 + 1) * HD] for h in range(2)))

            pe.wait_ge(sem("k_out"), 8)
            pe.wait_ge(sem("v_out"), 2)
            pe.wait_ge(sem("ld_toep"), 16)
            attend(0, 8, *own)
            turn("mixA", 4, mix)
            pe.wait_ge(sem("norm_f"), norm_count("mixA", "f", 1))
            fm_phase("c_q")
            fm_phase("c_k", lambda i, s: pe.wait_ge(sem("q_out"), 8 + 2 * s + 2))
            phase("c_v", lambda g, i, k: token_major(k, k // 2, 4, 4, H))
            pe.wait_ge(sem("k_out"), 16)
            pe.wait_ge(sem("v_out"), 4)
            pe.wait_ge(sem("ld_toep"), 32)
            attend(8, 8, *own)
            turn("mixC", 4, mix)
            pe.wait_ge(sem("norm_f"), norm_count("mixC", "f", 1))

            def small_step(g, i, k):
                u = k // 2
                if u < 5:
                    if k == 8:
                        pe.wait_ge(sem("small_out"), 2)
                    return feature_major(k, ps[:, u % 4, 0:T])
                for j in range(8):
                    c = (k % 2) * 8 + j
                    for h in range(TH):
                        ins = three(ps[:, 4 + h, (u - 5) * P:(u - 4) * P], H(c, h * P, (h + 1) * P), w(k, j * P, P),
                                    c == 0, c == DC - 1)
                return ins
            phase("small", small_step, per_iter=2)

            def narrow(n, ready, name):
                for r in ready:
                    pe.wait_ge(sem(r), 1)
                for h in range(TH):
                    for c in range(DC):
                        ins = three(ps[:, 6 + h, 0:n], H(c, h * P, (h + 1) * P), (n_hi[:, c, 0:n], n_lo[:, c, 0:n]),
                                    c == 0, c == DC - 1)
                ins.then_inc(sem(name), 1)
            narrow(24, ("narrow_hi", "narrow_lo"), "gate_sum")
            pe.wait_ge(sem("ld_cmp"), 64)
            for n, w1 in enumerate((w1k, w1v)):
                pe.wait_ge(sem("blocks_ready"), 4 * n + 4)
                for r in range(16):
                    ins = mm(ps[:, n, 0:30], w1[:, r, :], blocks[:, n, 30 * r:30 * r + 30], r == 0, r == 15)
                ins.then_inc(sem("cmp_hidden"), 1)
            pe.wait_ge(sem("hid_act"), 2)
            mm(ps[0:64, 2, 0:30], w2c[:, 0, :], hidc[:, 0, :])
            for g in range(2):
                ins = mm(ps[0:N_CMP, 3, g * HD:(g + 1) * HD], hidc[:, 1, g * N_CMP:(g + 1) * N_CMP], w2c[:, 1, :])
            ins.then_inc(sem("cmp_kv"), 1)
            pe.wait_ge(sem("kc_ready"), 2)
            fm_phase("b_q")
            pe.wait_ge(sem("q_out"), 24)
            pe.wait_ge(sem("ld_toep"), 48)
            attend(16, 8, *shared(0, 0))
            turn("mixB", 4, mix)
            pe.wait_ge(sem("norm_f"), norm_count("mixB", "f", 1))
            fm_phase("d_q")
            pe.wait_ge(sem("q_out"), 32)
            pe.wait_ge(sem("gates_ready"), 1)
            for h in range(8):
                for half in range(TH):
                    o = (2 * h + half) * 16
                    ins = mm(ps[:, 7, o:o + N_CMP], qT[:, h, half * P:(half + 1) * P], kc[:, h // 4, :])
            ins.then_inc(sem("cmp_s"), 1)
            pe.wait_ge(sem("cmp_p"), 1)
            for r in range(4):
                for j in range(4):
                    h, half = 2 * r + j // 2, j % 2
                    ins = pe.transpose(ps[0:N_CMP, 6, j * P:(j + 1) * P], cp[:, h, half, 0:N_CMP], ident)
                ins.then_inc(sem("cmp_t"), 1)
                pe.wait_ge(sem("cmp_pt"), r + 1)
                for j in range(4):
                    n, h = 4 * r + j, 2 * r + j // 2
                    ins = mm(ps[:, 4 + n // 8, (n % 8) * HD:(n % 8 + 1) * HD], cpT[0:N_CMP, j * P:(j + 1) * P], vc[:, h // 4, :])
                ins.then_inc(sem("cmp_pv"), 1)
            pe.wait_ge(sem("att_out"), 50)
            slc, win = shared(3, 1), shared(4, 2)
            pe.wait_ge(sem("ld_toep"), 64)
            attend(24, 16, lambda t: (slc if t < 8 else win)[0](t), lambda t: (slc if t < 8 else win)[1](t))
            turn("mixD", 4, mix)
            pe.wait_ge(sem("norm_lo"), norm_count("mixD", "lo", 1))

            def spread_row(n):
                for c in range(DC):
                    pe.wait_ge(sem("diag_ready"), DC * n + c + 1)
                    mm(ps[:, 4 + c // 4, (c % 4) * P:(c % 4 + 1) * P], ones[:, :], diag[:, c % 2, :]).then_inc(sem("row_mm"), 1)
                pe.wait_ge(sem("row_ready"), 4 * n + 4)
            spread_row(0)

            def column_blocks(name, first, per_cb, src):
                def step(g, i, k):
                    u = k // 2
                    cb, kq = divmod(u, per_cb)
                    if k % 2 == 0 and kq == 0:
                        pe.wait_ge(sem("cols_added"), 2 * i + (first + cb + 1))
                    return token_major(k, kq, per_cb, 4 + 2 * (cb % 2), src)
                phase(name, step, per_iter=2 if per_cb == 4 else 3)
            column_blocks("mix_out", 0, 4, R)

            turn("hm")
            pe.wait_ge(sem("norm_lo"), norm_count("hm", "lo", 4))
            narrow(16, ("router_hi", "router_lo"), "logits")
            pe.wait_ge(sem("affinity"), 1)
            spread_row(1)

            def expert_step(g, i, k):
                u = k // 2
                if u < 8:
                    if k % 4 == 0:
                        pe.wait_ge(sem("moe_pair"), 4 * i + (k // 4 + 1))
                    return feature_major(k, ps[:, u % 4, 0:T])
                cb = u - 8
                if k == 16:
                    pe.wait_ge(sem("moe_lo"), 4 * i + 4)
                if k % 2 == 0:
                    pe.wait_ge(sem("down_out"), 4 * i + (cb + 1))
                return token_major(k, 0, 1, 4 + 2 * (cb % 2), R)
            phase("moe", expert_step, per_iter=3)

            turn("h2")
            pe.wait_ge(sem("norm_lo"), norm_count("h2", "lo", 4))
            fm_phase("hyena", lambda i, s: pe.wait_ge(sem("conv_out"), 4 * i + (s + 1)))
            pe.wait_ge(sem("conv_out"), 4 + 24)
            for n in range(12):
                if n >= 4:
                    pe.wait_ge(sem("seq_odd" if n % 2 else "seq_even"), (n - 4) // 2 + 1)
                for c in range(2):
                    for h in range(TH):
                        ins = pe.transpose(ps[:, n % 4, c * T + h * P:c * T + (h + 1) * P],
                                           cvT[:, 2 * n + c, h * P:(h + 1) * P], ident)
                ins.then_inc(sem("seq_t"), 1)
            pe.wait_ge(sem("seq_odd"), 6)
            pe.wait_ge(sem("seq_even"), 6)
            pe.wait_ge(sem("ld_dftz"), 16)
            for b in range(4):
                q = b % 2
                cut = slice(q * 512, (q + 1) * 512)
                if b:
                    pe.wait_ge(sem("spec_ready"), 4 * b)
                    pe.wait_ge(sem("conv_step"), 2 * b)
                for n in range(4):
                    for lt in range(TH):
                        ins = mm(ps[:, n, :], dftz[:, n // 2, lt, (n % 2) * P:(n % 2 + 1) * P], seq[:, 0, lt, cut],
                                 lt == 0, lt == 1)
                    ins.then_inc(sem("spec_mm"), 1)
                for lt in range(TH):
                    for n in range(4):
                        if lt == 0:
                            pe.wait_ge(sem("spec_ready"), 4 * b + (1, 3, 2, 4)[n])
                        ins = mm(ps[:, 4 + lt, :], dftz[:, 2 + n // 2, n % 2, lt * P:(lt + 1) * P], yr[:, n, :], n == 0, n == 3)
                    ins.then_inc(sem("inv_mm"), 1)
            pe.wait_ge(sem("conv_step"), 8)
            for c in range(8):
                if c >= 4:
                    pe.wait_ge(sem("yhy_split"), c - 3)
                for h in range(TH):
                    ins = pe.transpose(ps[:, c % 4, h * P:(h + 1) * P], seq[:, 0, h, c * P:(c + 1) * P], ident)
                ins.then_inc(sem("yhy_t"), 1)
            pe.wait_ge(sem("yhy_split"), 8)
            fm_phase("sgu_u", lambda i, s: pe.wait_ge(sem("u_out"), 4 * i + (s + 1)))
            phase("sgu_v", lambda g, i, k: token_major(k, (k // 2) % 4, 4, 4 + 2 * (k // 8), H), per_iter=2)
            pe.wait_ge(sem("v_normed"), 2)
            pe.wait_ge(sem("u_out"), 4 + 8)
            for h in range(8):
                if h >= 4:
                    pe.wait_ge(sem("ysgu_f"), h - 3)
                for n in range(TH):
                    o = ps[:, h % 4, n * P:(n + 1) * P]
                    mm(o, vg[:, n, h * P:(h + 1) * P], wsT[:, h, :], True, False)
                    ins = mm(o, ones[0:1, :], bs[0:1, h, :], False, True)
                ins.then_inc(sem("spatial_mm"), 1)
            pe.wait_ge(sem("ysgu_lo"), 8)
            def branch(name, first_chunk, credit):
                def step(g, i, k):
                    pe.wait_ge(sem(credit), 8 * i + (k + 1))
                    for j in range(8):
                        ins = three(ps[:, k % 4, 0:T], w(k, j * P, P), R(first_chunk + j), j == 0, j == 7)
                    return ins
                phase(name, step)
            fm_phase("gate_hy", lambda i, s: pe.wait_ge(sem("sg1_out"), 4 * i + (s + 1)))
            pe.wait_ge(sem("sg1_out"), 4 + 16)
            branch("branch_hy", 0, "bhy_out")
            pe.wait_ge(sem("bhy_out"), 4 + 16)
            fm_phase("gate_sgu", lambda i, s: pe.wait_ge(sem("sg2_out"), 4 * i + (s + 1)))
            pe.wait_ge(sem("sg2_out"), 4 + 16)
            branch("branch_sgu", 8, "merged_f")
            pe.wait_ge(sem("merged_lo"), 16)
            column_blocks("out2", 4, 4, H)
            turn("hf")
            pe.wait_ge(sem("norm_lo"), norm_count("hf", "lo", 4))
            for part in range(3):
                n0 = sum(FFN_TILES[:part])

                def pair_free(i, s, n0=n0):
                    if s % 2 == 0:
                        pe.wait_ge(sem("ffn_pair"), 2 * i + (n0 + s // 2 + 1))
                fm_phase(f"ffn_in{part}", pair_free)
                pe.wait_ge(sem("ffn_lo"), n0 + FFN_TILES[part])
                column_blocks(f"ffn_down{part}", 8 + 4 * part, FFN_TILES[part] // 4, R)


def _layout(a):
    c = np.ascontiguousarray
    lay = lambda v: v.reshape(-1, P).T

    def fm(w):
        return [w[:, j:j + P].reshape(DC, P, P).transpose(1, 0, 2).reshape(P, UNIT) for j in range(0, w.shape[1], P)]

    def rows(w):
        return [w[:, j:j + P].T for j in range(0, w.shape[1], P)]

    def tm(w):
        return [w[r:r + 512, j:j + 512].reshape(4, P, 512).transpose(1, 0, 2).reshape(P, UNIT)
                for j in range(0, w.shape[1], 512) for r in range(0, w.shape[0], 512)]

    def br(w):
        return [w[:, j:j + 2 * P].reshape(8, P, 2, P).transpose(1, 2, 0, 3).reshape(P, UNIT) for j in range(0, w.shape[1], 2 * P)]

    win = a["w_in"][0]
    o = np.cumsum([0, 512, 512, 512, 512, 128, 128, 512, 512, 512, 512, 128, 128, 128, 128, 128, 128, 24])
    sec = [win[:, o[i]:o[i + 1]] for i in range(17)]
    units = rows(a["ada_w"][0]) + fm(sec[0]) + fm(sec[1]) + tm(sec[2]) + fm(sec[6]) + fm(sec[7]) + tm(sec[8])
    for i in (4, 10, 11, 12, 14, 5, 13, 15):
        units += fm(sec[i])
    units += fm(sec[3]) + fm(sec[9]) + tm(a["w_out"][0])
    for e in range(N_EXP):
        g, u = fm(a["exp_w_gate"][0, e]), fm(a["exp_w_up"][0, e])
        units += [t for pair in zip(g, u) for t in pair] + tm(a["exp_w_down"][0, e])
    w2 = a["w_in_2"][0]
    units += fm(w2[:, 0:3072]) + fm(w2[:, 3072:4096]) + tm(w2[:, 4096:5120])
    units += fm(w2[:, 5120:7168]) + br(a["w_branch_hyena_2"][0]) + fm(w2[:, 7168:9216]) + br(a["w_branch_sgu_2"][0])
    units += tm(a["w_out_2"][0])
    fi, fo = a["w_ffn_in_2"][0], a["w_ffn_out_2"][0]
    n0 = 0
    for n in FFN_TILES:
        g, u = fm(fi[:, n0 * P:(n0 + n) * P]), fm(fi[:, DF + n0 * P:DF + (n0 + n) * P])
        units += [t for pair in zip(g, u) for t in pair] + tm(fo[n0 * P:(n0 + n) * P])
        n0 += n
    stream = np.stack(units)
    del units

    cols = np.zeros((P, NCOLS), np.float32)

    def put(name, v):
        cols[0:v.shape[0], COLS[name]:COLS[name] + v.shape[1]] = v
    for name, key in (("norm1", "norm1_g"), ("norm2", "norm2_g"), ("mixg", "mix_norm_g"),
                      ("normmix2", "norm_mix_g_2"), ("normffn2", "norm_ffn_g_2"), ("ada_b", "ada_b"),
                      ("conv_w", "short_conv_w_2"), ("conv_b", "short_conv_b_2")):
        put(name, lay(a[key]))
    put("fb", np.stack([a["filt_b1_2"][0], a["filt_b2_2"][0], a["filt_b3_2"][0]], 1))
    put("ffreq", a["filt_freq_2"][0][:, None])
    d = dict(shape_tables(), stream=stream, cols=cols, x=a["x"][0], c_row=a["c"].reshape(-1), rel_bias=a["rel_bias"])
    d["w_gate_nsa"] = sec[16].reshape(DC, P, 24).transpose(1, 0, 2)
    d["router_w"] = a["router_w"].reshape(DC, P, N_EXP).transpose(1, 0, 2)
    d["router_bias"], d["sinks"], d["final_g"], d["norm_final_g"] = a["router_bias"], a["sinks"][0], a["final_g"], a["norm_final_g_2"]
    for n in (1, 2, 3):
        d[f"filt_w{n}"] = a[f"filt_w{n}_2"][0]
    d["filt_w4"] = a["filt_w4_2"][0].reshape(64, 2, 2, 2, 512).transpose(2, 3, 0, 1, 4).reshape(4, 64, 1024)
    d["hyena_bias"] = a["hyena_bias_2"][0].reshape(4, 512)
    cmp1 = lambda v: v.reshape(16, P, P).transpose(1, 0, 2)
    d["w1k"], d["w1v"] = cmp1(a["nsa_cmp_w1_k"][0]), cmp1(a["nsa_cmp_w1_v"][0])
    d["w2kv"] = np.stack([a["nsa_cmp_w2_k"][0], a["nsa_cmp_w2_v"][0]], 1)
    d["pe"] = np.stack([a["nsa_pe_k"][0].T, a["nsa_pe_v"][0].T], 1)
    d["ln_g"], d["ln_b"] = a["sgu_ln_g_2"][0], a["sgu_ln_b_2"][0]
    d["w_s"] = a["sgu_w_s_2"][0].transpose(2, 0, 1)
    d["b_s"] = a["sgu_b_s_2"][0].reshape(1, 1024)
    return {k: c(v) for k, v in d.items()}


def kernel(**inputs):
    import concourse.bacc as bacc
    from concourse.bass_utils import run_bass_kernel_spmd as run

    nc = bacc.Bacc("TRN2", target_bir_lowering=False, num_devices=1)
    arrays = _layout({k: np.asarray(v) for k, v in inputs.items()})
    d = {k: nc.dram_tensor(f"in_{k}", v.shape, F32, kind="ExternalInput").ap() for k, v in arrays.items()}
    out = nc.dram_tensor("y", (1, T, D), F32, kind="ExternalOutput").ap()
    two_blocks(nc, d, out)
    r = run(nc, [{f"in_{k}": v for k, v in arrays.items()}], core_ids=[0])
    return r.results[0]["y"]
```

```python
import math
from contextlib import ExitStack

import numpy as np
import concourse.bass as bass
from concourse import mybir

F32 = mybir.dt.float32
F32R = mybir.dt.float32r
ACT = mybir.ActivationFunctionType
ALU = mybir.AluOpType
AX = mybir.AxisListType.X

P = 128
T = 256
TH = T // P
D = 2048
DC = D // P
HD = 64
NH = 8
UNIT = 2048
HALF = UNIT // 2
ARENA = 14400
SLOTS = 4
SCALE = HD ** -0.5
EPS = 1e-6
NEG = -1e30
TINY = float(np.finfo(np.float32).tiny)
N_EXP = 16
N_CMP = 15
DF = 5632
CH = 1024
MAGIC = 1.5 * 2 ** 23
PI_IN = 3.1415925
TWO_PI = (6.28125, 0.0019350051879882812, 3.0199159819e-07)

ADA_UNITS = 5 * DC
LATE_UNITS = DC
PHASES = [
    ("a_q", 4), ("a_k", 4), ("a_v", 4), ("c_q", 4), ("c_k", 4), ("c_v", 4), ("b_q", 4), ("small", 8),
    ("d_q", 4), ("mix_out", 16), ("moe", 12 * N_EXP), ("hyena", 24), ("sgu_u", 8), ("sgu_v", 8),
    ("gate_hy", 16), ("branch_hy", 8), ("gate_sgu", 16), ("branch_sgu", 8), ("out2", 16),
    ("ffn_in0", 32), ("ffn_down0", 16), ("ffn_in1", 32), ("ffn_down1", 16), ("ffn_in2", 24), ("ffn_down2", 12),
]
NORMS = [("h1", 16), ("mixA", 4), ("mixC", 4), ("mixB", 4), ("mixD", 4), ("hm", 16), ("x1", 0), ("h2", 16), ("hf", 16), ("y", 0)]


SHARED = {"hm": 2 + 4, "hf": 2 + 8, "y": 2 + 20}


def norm_count(name, kind, n):
    for other, tiles in NORMS:
        if other == name:
            return n
        n += {"sq": 2 - (other in SHARED), "ms": 1, "rt": 1, "rs": tiles == 16, "xa": tiles == 16, "xh": 2 * (tiles > 0) - (tiles == 16), "t": tiles // 2, "f": tiles // 4, "hi": tiles // 4,
              "lo": tiles // 4}[kind]


FFN_TILES = (16, 16, 12)
BASE, UNITS = {}, 0
for _name, _n in PHASES:
    BASE[_name] = UNITS
    UNITS += _n
SIZE = dict(PHASES)

COLS, NCOLS = {}, 0
for _name, _n in [("norm1", 16), ("norm2", 16), ("mixg", 16), ("normmix2", 16), ("normffn2", 16),
                  ("ada_b", 96), ("conv_w", 72), ("conv_b", 24), ("fb", 3), ("ffreq", 1)]:
    COLS[_name] = NCOLS
    NCOLS += _n

TAB_ID, TAB_TRI, TAB_CADD, TAB_C01, TAB_FLIP, NTAB = 0, 128, 144, 176, 208, 336


def t5_buckets(dist):
    f = np.float32
    large = 16 + (np.log(np.maximum(dist, 1).astype(f) / f(16)) / f(math.log(2048 / 16)) * f(16)).astype(np.int32)
    return np.where(dist < 16, dist, np.minimum(large, 31))


def shape_tables():
    f = np.float32
    tab = np.zeros((P, NTAB), f)
    tab[:, TAB_ID:TAB_ID + P] = np.eye(P)
    tab[:, TAB_TRI:TAB_TRI + 16] = (np.arange(4)[None, :] < np.arange(4)[:, None]).reshape(1, 16)
    tab[:, TAB_FLIP:TAB_FLIP + P] = np.eye(P)[::-1]
    pos = np.arange(P)[:, None, None] + P * np.arange(TH)[None, :, None]
    seen = (np.arange(16)[None, None, :] * 16 + 31 <= pos) & (np.arange(16) < N_CMP)
    tab[:, TAB_CADD:TAB_CADD + 32] = np.where(seen, 0.0, NEG).reshape(P, 32)
    tab[:, TAB_C01:TAB_C01 + 32] = seen.reshape(P, 32)
    dist = 255 - np.arange(384)
    ok = dist >= 0
    onehot = np.zeros((36, 384), f)
    onehot[t5_buckets(np.maximum(dist, 0))[ok], np.arange(384)[ok]] = 1.0
    times = ok * ((dist <= 128).astype(int) + (dist % 4 == 0) + (dist % 16 == 0))
    onehot[32] = np.where(times > 0, np.log(np.maximum(times, 1)), NEG)
    onehot[33] = np.where(ok & (dist <= 127), 0.0, NEG)
    onehot[34] = onehot[35] = np.where(ok, 0.0, NEG)
    owner = np.zeros((4, 32), f)
    for m in range(4):
        owner[m, 8 * m:8 * m + 8] = 1.0
    n = np.arange(T, dtype=np.float64)
    ang = 2 * math.pi * np.outer(n, n) / (2 * T)
    cos, sin = np.cos(ang), -np.sin(ang)
    alt = (-1.0) ** n
    zs = sin.copy(); zs[:, 0] = alt
    c0 = cos[:, :P].copy(); c0[:, 0] = alt
    ic = cos * 2 / (2 * T); ic[0] = 1 / (2 * T)
    inv_s = sin * 2 / (2 * T); inv_s[0] = alt / (2 * T)
    rows = lambda m: m.reshape(TH, P, -1).transpose(1, 0, 2).reshape(P, -1).astype(f)
    dft_k = np.concatenate([rows(cos), rows(sin), rows(c0)], 1)
    dft_z = np.concatenate([rows(cos), rows(zs), rows(ic), rows(inv_s)], 1)
    t = (np.arange(T, dtype=f) * f(1 / f(T - 1))).astype(f)
    w = f(2 * math.pi) * np.arange(T, dtype=f) / f(T)
    s = np.arange(16, dtype=f) / f(15)
    fr = (f(1e-4) * (f(1) - s) + f(15) * s).astype(f)
    fw = (fr[:, None] * w[None, :]).astype(f).astype(np.float64)
    zt = np.concatenate([t[None], np.cos(fw), -np.sin(fw)], 0).astype(f)
    lo, hi = math.log(1e-2) / 1.5, math.log(1e-2) / 0.3
    dl = np.abs(np.linspace(lo, hi, CH, dtype=f))
    decay = np.exp(-(t[:, None] * dl[None]).astype(f).astype(np.float64)).astype(f)
    decay = decay.reshape(TH, P, 2, 512).transpose(2, 1, 0, 3)
    decay = np.concatenate([decay, decay]).reshape(4, P, 1024)
    return dict(tab=tab, onehot=onehot, owner=owner, dft_k=dft_k, dft_z=dft_z, zt=zt, decay=decay)


class Chain:

    def __init__(self, engine, sem):
        self.engine, self.sem, self.n, self.off = engine, sem, 0, 0

    def __call__(self, instruction):
        self.n += 1
        instruction.then_inc(self.sem, 1)
        self.engine.wait_ge(self.sem, self.n + self.off)

    def enter(self, i, per):
        self.start, self.per, self.off = self.n, per, i * per

    def leave(self, times):
        assert self.n - self.start == self.per, (self.n - self.start, self.per)
        self.n, self.off = self.n + self.per * (times - 1), 0


def two_blocks(nc, d, out):
    with ExitStack() as ctx:
        def sb(name, shape, dt=F32):
            return ctx.enter_context(nc.sbuf_tensor(name, shape, dt))

        raw = sb("raw", [P, SLOTS, UNIT])
        w_hi = sb("w_hi", [P, 4, HALF], F32R)
        w_lo = sb("w_lo", [P, 4, HALF], F32R)
        x = sb("x", [P, TH, D])
        h_hi = sb("h_hi", [P, DC, T], F32R)
        h_lo = sb("h_lo", [P, DC, T], F32R)
        r_hi = sb("r_hi", [P, 16, T], F32R)
        r_lo = sb("r_lo", [P, 16, T], F32R)
        n_hi = sb("n_hi", [P, DC, 24], F32R)
        n_lo = sb("n_lo", [P, DC, 24], F32R)
        cols = sb("cols", [P, NCOLS])
        tab = sb("tab", [P, NTAB])
        ones = sb("ones", [P, P])
        mod = sb("mod", [P, 6 * DC])
        gain = sb("gain", [P, DC])
        stat = sb("stat", [P, 160])
        gates = sb("gates", [P, TH, 24])
        comb = sb("comb", [P, TH, N_EXP])
        arena = sb("arena", [P, ARENA])

        def at(off, *shape, parts=P):
            assert off + int(np.prod(shape)) <= ARENA
            v = arena[0:parts, off:off + int(np.prod(shape))]
            if len(shape) == 2:
                v = v.rearrange("p (a b) -> p a b", a=shape[0])
            if len(shape) == 3:
                v = v.rearrange("p (a b c) -> p a b c", a=shape[0], b=shape[1])
            return v

        ident = tab[:, TAB_ID:TAB_ID + P]
        flip = tab[:, TAB_FLIP:TAB_FLIP + P]

        def col(name, n=1):
            return cols[:, COLS[name]:COLS[name] + n]

        qT2, toep2 = x[0:64, 0, :].rearrange("p (h t) -> p h t", h=8), x[:, 1, :].rearrange("p (h t) -> p h t", h=8)
        late_slot, late_c = at(4096, UNIT), at(6144, D)
        mod_sums = stat[:, 144:148]

        ps = ctx.enter_context(nc.psum_tensor("ps", [P, 8, 512], F32))

        brow = nc.dram_tensor("bias_rows", (32, 384), F32, kind="Internal").ap()
        kf_dram = nc.dram_tensor("filters", (4, P, 5 * 512), F32, kind="Internal").ap()

        sems = {}

        def sem(name):
            if name not in sems:
                sems[name] = ctx.enter_context(nc.semaphore(name))
            return sems[name]

        landed = [sem(f"landed{s}") for s in range(SLOTS)]
        ada_done, hi_ready, lo_ready, half_done = sem("ada_done"), sem("hi_ready"), sem("lo_ready"), sem("half_done")
        mod_ready = sem("mod_ready")

        F_DFT, F_ZT, F_W1, F_W2, F_W3 = 0, 1280, 1536, 1600, 1664
        F_A, F_T, F_R, F_H = 1792, 2048, 2304, 2560
        F_W4, F_DEC, F_HB, F_TAPS, F_ABS, F_RN, F_KO = 2816, 3840, 4864, 5376, 7424, F_A, 9472
        F_RELB, F_ONEH, F_BOUT = F_KO, F_KO + 32, F_KO + 416
        F_C = 12032
        c_row = at(F_C, D)
        qT, kT, v_a = at(0, 8, T, parts=64), at(2048, 8, T, parts=64), at(4096, TH, 512)
        smk, smv = at(2048, 5, 2, T), at(4608, 3, 2, P)
        toep = at(5376, 8, T)
        mix = at(7424, TH, 512)
        prob, pT = at(9216, 2, 384), at(9984, 2, 384)
        blocks = at(10752, 2, 16 * 30)
        hidc, kc, vc = at(11712, 2, 30), at(11772, 2, N_CMP, parts=64), at(11808, 2, HD, parts=N_CMP)
        cs, cp = at(11936, 8, 2, 16), at(12192, 8, 2, 16)
        cpT = at(12448, 512)
        mixf = at(12960, 4, T)
        mix_junk = at(12960, TH, 512)
        w1v, w2c, peT = at(5376, 16, P), at(13984, 2, HD), at(14112, 2, 32, parts=64)
        v_f = at(9216, 3, T)
        narrow_f, narrow_r = at(9984, T, parts=24), at(10496, T, parts=16)
        w1k = x[:, 0, :].rearrange("p (r n) -> p r n", r=16)
        xhat, hf = at(0, TH, D), at(4096, DC, T)
        row = at(8192, D)
        diag = at(10240, 8, P)
        acc = at(0, TH, D)
        g_act, hid = at(10496, 2, T), at(11008, 2, T)
        ro = 12000
        cvT = at(0, 24, T)
        seq = at(6144, 3, TH, CH)

        def seq_pair(n):
            c = 2 * n
            return seq[:, c // 8, :, (c % 8) * P:(c % 8 + 2) * P].rearrange("p h (c n) -> p c h n", c=2)

        def bank_pair(n):
            return ps[:, n % 4, :].rearrange("p (c h n) -> p c h n", c=2, h=2)

        kf, dftz = at(0, 5, 512), at(2560, 4, 2, T)
        prods = at(4608, 2, 512)
        yr = at(12288, 4, 512)
        uT, vg, ln_row = at(0, 8, T), at(2048, TH, CH), at(4096, 2, CH)
        wsT, bs = at(6144, 8, P), at(7168, 8, P)
        yf = at(8192, 2, T)
        sg1, sg2 = at(0, DC, T), at(4096, DC, T)
        mf = at(8192, 2, T)

        block = ctx.enter_context(nc.Block())

        def group_base(phase):
            return BASE[phase] // SLOTS

        def run_groups(engine, phase, body, per_iter=1, before=None, after=None):
            gb, n = group_base(phase), SIZE[phase] // SLOTS // per_iter
            final = BASE[phase] + SIZE[phase] == UNITS
            body_n = n - final
            if body_n == 1:
                body(gb, 0, False)
            elif body_n > 1:
                with engine.Fori(0, body_n) as i:
                    if before:
                        before(i)
                    body(gb + per_iter * i, i, False)
                if after:
                    after(body_n)
            if final:
                if before:
                    before(0)
                body(gb + per_iter * (n - 1), n - 1, True)
                if after:
                    after(1)

        @block.sync
        def _(sp):
            for s in range(SLOTS):
                sp.dma_start(raw[:, s, :], d["stream"][s]).then_inc(landed[s], 16)
            sp_units = d["stream"]
            with sp.Fori(1, ADA_UNITS // SLOTS) as g:
                for s in range(SLOTS):
                    sp.wait_ge(ada_done, 4 * g + s - 3)
                    sp.dma_start(raw[:, s, :], sp_units[bass.ds(4 * g + s, 1)].rearrange("a p n -> (a p) n"))\
                        .then_inc(landed[s], 16)
            for s in range(SLOTS):
                sp.wait_ge(ada_done, ADA_UNITS - 3 + s)
                sp.dma_start(raw[:, s, :], sp_units[ADA_UNITS + s]).then_inc(landed[s], 16)
            with sp.Fori(1, UNITS // SLOTS) as g:
                for s in range(SLOTS):
                    sp.wait_ge(lo_ready, 8 * g + 2 * s - 6)
                    sp.dma_start(raw[:, s, :],
                                 sp_units[bass.ds(ADA_UNITS + 4 * g + s, 1)].rearrange("a p n -> (a p) n"))\
                        .then_inc(landed[s], 16)
            for h in range(TH):
                sp.wait_ge(sem("y_ready"), h + 1)
                sp.dma_start(out[0, h * P:(h + 1) * P, :], x[:, h, :]).then_inc(sem("y_stored"), 16)
            sp.wait_ge(sem("y_stored"), 16 * TH)

        @block.gpsimd
        def _(pool):
            def load(name, *pairs):
                for dst, src in pairs:
                    pool.dma_start(dst, src).then_inc(sem(name), 16)

            load("ld_small", (cols[:, :], d["cols"]), (tab[:, :], d["tab"]))
            pool.memset(ones[:, :], 1.0).then_inc(sem("ones_set"), 1)
            load("ld_bias", (at(F_RELB, 32, parts=32), d["rel_bias"]), (arena[32:36, F_RELB:F_RELB + 32], d["owner"]),
                 (at(F_ONEH, 384, parts=36), d["onehot"]))
            load("ld_filt", (at(F_DFT, 1280), d["dft_k"]), (at(F_ZT, T, parts=33), d["zt"]),
                 (at(F_W1, 64, parts=33), d["filt_w1"]), (at(F_W2, 64, parts=64), d["filt_w2"]),
                 (at(F_W3, 64, parts=64), d["filt_w3"]))
            load("ld_c", (c_row, d["c_row"].partition_broadcast(P)))
            x_rows = d["x"].rearrange("(h p) n -> p h n", p=P)
            load("ld_x", (x[:, :, :], x_rows))
            pool.wait_ge(sem("bias_rows_out"), 1)
            pool.dma_start(brow, at(F_BOUT, 384, parts=32)).then_inc(sem("brow_stored"), 16)
            with pool.Fori(0, 4) as b:
                load("ld_block", (at(F_W4, 1024, parts=64), d["filt_w4"][bass.ds(b, 1)].rearrange("a p n -> (a p) n")),
                     (at(F_DEC, 1024), d["decay"][bass.ds(b, 1)].rearrange("a p n -> (a p) n")),
                     (at(F_HB, 512), d["hyena_bias"][bass.ds(b, 1)].rearrange("a n -> (a n)").partition_broadcast(P)))
                pool.wait_ge(sem("spectrum_out"), 5 * b + 5)
                pool.dma_start(kf_dram[bass.ds(b, 1)].rearrange("a p n -> (a p) n"), at(F_KO, 2560))\
                    .then_inc(sem("kf_stored"), 16)
                pool.wait_ge(sem("kf_stored"), 16 * b + 16)
            pool.wait_ge(sem("brow_stored"), 16)
            pool.wait_ge(sem("kf_stored"), 64)
            pool.wait_ge(mod_ready, ADA_UNITS // 4)
            load("ld_narrow", (at(12960, DC, 24), d["w_gate_nsa"]))
            pool.wait_ge(sem("norm_lo"), norm_count("h1", "lo", 4))

            def toeplitz(m, toep):
                src = bass.AP(tensor=brow.tensor, offset=8 * m * 384, ap=[[1, P], [384, 8], [1, T]])
                load("ld_toep" if m in (0, 3) else "ld_toep2", (toep, src))

            toeplitz(0, toep)
            toeplitz(2, toep2)
            load("ld_sink", (stat[:, 32:40], d["sinks"].partition_broadcast(P)))
            pool.wait_ge(sem("att_out"), 16 * 2)
            toeplitz(1, toep2)
            load("ld_cmp", (w1k, d["w1k"]), (w1v, d["w1v"]), (w2c, d["w2kv"]), (peT, d["pe"]))
            pool.wait_ge(sem("cmp_hidden"), 2)
            toeplitz(3, toep)
            pool.wait_ge(sem("att_out"), 16 * 3)
            load("ld_x", (x[:, 1, :], x_rows[:, 1, :]))
            pool.wait_ge(sem("att_out"), 82)
            load("ld_x", (x[:, 0, :], x_rows[:, 0, :]))
            pool.wait_ge(sem("norm_lo"), norm_count("hm", "lo", 4))
            load("ld_c", (late_c, d["c_row"].partition_broadcast(P)))
            load("ld_router", (at(ro, DC, 16), d["router_w"]), (at(ro + 256, 16), d["router_bias"].partition_broadcast(P)))
            pool.wait_ge(sem("x_moe"), 2)
            load("ld_rowg", (row, d["final_g"].partition_broadcast(P)))
            pool.wait_ge(sem("seq_t"), 12)
            load("ld_dftz", (at(2560, 2048), d["dft_z"]))
            for b in range(4):
                if b:
                    pool.wait_ge(sem("spec_ready"), 4 * b)
                load("ld_kf", (at(0, 2560), kf_dram[b]))
            pool.wait_ge(sem("yhy_split"), 8)
            load("ld_sgu", (at(4096, CH), d["ln_g"].partition_broadcast(P)), (at(5120, CH), d["ln_b"].partition_broadcast(P)),
                 (wsT, d["w_s"]), (at(7168, 1024, parts=1), d["b_s"]))
            pool.wait_ge(sem("cols_added"), 2 + 8)
            load("ld_rowf", (row, d["norm_final_g"].partition_broadcast(P)))

        @block.scalar
        def _(act):
            def hi(g, k):
                s, static = (k // 2) % SLOTS, isinstance(g, int)
                if k % 2 == 0:
                    act.wait_ge(landed[s], 16 * (ADA_UNITS // SLOTS + 1) + 16 * (g + k // 8))
                if not (static and 8 * g + k < 4):
                    act.wait_ge(half_done, 8 * g + (k - 3))
                act.activation(w_hi[:, k % 4, :], raw[:, s, (k % 2) * HALF:(k % 2 + 1) * HALF], ACT.Copy)\
                    .then_inc(hi_ready, 1)

            def load_mod(dst, j):
                act.wait_ge(ada_done, j)
                act.dma_start(dst, d["mod_units"][bass.ds(j - ADA_UNITS, 1)].rearrange("a p n -> (a p) n"))\
                    .then_inc(sem("mod_landed"), 16)

            def phase(name, step=None, per_iter=1):
                def body(g, i, final):
                    for k in range(8 * per_iter):
                        if not (final and k + 3 >= 8 * per_iter):
                            hi(g, k + 3)
                        if step:
                            step(g, i, k)
                run_groups(act, name, body, per_iter)

            def done(g, k):
                act.wait_ge(half_done, 8 * g + (k + 1))

            def copy(dst, src):
                return act.activation(dst, src, ACT.Copy)

            act.wait_ge(sem("ld_c"), 16)
            act.activation(c_row, c_row, ACT.Silu).then_inc(sem("c_ready"), 1)
            for n in range(3):
                act.wait_ge(sem("sin_arg"), n + 1)
                act.activation(at(F_H, T, parts=64), at(F_R, T, parts=64), ACT.Sin).then_inc(sem("sin_out"), 1)
            def norm(name, ready, width=D, src=x, spread=True, dst=h_hi, tiles=DC, f=hf, junk=xhat, first=0):
                norm_root(name, ready, width, src, junk, xhat if spread and width == D else None)
                if spread:
                    norm_hi(name, dst, tiles, f, first)

            def norm_root(name, ready, width, src, junk, unit=None):
                halves = ready[0] in ("x_moe", "x1_done")
                for h in range(1 if name in SHARED else TH):
                    if halves or h == 0:
                        act.wait_ge(sem(ready[0]), ready[1] - (halves and h == 0))
                    act.activation(junk[:, h, 0:width], src[:, h, 0:width], ACT.Square,
                                   accum_out=stat[:, h:h + 1]).then_inc(sem("norm_sq"), 1)
                act.wait_ge(sem("norm_ms"), norm_count(name, "ms", 1))
                act.activation(stat[:, 4:6], stat[:, 2:4], ACT.Sqrt).then_inc(sem("norm_rt"), 1)
                if unit is not None:
                    act.wait_ge(sem("norm_rs"), norm_count(name, "rs", 1))
                    act.activation(unit[:, 0, :], src[:, 0, :], ACT.Copy, scale=stat[:, 6:7]).then_inc(sem("norm_xa"), 1)

            def norm_hi(name, dst, tiles, f, first):
                for c in range(0, tiles, 4):
                    act.wait_ge(sem("norm_f"), norm_count(name, "f", c // 4 + 1))
                    copy(dst[:, first + c:first + c + 4, :], f[:, c:c + 4, :]).then_inc(sem("norm_hi"), 1)

            norm_root("h1", ("ld_x", 16), D, x, at(F_TAPS, TH, D), unit=x)
            with act.Fori(0, 4) as b:
                for n in range(4):
                    act.wait_ge(sem("taps_ready"), 4 * b + n + 1)
                    act.activation(at(F_ABS + 512 * n, 512), at(F_TAPS + 512 * n, 512), ACT.Abs).then_inc(sem("abs_ready"), 1)
            norm_hi("h1", h_hi, DC, hf, 0)
            act.wait_ge(sem("ld_narrow"), 16)
            copy(n_hi[:, :, :], at(12960, DC, 24)).then_inc(sem("narrow_hi"), 1)
            for k in range(3):
                hi(0, k)

            def heads_out(dst, sem_name, bank=lambda s: s):
                def step(g, i, k):
                    if k % 2 == 0:
                        return
                    done(g, k)
                    s = k // 2
                    copy(dst[:, 2 * s, :], ps[0:64, bank(s), 0:T]).then_inc(sem(sem_name), 1)
                    copy(dst[:, 2 * s + 1, :], ps[64:128, bank(s), 0:T]).then_inc(sem(sem_name), 1)
                return step

            def values_out(sem_name):
                def step(g, i, k):
                    if k == 7:
                        done(g, k)
                        for h in range(TH):
                            copy(v_a[:, h, :], ps[:, 4 + h, :]).then_inc(sem(sem_name), 1)
                return step

            def exps(first, n, sink, beside=None, dst=None):
                if beside:
                    g, heads = group_base(beside), heads_out(dst, "q_out", lambda s: 6 + s % 2)
                for t in range(n + 1):
                    if t < n:
                        a = first + t
                        act.wait_ge(sem("att_max"), a + 1)
                        if a >= 2:
                            act.wait_ge(sem("att_t"), a - 1)
                        if sink:
                            act.activation(stat[:, 128 + 2 * (t % 4):130 + 2 * (t % 4)], stat[:, 8 + 2 * (t % 2):10 + 2 * (t % 2)],
                                           ACT.Exp, bias=stat[:, 32 + t:33 + t]).then_inc(sem("sink_exp"), 1)
                        for h, (lo, w) in enumerate(((0, 128), (128, 256))):
                            act.activation(prob[:, t % 2, lo:lo + w], ps[:, t % 2, lo:lo + w], ACT.Exp,
                                           scale=SCALE, bias=stat[:, 8 + 2 * (t % 2) + h:9 + 2 * (t % 2) + h],
                                           accum_out=stat[:, 120 + 2 * (t % 4) + h:121 + 2 * (t % 4) + h]).then_inc(sem("att_p"), 1)
                    if t >= 1:
                        a = first + t - 1
                        act.wait_ge(sem("att_t"), a + 1)
                        if a >= 2:
                            act.wait_ge(sem("att_pv"), a - 1)
                        copy(pT[:, (t - 1) % 2, :], ps[:, 2 + (t - 1) % 2, 0:384]).then_inc(sem("att_pt"), 1)
                        if beside:
                            heads(g, 0, t - 1)
                    if beside and t < 8:
                        hi(g, t + 3)

            phase("a_q", heads_out(qT, "q_out"))
            phase("a_k", heads_out(kT, "k_out"))
            phase("a_v", values_out("v_out"))
            exps(0, 8, False, "c_q", qT2)
            norm_root("mixA", ("att_out", 16), 512, mix, mix_junk)
            phase("c_k", heads_out(kT, "k_out"))
            norm_hi("mixA", r_hi, 4, mixf, 0)
            phase("c_v", values_out("v_out"))
            exps(8, 8, False, "b_q", qT)
            norm_root("mixC", ("att_out", 32), 512, mix, mix_junk)

            def small_out(g, i, k):
                if k % 2 == 0:
                    return
                u = k // 2
                done(g, k)
                if u < 5:
                    copy(smk[0:64, u, 0, :], ps[0:64, u % 4, 0:T]).then_inc(sem("small_out"), 1)
                    copy(smk[0:64, u, 1, :], ps[64:128, u % 4, 0:T]).then_inc(sem("small_out"), 1)
                else:
                    copy(v_f[:, u - 5, :], ps[:, u % 4, 0:T]).then_inc(sem("small_out"), 1)
            phase("small", small_out, per_iter=2)
            act.wait_ge(sem("v_turned"), 1)
            for h in range(TH):
                copy(smv[:, :, h, :], ps[:, 4 + h, 0:3 * P].rearrange("p (a b) -> p a b", a=3)).then_inc(sem("v_small"), 1)
            act.wait_ge(sem("narrow_mm"), 1)
            copy(narrow_f, ps[0:24, 6, 0:T]).then_inc(sem("narrow_out"), 1)
            norm_hi("mixC", r_hi, 4, mixf, 8)
            act.wait_ge(sem("narrow_t"), 1)
            act.activation(gates[:, :, :], ps[:, 7, 0:48].rearrange("p (h n) -> p h n", h=2), ACT.Sigmoid)\
                .then_inc(sem("gates_ready"), 1)
            for n in range(2):
                act.wait_ge(sem("cmp_hidden"), n + 1)
                act.activation(hidc[:, n, :], ps[:, n, 0:30], ACT.Gelu_apprx_tanh).then_inc(sem("hid_act"), 1)
            act.wait_ge(sem("cmp_kv"), 1)
            copy(kc, ps[0:64, 2, 0:30].rearrange("p (a b) -> p a b", a=2)).then_inc(sem("kc_ready"), 1)
            copy(vc, ps[0:N_CMP, 3, 0:128].rearrange("p (a b) -> p a b", a=2)).then_inc(sem("kc_ready"), 1)
            exps(16, 8, True, "d_q", qT2)
            norm_root("mixB", ("att_out", 48), 512, mix, mix_junk)
            act.wait_ge(sem("cmp_max"), 1)
            act.activation(cp[:, :, :, 0:N_CMP], cs[:, :, :, 0:N_CMP], ACT.Exp).then_inc(sem("cmp_exp"), 1)
            norm_hi("mixB", r_hi, 4, mixf, 4)
            for r in range(4):
                act.wait_ge(sem("cmp_t"), r + 1)
                if r >= 1:
                    act.wait_ge(sem("cmp_pv"), r)
                copy(cpT[0:N_CMP, :], ps[0:N_CMP, 6, :]).then_inc(sem("cmp_pt"), 1)
            exps(24, 16, False)
            norm("mixD", ("att_out", 82), 512, mix, True, r_hi, 4, mixf, mix_junk, 12)
            phase("mix_out")
            norm("hm", ("cols_added", SHARED["hm"]))
            act.wait_ge(sem("ld_c"), 32)
            act.activation(late_c, late_c, ACT.Silu).then_inc(sem("c_ready"), 1)
            act.wait_ge(sem("ld_router"), 32)
            copy(n_hi[:, :, 0:16], at(ro, DC, 16)).then_inc(sem("router_hi"), 1)
            act.wait_ge(sem("narrow_mm"), 2)
            copy(narrow_r, ps[0:16, 6, 0:T]).then_inc(sem("narrow_out"), 1)
            act.wait_ge(sem("narrow_t"), 2)
            act.activation(at(ro + 272, TH, 16), ps[:, 7, 0:32].rearrange("p (h n) -> p h n", h=2), ACT.Sigmoid).then_inc(sem("affinity"), 1)

            def expert_step(g, i, k):
                u = k // 2
                if k == 0:
                    load_mod(late_slot, i + ADA_UNITS)
                if u >= 8 or k % 4 == 0 or k % 4 == 2:
                    return
                f = u // 2
                if k % 4 == 1:
                    done(g, k)
                    act.wait_ge(sem("moe_pair"), 4 * i + f + 1)
                    act.activation(g_act[:, f % 2, :], ps[:, u % 4, 0:T], ACT.Silu).then_inc(sem("moe_silu"), 1)
                else:
                    act.wait_ge(sem("moe_pair"), 4 * i + f + 3)
                    copy(r_hi[:, f, :], hid[:, f % 2, :]).then_inc(sem("moe_hi"), 1)
            phase("moe", expert_step, per_iter=3)
            norm("x1", ("x_moe", 2), spread=False)
            norm("h2", ("x1_done", 2))

            phase("hyena")
            for n in range(1, 12, 2):
                act.wait_ge(sem("seq_t"), n + 1)
                copy(seq_pair(n), bank_pair(n)).then_inc(sem("seq_odd"), 1)
            for c in range(8):
                act.wait_ge(sem("yhy_t"), c + 1)
                copy(r_hi[:, c, :], ps[:, c % 4, 0:T]).then_inc(sem("yhy_hi"), 1)

            def gelu_u(g, i, k):
                if k % 2:
                    done(g, k)
                    act.activation(uT[:, bass.ds(4 * i + k // 2, 1), :],
                                   ps[:, k // 2:k // 2 + 1, 0:T], ACT.Gelu)\
                        .then_inc(sem("u_out"), 1)
            phase("sgu_u", gelu_u)

            def gelu_v(g, i, k):
                if k % 8 == 7:
                    cb = k // 8
                    done(g, k)
                    for h in range(TH):
                        act.activation(vg[:, h, cb * 512:(cb + 1) * 512], ps[:, 4 + 2 * cb + h, :], ACT.Gelu)\
                            .then_inc(sem("v_gelu"), 1)
            phase("sgu_v", gelu_v, per_iter=2)
            act.wait_ge(sem("ln_var"), 1)
            act.activation(stat[:, 4:6], stat[:, 2:4], ACT.Sqrt).then_inc(sem("ln_rt"), 1)
            for h in range(8):
                act.wait_ge(sem("ysgu_f"), h + 1)
                copy(r_hi[:, 8 + h, :], yf[:, h % 2, :]).then_inc(sem("ysgu_hi"), 1)

            def sigmoid(dst, name):
                def step(g, i, k):
                    if k % 2:
                        done(g, k)
                        act.activation(dst[:, bass.ds(4 * i + k // 2, 1), :], ps[:, k // 2:k // 2 + 1, 0:T], ACT.Sigmoid)\
                            .then_inc(sem(name), 1)
                return step
            phase("gate_hy", sigmoid(sg1, "sg1_out"))
            phase("branch_hy")
            phase("gate_sgu", sigmoid(sg2, "sg2_out"))

            def merged_hi(g, i, k):
                act.wait_ge(sem("merged_f"), 8 * i + k + 5)
                copy(h_hi[:, bass.ds(8 * i + k, 1), :], mf[:, k % 2:k % 2 + 1, :]).then_inc(sem("merged_hi"), 1)
            phase("branch_sgu", merged_hi)
            phase("out2")
            norm("hf", ("cols_added", SHARED["hf"]))

            for part in range(3):
                def ffn_step(g, i, k, part=part):
                    n0 = sum(FFN_TILES[:part])
                    f = k // 4
                    if k % 4 == 1:
                        done(g, k)
                        act.wait_ge(sem("ffn_pair"), 2 * i + (n0 + f + 1))
                        act.activation(g_act[:, f, :], ps[:, k // 2, 0:T], ACT.Silu).then_inc(sem("ffn_silu"), 1)
                    elif k % 4 == 3:
                        act.wait_ge(sem("ffn_pair"), 2 * i + (n0 + f + 3))
                        copy(r_hi[:, bass.ds(2 * i + f, 1), :], hid[:, f:f + 1, :]).then_inc(sem("ffn_hi"), 1)
                phase(f"ffn_in{part}", ffn_step)
                phase(f"ffn_down{part}")
            norm("y", ("cols_added", SHARED["y"]), spread=False)

        @block.vector
        def _(dve):
            ch = Chain(dve, sem("dve_chain"))

            def lo(g, k):
                s = (k // 2) % SLOTS
                dve.wait_ge(hi_ready, 8 * g + (k + 1))
                dve.tensor_tensor(w_lo[:, k % 4, :], raw[:, s, (k % 2) * HALF:(k % 2 + 1) * HALF],
                                  w_hi[:, k % 4, :].bitcast(F32), ALU.subtract).then_inc(lo_ready, 1)

            def phase(name, step=None, per_iter=1, links=0, early=None):
                def body(g, i, final):
                    for k in range(8 * per_iter):
                        if early:
                            early(i, k)
                        if not (final and k + 3 >= 8 * per_iter):
                            lo(g, k + 3)
                        if step:
                            step(g, i, k)
                before = (lambda i: ch.enter(i, links)) if links else None
                run_groups(dve, name, body, per_iter, before, ch.leave if links else None)

            def done(g, k):
                dve.wait_ge(half_done, 8 * g + (k + 1))

            for name, n in (("moe_pair", 2), ("ffn_pair", 2), ("down_out", 2), ("cols_added", 2),
                            ("conv_out", 4), ("bhy_out", 4), ("merged_f", 4), ("u_out", 4), ("sg1_out", 4), ("sg2_out", 4)):
                dve.sem_inc(sem(name), n)

            def norm(name, width=D, src=x, spread=True, dst=(h_hi, h_lo), tiles=DC, f=hf, xh=xhat, first=0, gain=None, bias=None):
                norm_unit(name, width, src, spread, xh)
                if spread:
                    norm_split(name, dst, tiles, f, first, gain, bias)

            def norm_unit(name, width, src, spread, xh):
                if name in SHARED:
                    dve.wait_ge(sem("cols_added"), SHARED[name])
                    ch(dve.tensor_tensor_reduce(xhat[:, 1, :], src[:, 1, :], src[:, 1, :], 1.0, 0.0, ALU.mult, ALU.add, stat[:, 1:2]))
                dve.wait_ge(sem("norm_sq"), norm_count(name, "sq", 1 if name in SHARED else 2))
                dve.tensor_scalar(stat[:, 2:4], stat[:, 0:2], 1.0 / width, EPS, ALU.mult, ALU.add).then_inc(sem("norm_ms"), 1)
                dve.wait_ge(sem("norm_rt"), norm_count(name, "rt", 1))
                if spread and width == D:
                    dve.reciprocal(stat[:, 6:8], stat[:, 4:6]).then_inc(sem("norm_rs"), 1)
                    dve.wait_ge(sem("norm_rs"), norm_count(name, "rs", 1))
                else:
                    ch(dve.reciprocal(stat[:, 6:8], stat[:, 4:6]))
                if not spread:
                    return
                for h in range(1 if width == D else 0, TH):
                    dve.tensor_scalar(xh[:, h, 0:width], src[:, h, 0:width], stat[:, 6 + h:7 + h], None, ALU.mult)\
                        .then_inc(sem("norm_xh"), 1)

            def norm_split(name, dst, tiles, f, first, gain, bias):
                def low(c):
                    dve.wait_ge(sem("norm_hi"), norm_count(name, "hi", c // 4 + 1))
                    dve.tensor_tensor(dst[1][:, first + c:first + c + 4, :], f[:, c:c + 4, :],
                                      dst[0][:, first + c:first + c + 4, :].bitcast(F32), ALU.subtract)\
                        .then_inc(sem("norm_lo"), 1)
                for c in range(tiles):
                    if c % 2 == 0:
                        dve.wait_ge(sem("norm_t"), norm_count(name, "t", c // 2 + 1))
                    src_ps = ps[:, (c // 2) % 4, (c % 2) * T:(c % 2 + 1) * T]
                    if bias is None:
                        ins = dve.tensor_scalar(f[:, c, :], src_ps, gain[:, c:c + 1], None, ALU.mult)
                    else:
                        ins = dve.tensor_scalar(f[:, c, :], src_ps, gain[:, c:c + 1], bias[:, c:c + 1], ALU.mult, ALU.add)
                    if c % 4 == 3:
                        ins.then_inc(sem("norm_f"), 1)
                        dve.wait_ge(sem("norm_f"), norm_count(name, "f", c // 4 + 1))
                        if c >= 7:
                            low(c - 7)
                low(tiles - 4)

            def modulation(g):
                if not (isinstance(g, int) and g == 0):
                    dve.wait_ge(mod_ready, g)
                for s in range(SLOTS):
                    dve.wait_ge(landed[s], 16 * g + 16)
                    dve.tensor_tensor_reduce(raw[:, s, :], raw[:, s, :], c_row, 1.0, 0.0, ALU.mult, ALU.add, mod_sums[:, s:s + 1])\
                        .then_inc(ada_done, 1)
                dve.wait_ge(ada_done, 4 * g + 4)
                dve.tensor_tensor(mod[:, bass.ds(4 * g, 4)], mod_sums, cols[:, bass.ds(4 * g + COLS["ada_b"], 4)], ALU.add)\
                    .then_inc(mod_ready, 1)

            def late_modulation(i):
                n = i + ADA_UNITS
                dve.wait_ge(mod_ready, i + ADA_UNITS // 4)
                dve.wait_ge(sem("mod_landed"), 16 * i + 16)
                dve.tensor_tensor_reduce(late_slot, late_slot, late_c, 1.0, 0.0, ALU.mult, ALU.add, mod_sums[:, 0:1])\
                    .then_inc(ada_done, 1)
                dve.wait_ge(ada_done, n + 1)
                dve.tensor_tensor(mod[:, bass.ds(n, 1)], mod_sums[:, 0:1], cols[:, bass.ds(n + COLS["ada_b"], 1)], ALU.add)\
                    .then_inc(mod_ready, 1)

            dve.wait_ge(sem("bias_mm"), 1)
            dve.tensor_scalar(at(F_BOUT, 384, parts=32), ps[0:32, 4, 0:384], 1 / SCALE, None, ALU.mult)\
                .then_inc(sem("bias_rows_out"), 1)
            a, tt, r = (at(o, T, parts=64) for o in (F_A, F_T, F_R))
            dve.wait_ge(sem("ld_small"), 32)
            dve.wait_ge(sem("c_ready"), 1)
            for n in range(3):
                dve.wait_ge(sem("mlp_mm"), n + 1)
                ch(dve.tensor_scalar(a, ps[0:64, 5, 0:T], cols[0:64, COLS["fb"] + n:COLS["fb"] + n + 1],
                                     cols[0:64, COLS["ffreq"]:COLS["ffreq"] + 1], ALU.add, ALU.mult))
                ch(dve.tensor_scalar(tt, a, 1 / (2 * math.pi), MAGIC, ALU.mult, ALU.add))
                ch(dve.tensor_scalar(tt, tt, MAGIC, None, ALU.subtract))
                for part in TWO_PI:
                    ch(dve.scalar_tensor_tensor(a, tt, -part, a, ALU.mult, ALU.add))
                if n:
                    dve.wait_ge(sem("sin_out"), n)
                dve.tensor_scalar(r, a, PI_IN, -PI_IN, ALU.min, ALU.max).then_inc(sem("sin_arg"), 1)
                modulation(n)
            modulation(3)
            norm_unit("h1", D, x, True, x)
            dve.wait_ge(sem("brow_stored"), 16)
            with dve.Fori(0, 4) as b:
                ch.enter(b, 2)
                modulation(4 * b + 4)
                dve.wait_ge(sem("ld_block"), 48 * b + 48)
                for n in range(4):
                    dve.wait_ge(sem("taps_mm"), 4 * b + n + 1)
                    ins = dve.tensor_tensor(at(F_TAPS + 512 * n, 512), ps[:, n, :], at(F_DEC + 512 * (n // 2), 512), ALU.mult)
                    if n == 1:
                        ch(ins)
                        ins = dve.memset(arena[0:1, F_TAPS + 512:F_TAPS + 1024], 0.0)
                    ins.then_inc(sem("taps_ready"), 1)
                modulation(4 * b + 5)
                dve.wait_ge(sem("taps_ready"), 4 * b + 4)
                dve.wait_ge(sem("norm_mm"), b + 1)
                ch(dve.reciprocal(at(F_RN, 512), ps[:, 4, :]))
                for t in range(TH):
                    for op, o in ((ALU.add, 0), (ALU.subtract, 1024)):
                        dve.tensor_tensor(at(F_ABS + o + 512 * t, 512), at(F_TAPS + 1024 * t, 512),
                                          at(F_TAPS + 1024 * t + 512, 512), op).then_inc(sem("parity_ready"), 1)
                modulation(4 * b + 6)
                for n in range(5):
                    dve.wait_ge(sem("spectrum_mm"), 5 * b + n + 1)
                    dve.tensor_tensor(at(F_KO + 512 * n, 512), ps[:, (0, 1, 2, 3, 5)[n], :], at(F_RN, 512), ALU.mult)\
                        .then_inc(sem("spectrum_out" if n in (2, 3) else "spectrum_cos"), 1)
                dve.wait_ge(sem("spectrum_cos"), 3 * b + 3)
                for n in (0, 1, 4):
                    o = at(F_KO + 512 * n, 512)
                    dve.tensor_tensor(o, o, at(F_HB, 512), ALU.add).then_inc(sem("spectrum_out"), 1)
                modulation(4 * b + 7)
            ch.leave(4)
            dve.wait_ge(mod_ready, ADA_UNITS // 4)

            def gated_norm_gain(section, name):
                ch(dve.scalar_tensor_tensor(gain[:, :], mod[:, section * DC:(section + 1) * DC], 1.0, col(name, DC),
                                            ALU.add, ALU.mult))

            gated_norm_gain(1, "norm1")
            norm_split("h1", (h_hi, h_lo), DC, hf, 0, gain, mod[:, 0:DC])
            dve.wait_ge(sem("narrow_hi"), 1)
            dve.tensor_tensor(n_lo[:, :, :], at(12960, DC, 24), n_hi[:, :, :].bitcast(F32), ALU.subtract)\
                .then_inc(sem("narrow_lo"), 1)
            for k in range(3):
                lo(0, k)

            def scores(first, n, sink, out_of, beside=None):
                for t in range(n + 2):
                    a = first + t
                    if t < n:
                        b = t % 2
                        dve.wait_ge(sem("att_s"), a + 1)
                        if a >= 2:
                            dve.wait_ge(sem("att_p"), 2 * (a - 1))
                        m = stat[:, 8 + 2 * b:10 + 2 * b]
                        dve.tensor_reduce(m[:, 0:1], ps[:, b, 0:128], AX, ALU.max, negate=True)
                        ch(dve.tensor_reduce(m[:, 1:2], ps[:, b, 128:384], AX, ALU.max, negate=True))
                        if sink:
                            ins = dve.tensor_scalar(m, m, SCALE, stat[:, 40 + t:41 + t], ALU.mult, ALU.min)
                        else:
                            ins = dve.tensor_scalar(m, m, SCALE, None, ALU.mult)
                        ins.then_inc(sem("att_max"), 1)
                    if t >= 2:
                        a, b = a - 2, t % 2
                        dve.wait_ge(sem("att_pv"), a + 1)
                        four = (t - 2) % 4
                        den = rden = stat[:, 120 + 2 * four:122 + 2 * four]
                        if sink:
                            dve.wait_ge(sem("sink_exp"), t - 1)
                            ch(dve.tensor_tensor(den, den, stat[:, 128 + 2 * four:130 + 2 * four], ALU.add))
                        ch(dve.reciprocal(rden, den))
                        out_of(a, t - 2, b, rden)
                    if beside and t < 8:
                        lo(group_base(beside), t + 3)

            def head_out(a, h, b, rden):
                for half in range(TH):
                    dve.tensor_scalar(mix[:, half, h * HD:(h + 1) * HD], ps[:, 4 + b, half * HD:(half + 1) * HD],
                                      rden[:, half:half + 1], None, ALU.mult).then_inc(sem("att_out"), 1)

            phase("a_q")
            phase("a_k")
            phase("a_v")
            scores(0, 8, False, head_out, "c_q")

            def mixer_unit(name, count):
                dve.wait_ge(sem("att_out"), count)
                norm_unit(name, 512, mix, True, mix)

            def mixer_split(m, name):
                norm_split(name, (r_hi, r_lo), 4, mixf, 4 * m, col("mixg", 16)[:, 4 * m:4 * m + 4], None)
            mixer_unit("mixA", 16)
            phase("c_k")
            mixer_split(0, "mixA")
            phase("c_v")
            scores(8, 8, False, head_out, "b_q")
            mixer_unit("mixC", 32)
            phase("small", per_iter=2)
            mixer_split(2, "mixC")
            dve.wait_ge(sem("ld_cmp"), 64)
            dve.wait_ge(sem("small_out"), 10)
            for n in range(2):
                for par in range(2):
                    for part in range(2):
                        src = smk[0:64, 1 + n, :, 16 * part:16 * part + 240].rearrange("p g (n b) -> p b g n", b=16)
                        dst = blocks[64 * par:64 * par + 64, n, 240 * part:240 * part + 240]\
                            .rearrange("p (r g n) -> p r g n", r=8, g=2)
                        pe_v = peT[:, n, 16 * part:16 * part + 16].rearrange("p (r q) -> p q r", q=2)[:, par, :]
                        dve.tensor_tensor(dst, src[:, par:16:2, :, :],
                                          pe_v.unsqueeze(2).unsqueeze(3).broadcast_to([64, 8, 2, N_CMP]), ALU.add)\
                            .then_inc(sem("blocks_ready"), 1)
            dve.wait_ge(sem("ld_sink"), 16)
            ch(dve.tensor_scalar(stat[:, 40:48], stat[:, 32:40], -1.0, None, ALU.mult))
            scores(16, 8, True, head_out, "d_q")
            mixer_unit("mixB", 48)
            dve.wait_ge(sem("cmp_s"), 1)
            v15 = lambda v: v[:, :, :, 0:N_CMP]
            add, keep = (tab[:, o:o + 32].rearrange("p (a b) -> p a b", a=2)[:, :, 0:N_CMP].unsqueeze(1)
                         .broadcast_to([P, 8, 2, N_CMP]) for o in (TAB_CADD, TAB_C01))
            ch(dve.tensor_scalar(v15(cs), v15(ps[:, 7, 0:256].rearrange("p (a b c) -> p a b c", a=8, b=2)), SCALE, None, ALU.mult))
            ch(dve.tensor_tensor(v15(cs), v15(cs), add, ALU.add))
            cm, cden = stat[:, 48:64], stat[:, 64:80]
            ch(dve.tensor_reduce(cm.rearrange("p (a b) -> p a b", a=8), v15(cs), AX, ALU.max, negate=True))
            bc = cm.rearrange("p (a b) -> p a b", a=8).unsqueeze(3).broadcast_to([P, 8, 2, N_CMP])
            dve.tensor_tensor(v15(cs), v15(cs), bc, ALU.add).then_inc(sem("cmp_max"), 1)
            mixer_split(1, "mixB")
            dve.wait_ge(sem("cmp_exp"), 1)
            dve.tensor_tensor(v15(cp), v15(cp), keep, ALU.mult).then_inc(sem("cmp_p"), 1)
            dve.wait_ge(sem("cmp_p"), 1)
            ch(dve.tensor_reduce(cden.rearrange("p (a b) -> p a b", a=8), v15(cp), AX, ALU.add))
            ch(dve.tensor_scalar(cden, cden, TINY, None, ALU.max))
            ch(dve.reciprocal(cden, cden))
            dve.wait_ge(sem("gates_ready"), 1)
            gate = gates[:, :, :].rearrange("p t (h g) -> p g h t", g=3)
            ch(dve.tensor_tensor(cden.rearrange("p (a b) -> p a b", a=8), cden.rearrange("p (a b) -> p a b", a=8),
                                 gate[:, 0], ALU.mult))
            for q in range(2):
                dve.wait_ge(sem("cmp_pv"), 2 * q + 2)
                w = cden.rearrange("p (a b) -> p a b", a=8)[:, 4 * q:4 * q + 4, :].unsqueeze(3).broadcast_to([P, 4, 2, HD])
                dve.tensor_tensor(mix[:, :, 256 * q:256 * q + 256].rearrange("p t (h n) -> p h t n", h=4),
                                  ps[:, 4 + q, :].rearrange("p (h t n) -> p h t n", h=4, t=2), w, ALU.mult)\
                    .then_inc(sem("att_out"), 1)

            def nsa_out(a, n, b, rden):
                h, branch = n % 8, 1 + n // 8
                for half in range(TH):
                    ch(dve.tensor_tensor(rden[:, half:half + 1], rden[:, half:half + 1],
                                         gates[:, half, 3 * h + branch:3 * h + branch + 1], ALU.mult))
                dve.wait_ge(sem("att_out"), 50 if branch == 1 else 50 + 2 * h + 2)
                for half in range(TH):
                    o = mix[:, half, h * HD:(h + 1) * HD]
                    dve.scalar_tensor_tensor(o, ps[:, 4 + b, half * HD:(half + 1) * HD], rden[:, half:half + 1], o,
                                             ALU.mult, ALU.add).then_inc(sem("att_out"), 1)
            scores(24, 16, False, nsa_out)
            mixer_unit("mixD", 82)
            mixer_split(3, "mixD")

            def gate_row(section, n):
                for c in range(DC):
                    if c >= 8:
                        dve.wait_ge(sem("row_mm"), DC * n + c - 7)
                    dve.tensor_scalar(diag[:, c % 8, :], ident, mod[:, section * DC + c:section * DC + c + 1], None, ALU.mult)\
                        .then_inc(sem("diag_ready"), 1)
                for q in range(4):
                    dve.wait_ge(sem("row_mm"), DC * n + 4 * q + 4)
                    dve.tensor_copy(row[:, q * 512:(q + 1) * 512], ps[:, 4 + q, :]).then_inc(sem("row_ready"), 1)
                dve.wait_ge(sem("row_ready"), 4 * n + 4)

            gate_row(2, 0)
            dve.wait_ge(sem("ld_x"), 48)

            def add_cols(first, per_cb, gated=False):
                def step(g, i, k):
                    u, r = divmod(k, 2)
                    if not r or u % per_cb != per_cb - 1:
                        return
                    cb = u // per_cb
                    per = 2 if per_cb == 4 else 4
                    done(g, k)
                    for h in range(TH):
                        o = x[:, h, bass.ds(512 * per * i + 512 * cb, 512)] if not isinstance(i, int) else \
                            x[:, h, 512 * (per * i + cb):512 * (per * i + cb) + 512]
                        acc_ps = ps[:, 4 + 2 * (cb % 2) + h, :]
                        if gated:
                            rw = row[:, bass.ds(512 * per * i + 512 * cb, 512)]
                            tmp = at(11000 + 512 * h, 512)
                            ch(dve.tensor_tensor(tmp, acc_ps, rw, ALU.mult))
                            ins = dve.tensor_tensor(o, o, tmp, ALU.add)
                        else:
                            ins = dve.tensor_tensor(o, o, acc_ps, ALU.add)
                        if h:
                            ins.then_inc(sem("cols_added"), 1)
                return step
            phase("mix_out", add_cols(0, 4, True), per_iter=2, links=4)

            gated_norm_gain(4, "norm2")
            norm("hm", gain=gain, bias=mod[:, 3 * DC:4 * DC])
            dve.wait_ge(sem("router_hi"), 1)
            dve.tensor_tensor(n_lo[:, :, 0:16], at(ro, DC, 16), n_hi[:, :, 0:16].bitcast(F32), ALU.subtract)\
                .then_inc(sem("router_lo"), 1)
            dve.memset(acc, 0.0).then_inc(sem("acc_zero"), 1)
            aff, score, beat, tie = at(ro + 272, 32), at(ro + 304, 32), at(ro + 336, 128), at(ro + 464, 128)
            rank, sel = at(ro + 592, 32), at(ro + 624, 32)
            gsc, gbeat, gtie, grank, wsum = at(ro + 656, 8), at(ro + 664, 32), at(ro + 696, 32), at(ro + 728, 8), at(ro + 736, 2)
            dve.wait_ge(sem("affinity"), 1)
            ch(dve.tensor_tensor(score.rearrange("p (h e) -> p h e", h=2), aff.rearrange("p (h e) -> p h e", h=2),
                                 at(ro + 256, 16).unsqueeze(1).broadcast_to([P, 2, 16]), ALU.add))
            tri = tab[:, TAB_TRI:TAB_TRI + 16].rearrange("p (a b) -> p a b", a=4)

            def ranks(s, wins, ties, out_rank, n):
                s3 = s.rearrange("p (g e) -> p g e", e=4)
                w4, t4 = (v.rearrange("p (g e j) -> p g e j", e=4, j=4) for v in (wins, ties))
                sj, se = s3.unsqueeze(2).broadcast_to([P, n, 4, 4]), s3.unsqueeze(3).broadcast_to([P, n, 4, 4])
                ch(dve.tensor_tensor(w4, sj, se, ALU.is_gt))
                ch(dve.tensor_tensor(t4, sj, se, ALU.is_equal))
                ch(dve.tensor_tensor(t4, t4, tri.unsqueeze(1).broadcast_to([P, n, 4, 4]), ALU.mult))
                ch(dve.tensor_tensor(wins, wins, ties, ALU.add))
                ch(dve.tensor_reduce(out_rank.rearrange("p (g e) -> p g e", e=4), w4, AX, ALU.add))

            ranks(score, beat, tie, rank, 8)
            ch(dve.tensor_scalar(sel, rank, 1.5, None, ALU.is_lt))
            ch(dve.tensor_tensor(rank, score, sel, ALU.mult))
            ch(dve.tensor_reduce(gsc, rank.rearrange("p (g e) -> p g e", e=4), AX, ALU.add))
            ranks(gsc, gbeat, gtie, grank, 2)
            ch(dve.tensor_scalar(grank, grank, 0.5, None, ALU.is_lt))
            ch(dve.tensor_tensor(sel.rearrange("p (g e) -> p g e", e=4), sel.rearrange("p (g e) -> p g e", e=4),
                                 grank.unsqueeze(2).broadcast_to([P, 8, 4]), ALU.mult))
            ch(dve.tensor_tensor(sel, sel, aff, ALU.mult))
            ch(dve.tensor_reduce(wsum, sel.rearrange("p (h e) -> p h e", h=2), AX, ALU.add))
            ch(dve.reciprocal(wsum, wsum))
            ch(dve.tensor_tensor(comb[:, :, :], sel.rearrange("p (h e) -> p h e", h=2),
                                 wsum.unsqueeze(2).broadcast_to([P, 2, 16]), ALU.mult))
            dve.wait_ge(sem("acc_zero"), 1)
            dve.wait_ge(sem("c_ready"), 2)

            def hidden_lo(i, k):
                if k in (4, 8, 12, 16):
                    f = k // 4 - 1
                    dve.wait_ge(sem("moe_hi"), 4 * i + (f + 1))
                    dve.tensor_tensor(r_lo[:, f, :], hid[:, f % 2, :], r_hi[:, f, :].bitcast(F32), ALU.subtract)\
                        .then_inc(sem("moe_lo"), 1)

            def expert_step(g, i, k):
                u = k // 2
                if k == 10:
                    late_modulation(i)
                if u < 8 and k % 4 == 3:
                    f = k // 4
                    done(g, k)
                    dve.wait_ge(sem("moe_silu"), 4 * i + (f + 1))
                    dve.tensor_tensor(hid[:, f % 2, :], g_act[:, f % 2, :], ps[:, u % 4, 0:T], ALU.mult)\
                        .then_inc(sem("moe_pair"), 1)
                if u >= 8 and k % 2:
                    cb = u - 8
                    done(g, k)
                    for h in range(TH):
                        o = acc[:, h, cb * 512:(cb + 1) * 512]
                        ins = dve.scalar_tensor_tensor(o, ps[:, 4 + 2 * (cb % 2) + h, :], comb[:, h, bass.ds(i, 1)], o,
                                                       ALU.mult, ALU.add)
                        if h == 0:
                            ch(ins)
                        else:
                            ins.then_inc(sem("down_out"), 1)
                            dve.wait_ge(sem("down_out"), 4 * i + (cb + 3))
            phase("moe", expert_step, per_iter=3, links=4, early=hidden_lo)
            dve.wait_ge(mod_ready, ADA_UNITS // 4 + LATE_UNITS)
            gate_row(5, 1)
            for h in range(TH):
                ch(dve.tensor_tensor(acc[:, h, :], acc[:, h, :], row, ALU.mult))
                dve.tensor_tensor(x[:, h, :], x[:, h, :], acc[:, h, :], ALU.add).then_inc(sem("x_moe"), 1)

            def scaled(name, row_sem, value, done_sem):
                norm(name, spread=False)
                dve.wait_ge(sem(row_sem), value)
                for h in range(TH):
                    dve.scalar_tensor_tensor(x[:, h, :], x[:, h, :], stat[:, 6 + h:7 + h], row, ALU.mult, ALU.mult)\
                        .then_inc(sem(done_sem), 1)
            scaled("x1", "ld_rowg", 16, "x1_done")
            dve.wait_ge(sem("x1_done"), 2)
            norm("h2", gain=col("normmix2", DC))

            def conv_step(g, i, k):
                if k % 2 == 0:
                    return
                s = k // 2
                done(g, k)
                tile = cvT[:, bass.ds(4 * i + s, 1), :].rearrange("p a n -> p (a n)")
                w = [cols[:, bass.ds(4 * i + (s + COLS["conv_w"] + 24 * j), 1)] for j in range(3)]
                b = cols[:, bass.ds(4 * i + (s + COLS["conv_b"]), 1)]
                ch(dve.tensor_scalar(tile, ps[:, s, 0:T], w[1], b, ALU.mult, ALU.add))
                ch(dve.scalar_tensor_tensor(tile[:, 1:T], ps[:, s, 0:T - 1], w[0], tile[:, 1:T], ALU.mult, ALU.add))
                dve.scalar_tensor_tensor(tile[:, 0:T - 1], ps[:, s, 1:T], w[2], tile[:, 0:T - 1], ALU.mult, ALU.add)\
                    .then_inc(sem("conv_out"), 1)
            phase("hyena", conv_step, links=8)
            for n in range(0, 12, 2):
                dve.wait_ge(sem("seq_t"), n + 1)
                dve.tensor_copy(seq_pair(n), bank_pair(n)).then_inc(sem("seq_even"), 1)
            for b in range(4):
                o, q = divmod(b, 2)
                cut = slice(q * 512, (q + 1) * 512)
                dve.wait_ge(sem("ld_kf"), 16 * (b + 1))
                if b:
                    dve.wait_ge(sem("inv_mm"), 2 * b)
                for ft in range(2):
                    re, im = ps[:, ft, :], ps[:, 2 + ft, :]
                    ka, kb, kc_ = kf[:, ft, :], kf[:, 2 + ft, :], kf[:, 4 if ft == 0 else 1, :]
                    dve.wait_ge(sem("spec_mm"), 4 * b + 2 + 2 * ft)
                    for (u, v, op, dst, part) in ((ka, kb, ALU.subtract, yr[:, ft, :], prods[:, 0, :]),
                                                  (kb, kc_, ALU.add, yr[:, 2 + ft, :], prods[:, 1, :])):
                        dve.tensor_tensor(dst, re, u, ALU.mult)
                        ch(dve.tensor_tensor(part, im, v, ALU.mult))
                        dve.tensor_tensor(dst, dst, part, op).then_inc(sem("spec_ready"), 1)
                for lt in range(TH):
                    dve.wait_ge(sem("inv_mm"), 2 * b + lt + 1)
                    dve.tensor_tensor(seq[:, 0, lt, cut], ps[:, 4 + lt, :], seq[:, 1 + o, lt, cut], ALU.mult)\
                        .then_inc(sem("conv_step"), 1)
            for c in range(8):
                dve.wait_ge(sem("yhy_hi"), c + 1)
                dve.tensor_tensor(r_lo[:, c, :], ps[:, c % 4, 0:T], r_hi[:, c, :].bitcast(F32), ALU.subtract)\
                    .then_inc(sem("yhy_split"), 1)

            phase("sgu_u")
            phase("sgu_v", per_iter=2)
            dve.wait_ge(sem("v_gelu"), 4)
            for h in range(TH):
                for q in range(2):
                    ch(dve.bn_stats(stat[:, 96 + 12 * h + 6 * q:102 + 12 * h + 6 * q], vg[:, h, q * 512:(q + 1) * 512]))
                ch(dve.bn_aggr(stat[:, 88 + 2 * h:90 + 2 * h], stat[:, 96 + 12 * h:108 + 12 * h]))
            dve.tensor_scalar(stat[:, 2:4], stat[:, 89:92:2], EPS, None, ALU.add).then_inc(sem("ln_var"), 1)
            dve.wait_ge(sem("ln_rt"), 1)
            ch(dve.reciprocal(stat[:, 6:8], stat[:, 4:6]))
            dve.wait_ge(sem("ld_sgu"), 64)
            for h in range(TH):
                ch(dve.tensor_scalar(vg[:, h, :], vg[:, h, :], stat[:, 88 + 2 * h:89 + 2 * h], stat[:, 6 + h:7 + h],
                                     ALU.subtract, ALU.mult))
                ch(dve.tensor_tensor(vg[:, h, :], vg[:, h, :], ln_row[:, 0, :], ALU.mult))
                dve.tensor_tensor(vg[:, h, :], vg[:, h, :], ln_row[:, 1, :], ALU.add).then_inc(sem("v_normed"), 1)
            dve.wait_ge(sem("u_out"), 4 + 8)
            for h in range(8):
                dve.wait_ge(sem("spatial_mm"), h + 1)
                dve.tensor_tensor(yf[:, h % 2, :], uT[:, h, :], ps[:, h % 4, 0:T], ALU.mult).then_inc(sem("ysgu_f"), 1)
                dve.wait_ge(sem("ysgu_hi"), h + 1)
                dve.tensor_tensor(r_lo[:, 8 + h, :], yf[:, h % 2, :], r_hi[:, 8 + h, :].bitcast(F32), ALU.subtract)\
                    .then_inc(sem("ysgu_lo"), 1)

            phase("gate_hy")
            dve.wait_ge(sem("sg1_out"), 4 + 16)

            def branch_step(g, i, k):
                done(g, k)
                t = sg1[:, bass.ds(8 * i + k, 1), :]
                dve.tensor_tensor(t, t, ps[:, k % 4:k % 4 + 1, 0:T], ALU.mult).then_inc(sem("bhy_out"), 1)
            phase("branch_hy", branch_step)
            phase("gate_sgu")
            dve.wait_ge(sem("sg2_out"), 4 + 16)
            dve.wait_ge(sem("bhy_out"), 4 + 16)

            def merge_step(g, i, k):
                done(g, k)
                m = mf[:, k % 2:k % 2 + 1, :]
                ch(dve.tensor_tensor(m, sg2[:, bass.ds(8 * i + k, 1), :], ps[:, k % 4:k % 4 + 1, 0:T], ALU.mult))
                dve.tensor_tensor(m, m, sg1[:, bass.ds(8 * i + k, 1), :], ALU.add).then_inc(sem("merged_f"), 1)
                dve.wait_ge(sem("merged_hi"), 8 * i + (k + 1))
                dve.tensor_tensor(h_lo[:, bass.ds(8 * i + k, 1), :], m, h_hi[:, bass.ds(8 * i + k, 1), :].bitcast(F32),
                                  ALU.subtract).then_inc(sem("merged_lo"), 1)
            phase("branch_sgu", merge_step, links=8)
            phase("out2", add_cols(4, 4), per_iter=2)
            norm("hf", gain=col("normffn2", DC))

            for part in range(3):
                def ffn_step(g, i, k, part=part):
                    n0 = sum(FFN_TILES[:part])
                    if k % 4 == 3:
                        f = k // 4
                        done(g, k)
                        dve.wait_ge(sem("ffn_silu"), 2 * i + (n0 + f + 1))
                        dve.tensor_tensor(hid[:, f, :], g_act[:, f, :], ps[:, k // 2, 0:T], ALU.mult).then_inc(sem("ffn_pair"), 1)
                        dve.wait_ge(sem("ffn_hi"), 2 * i + (n0 + f + 1))
                        dve.tensor_tensor(r_lo[:, bass.ds(2 * i + f, 1), :], hid[:, f:f + 1, :],
                                          r_hi[:, bass.ds(2 * i + f, 1), :].bitcast(F32), ALU.subtract).then_inc(sem("ffn_lo"), 1)
                phase(f"ffn_in{part}", ffn_step)
                per_cb = FFN_TILES[part] // 4
                phase(f"ffn_down{part}", add_cols(8 + 4 * part, per_cb), per_iter=2 if per_cb == 4 else 3)
            scaled("y", "ld_rowf", 16, "y_ready")

        @block.tensor
        def _(pe):
            def mm(o, a, b, start=True, stop=True):
                return pe.matmul(o, a, b, start=start, stop=stop)

            def three(o, a, b, start, stop):
                mm(o, a[0], b[0], start, False)
                mm(o, a[0], b[1], False, False)
                return mm(o, a[1], b[0], False, stop)

            def w(k, lo_col, n):
                return w_hi[:, k % 4, lo_col:lo_col + n], w_lo[:, k % 4, lo_col:lo_col + n]

            H = lambda c, a=0, b=T: (h_hi[:, c, a:b], h_lo[:, c, a:b])
            R = lambda c, a=0, b=T: (r_hi[:, c, a:b], r_lo[:, c, a:b])

            def phase(name, step, per_iter=1):
                def body(g, i, final):
                    for k in range(8 * per_iter):
                        pe.wait_ge(lo_ready, 8 * g + (k + 1))
                        step(g, i, k).then_inc(half_done, 1)
                run_groups(pe, name, body, per_iter)

            def feature_major(k, o, src=H):
                for j in range(8):
                    c = (k % 2) * 8 + j
                    ins = three(o, w(k, j * P, P), src(c), c == 0, c == DC - 1)
                return ins

            def token_major(k, kq, n_kq, bank, src):
                for j in range(2):
                    c = 4 * kq + (k % 2) * 2 + j
                    for h in range(TH):
                        ins = three(ps[:, bank + h, :], src(c, h * P, (h + 1) * P), w(k, j * 512, 512), c == 0, c == 4 * n_kq - 1)
                return ins

            def fm_phase(name, free=None, per=4):
                def step(g, i, k):
                    if k % 2 == 0 and free:
                        free(i, k // 2)
                    return feature_major(k, ps[:, k // 2, 0:T])
                phase(name, step)

            pe.wait_ge(sem("ld_bias"), 48)
            mm(ps[0:32, 4, 0:384], at(F_RELB, 32, parts=36), at(F_ONEH, 384, parts=36)).then_inc(sem("bias_mm"), 1)
            pe.wait_ge(sem("ld_filt"), 80)
            for n, (wo, kk, src) in enumerate(((F_W1, 33, F_ZT), (F_W2, 64, F_H), (F_W3, 64, F_H))):
                if n:
                    pe.wait_ge(sem("sin_out"), n)
                mm(ps[0:64, 5, 0:T], at(wo, 64, parts=kk), at(src, T, parts=kk)).then_inc(sem("mlp_mm"), 1)
            pe.wait_ge(sem("sin_out"), 3)
            pe.wait_ge(sem("ones_set"), 1)
            cosm, sinm = at(F_DFT, 2, T), at(F_DFT + 512, 2, T)
            nyq = at(F_DFT + 1024, 2, P)
            with pe.Fori(0, 4) as b:
                pe.wait_ge(sem("ld_block"), 48 * b + 48)
                for n in range(4):
                    mm(ps[:, n, :], arena[0:64, F_H + (n // 2) * P:F_H + (n // 2 + 1) * P],
                       arena[0:64, F_W4 + (n % 2) * 512:F_W4 + (n % 2 + 1) * 512]).then_inc(sem("taps_mm"), 1)
                for n in range(4):
                    pe.wait_ge(sem("abs_ready"), 4 * b + n + 1)
                    ins = mm(ps[:, 4, :], ones[:, :], at(F_ABS + 512 * n, 512), n == 0, n == 3)
                ins.then_inc(sem("norm_mm"), 1)
                pe.wait_ge(sem("parity_ready"), 4 * b + 4)
                for n, (m, c0, o) in enumerate(((cosm, 0, 0), (cosm, P, 0), (sinm, 0, 1024), (sinm, P, 1024), (nyq, 0, 0))):
                    for t in range(TH):
                        ins = mm(ps[:, (0, 1, 2, 3, 5)[n], :], m[:, t, c0:c0 + P], at(F_ABS + o + 512 * t, 512), t == 0, t == 1)
                    ins.then_inc(sem("spectrum_mm"), 1)
            def turn(name, tiles=DC, xh=xhat):
                pe.wait_ge(sem("norm_xh"), norm_count(name, "xh", 1 if tiles == DC else 2))
                if tiles == DC:
                    pe.wait_ge(sem("norm_xa"), norm_count(name, "xa", 1))
                for p in range(tiles // 2):
                    if p >= 4:
                        pe.wait_ge(sem("norm_f"), norm_count(name, "f", (p - 4) // 2 + 1))
                    for c in range(2):
                        for h in range(TH):
                            ins = pe.transpose(ps[:, p % 4, c * T + h * P:c * T + (h + 1) * P],
                                               xh[:, h, (2 * p + c) * P:(2 * p + c + 1) * P], ident)
                    ins.then_inc(sem("norm_t"), 1)

            pe.wait_ge(sem("spectrum_out"), 20)
            turn("h1", xh=x)
            pe.wait_ge(sem("norm_lo"), norm_count("h1", "lo", 4))
            fm_phase("a_q")
            fm_phase("a_k", lambda i, s: pe.wait_ge(sem("q_out"), 2 * s + 2))
            phase("a_v", lambda g, i, k: token_major(k, k // 2, 4, 4, H))

            def attend(first, n, keys, values, qT, toep, beside=None):
                for t in range(n + 2):
                    if t < n:
                        a, b = first + t, t % 2
                        if a >= 2:
                            pe.wait_ge(sem("att_p"), 2 * (a - 1))
                        q, kt, bias = qT[:, t % 8, :], keys(t), toep[:, t % 8, :]
                        mm(ps[:, b, 0:128], q[:, 0:P], kt[:, 0:P], True, False)
                        mm(ps[:, b, 0:128], flip, bias[:, P:T], False, True)
                        mm(ps[:, b, 128:384], q[:, P:T], kt, True, False)
                        mm(ps[:, b, 128:384], flip, bias, False, True).then_inc(sem("att_s"), 1)
                    if 1 <= t <= n:
                        a, b = first + t - 1, (t - 1) % 2
                        pe.wait_ge(sem("att_p"), 2 * a + 2)
                        if a >= 2:
                            pe.wait_ge(sem("att_pt"), a - 1)
                        for j in range(3):
                            ins = pe.transpose(ps[:, 2 + b, j * P:(j + 1) * P], prob[:, b, j * P:(j + 1) * P], ident)
                        ins.then_inc(sem("att_t"), 1)
                    if t >= 2:
                        a, b = first + t - 2, t % 2
                        pe.wait_ge(sem("att_pt"), a + 1)
                        if t >= 4:
                            pe.wait_ge(sem("att_out"), out_count(a - 2))
                        v0, v1 = values(t - 2)
                        mm(ps[:, 4 + b, 0:HD], pT[:, b, 0:P], v0)
                        mm(ps[:, 4 + b, HD:2 * HD], pT[:, b, P:2 * P], v0, True, False)
                        mm(ps[:, 4 + b, HD:2 * HD], pT[:, b, 2 * P:3 * P], v1, False, True).then_inc(sem("att_pv"), 1)
                    if beside and t < 8:
                        if t in (4, 6):
                            pe.wait_ge(sem("q_out"), first + 8 + t - 2)
                        pe.wait_ge(lo_ready, 8 * group_base(beside) + t + 1)
                        feature_major(t, ps[:, 6 + t // 2 % 2, 0:T]).then_inc(half_done, 1)

            def out_count(a):
                return 2 * a + 2 if a < 24 else 2 * a + 4

            own = (lambda t: kT[:, t, :], lambda t: (v_a[:, 0, t * HD:(t + 1) * HD], v_a[:, 1, t * HD:(t + 1) * HD]))

            def shared(kk, vv):
                return (lambda t: smk[0:64, kk, (t % 8) // 4, :],
                        lambda t: tuple(smv[:, vv, h, ((t % 8) // 4) * HD:((t % 8) // 4 + 1) * HD] for h in range(2)))

            pe.wait_ge(sem("k_out"), 8)
            pe.wait_ge(sem("v_out"), 2)
            pe.wait_ge(sem("ld_toep"), 16)
            attend(0, 8, *own, qT, toep, "c_q")
            fm_phase("c_k")
            pe.wait_ge(sem("k_out"), 12 + 2)
            turn("mixA", 4, mix)
            phase("c_v", lambda g, i, k: token_major(k, k // 2, 4, 4, H))
            pe.wait_ge(sem("norm_f"), norm_count("mixA", "f", 1))
            pe.wait_ge(sem("k_out"), 16)
            pe.wait_ge(sem("q_out"), 16)
            pe.wait_ge(sem("v_out"), 4)
            pe.wait_ge(sem("ld_toep2"), 16)
            attend(8, 8, *own, qT2, toep2, "b_q")

            def small_step(g, i, k):
                u = k // 2
                if k in (8, 10, 12, 14):
                    pe.wait_ge(sem("small_out"), k - 6)
                return feature_major(k, ps[:, u % 4, 0:T])
            phase("small", small_step, per_iter=2)

            def narrow(n, ready):
                for r in ready:
                    pe.wait_ge(sem(r), 1)
                for c in range(DC):
                    ins = three(ps[0:n, 6, 0:T], (n_hi[:, c, 0:n], n_lo[:, c, 0:n]), H(c), c == 0, c == DC - 1)
                ins.then_inc(sem("narrow_mm"), 1)

            def narrow_turn(n, src, count):
                pe.wait_ge(sem("narrow_out"), count)
                for h in range(TH):
                    ins = pe.transpose(ps[:, 7, h * n:(h + 1) * n], src[:, h * P:(h + 1) * P], tab[0:n, TAB_ID:TAB_ID + n])
                ins.then_inc(sem("narrow_t"), 1)
            pe.wait_ge(sem("q_out"), 24)
            narrow(24, ("narrow_hi", "narrow_lo"))
            pe.wait_ge(sem("small_out"), 13)
            pe.wait_ge(sem("att_out"), 32)
            for h in range(TH):
                for v in range(3):
                    ins = pe.transpose(ps[:, 4 + h, v * P:(v + 1) * P], v_f[:, v, h * P:(h + 1) * P], ident)
            ins.then_inc(sem("v_turned"), 1)
            turn("mixC", 4, mix)
            narrow_turn(24, narrow_f, 1)
            pe.wait_ge(sem("norm_f"), norm_count("mixC", "f", 1))
            pe.wait_ge(sem("ld_cmp"), 64)
            for n, w1 in enumerate((w1k, w1v)):
                pe.wait_ge(sem("blocks_ready"), 4 * n + 4)
                for r in range(16):
                    ins = mm(ps[:, n, 0:30], w1[:, r, :], blocks[:, n, 30 * r:30 * r + 30], r == 0, r == 15)
                ins.then_inc(sem("cmp_hidden"), 1)
            pe.wait_ge(sem("hid_act"), 2)
            mm(ps[0:64, 2, 0:30], w2c[:, 0, :], hidc[:, 0, :])
            for g in range(2):
                ins = mm(ps[0:N_CMP, 3, g * HD:(g + 1) * HD], hidc[:, 1, g * N_CMP:(g + 1) * N_CMP], w2c[:, 1, :])
            ins.then_inc(sem("cmp_kv"), 1)
            pe.wait_ge(sem("kc_ready"), 2)
            pe.wait_ge(sem("ld_toep2"), 32)
            pe.wait_ge(sem("gates_ready"), 1)
            pe.wait_ge(sem("v_small"), 2)
            attend(16, 8, *shared(0, 0), qT, toep2, "d_q")
            pe.wait_ge(sem("q_out"), 32)
            for h in range(8):
                for half in range(TH):
                    o = (2 * h + half) * 16
                    ins = mm(ps[:, 7, o:o + N_CMP], qT2[:, h, half * P:(half + 1) * P], kc[:, h // 4, :])
            ins.then_inc(sem("cmp_s"), 1)
            turn("mixB", 4, mix)
            pe.wait_ge(sem("cmp_p"), 1)
            for r in range(4):
                for j in range(4):
                    h, half = 2 * r + j // 2, j % 2
                    ins = pe.transpose(ps[0:N_CMP, 6, j * P:(j + 1) * P], cp[:, h, half, 0:N_CMP], ident)
                ins.then_inc(sem("cmp_t"), 1)
                pe.wait_ge(sem("cmp_pt"), r + 1)
                for j in range(4):
                    n, h = 4 * r + j, 2 * r + j // 2
                    ins = mm(ps[:, 4 + n // 8, (n % 8) * HD:(n % 8 + 1) * HD], cpT[0:N_CMP, j * P:(j + 1) * P], vc[:, h // 4, :])
                ins.then_inc(sem("cmp_pv"), 1)
            pe.wait_ge(sem("att_out"), 50)
            slc, win = shared(3, 1), shared(4, 2)
            pe.wait_ge(sem("ld_toep"), 32)
            pe.wait_ge(sem("norm_f"), norm_count("mixB", "f", 1))
            attend(24, 16, lambda t: (slc if t < 8 else win)[0](t), lambda t: (slc if t < 8 else win)[1](t), qT2, toep)
            turn("mixD", 4, mix)
            pe.wait_ge(sem("norm_lo"), norm_count("mixD", "lo", 1))

            def spread_row(n):
                for c in range(DC):
                    pe.wait_ge(sem("diag_ready"), DC * n + c + 1)
                    mm(ps[:, 4 + c // 4, (c % 4) * P:(c % 4 + 1) * P], ones[:, :], diag[:, c % 8, :]).then_inc(sem("row_mm"), 1)
                pe.wait_ge(sem("row_ready"), 4 * n + 4)
            spread_row(0)

            def column_blocks(name, first, per_cb, src, hidden=None):
                def step(g, i, k):
                    u = k // 2
                    cb, kq = divmod(u, per_cb)
                    if k % 2 == 0 and kq == 0:
                        pe.wait_ge(sem("cols_added"), 2 * i + (first + cb + 1))
                    if hidden is not None and cb == 0:
                        pe.wait_ge(sem("ffn_lo"), hidden + 2 * k + 2)
                    return token_major(k, kq, per_cb, 4 + 2 * (cb % 2), src)
                phase(name, step, per_iter=2 if per_cb == 4 else 3)
            column_blocks("mix_out", 0, 4, R)

            turn("hm")
            pe.wait_ge(sem("norm_lo"), norm_count("hm", "lo", 4))
            narrow(16, ("router_hi", "router_lo"))
            narrow_turn(16, narrow_r, 2)
            pe.wait_ge(sem("affinity"), 1)

            def expert_step(g, i, k):
                u = k // 2
                if u < 8:
                    if k % 4 == 0:
                        pe.wait_ge(sem("moe_pair"), 4 * i + (k // 4 + 1))
                    return feature_major(k, ps[:, u % 4, 0:T])
                cb = u - 8
                if k in (16, 17):
                    pe.wait_ge(sem("moe_lo"), 4 * i + (2 if k == 16 else 4))
                if k % 2 == 0:
                    pe.wait_ge(sem("down_out"), 4 * i + (cb + 1))
                return token_major(k, 0, 1, 4 + 2 * (cb % 2), R)
            phase("moe", expert_step, per_iter=3)
            pe.wait_ge(sem("down_out"), 2 + 4 * N_EXP)
            spread_row(1)

            turn("h2")
            pe.wait_ge(sem("norm_lo"), norm_count("h2", "lo", 4))
            fm_phase("hyena", lambda i, s: pe.wait_ge(sem("conv_out"), 4 * i + (s + 1)))
            pe.wait_ge(sem("conv_out"), 4 + 24)
            for n in range(12):
                if n >= 4:
                    pe.wait_ge(sem("seq_odd" if n % 2 else "seq_even"), (n - 4) // 2 + 1)
                for c in range(2):
                    for h in range(TH):
                        ins = pe.transpose(ps[:, n % 4, c * T + h * P:c * T + (h + 1) * P],
                                           cvT[:, 2 * n + c, h * P:(h + 1) * P], ident)
                ins.then_inc(sem("seq_t"), 1)
            pe.wait_ge(sem("seq_odd"), 6)
            pe.wait_ge(sem("seq_even"), 6)
            pe.wait_ge(sem("ld_dftz"), 16)
            for b in range(4):
                q = b % 2
                cut = slice(q * 512, (q + 1) * 512)
                if b:
                    pe.wait_ge(sem("spec_ready"), 4 * b)
                    pe.wait_ge(sem("conv_step"), 2 * b)
                for n in (0, 2, 1, 3):
                    for lt in range(TH):
                        ins = mm(ps[:, n, :], dftz[:, n // 2, lt, (n % 2) * P:(n % 2 + 1) * P], seq[:, 0, lt, cut],
                                 lt == 0, lt == 1)
                    ins.then_inc(sem("spec_mm"), 1)
                for lt in range(TH):
                    for n in (0, 2, 1, 3):
                        if lt == 0:
                            pe.wait_ge(sem("spec_ready"), 4 * b + (1, 3, 2, 4)[n])
                        ins = mm(ps[:, 4 + lt, :], dftz[:, 2 + n // 2, n % 2, lt * P:(lt + 1) * P], yr[:, n, :], n == 0, n == 3)
                    ins.then_inc(sem("inv_mm"), 1)
            pe.wait_ge(sem("conv_step"), 8)
            for c in range(8):
                if c >= 4:
                    pe.wait_ge(sem("yhy_split"), c - 3)
                for h in range(TH):
                    ins = pe.transpose(ps[:, c % 4, h * P:(h + 1) * P], seq[:, 0, h, c * P:(c + 1) * P], ident)
                ins.then_inc(sem("yhy_t"), 1)
            pe.wait_ge(sem("yhy_split"), 8)
            fm_phase("sgu_u", lambda i, s: pe.wait_ge(sem("u_out"), 4 * i + (s + 1)))
            phase("sgu_v", lambda g, i, k: token_major(k, (k // 2) % 4, 4, 4 + 2 * (k // 8), H), per_iter=2)
            pe.wait_ge(sem("v_normed"), 2)
            pe.wait_ge(sem("u_out"), 4 + 8)
            for h in range(8):
                if h >= 4:
                    pe.wait_ge(sem("ysgu_f"), h - 3)
                for n in range(TH):
                    o = ps[:, h % 4, n * P:(n + 1) * P]
                    mm(o, vg[:, n, h * P:(h + 1) * P], wsT[:, h, :], True, False)
                    ins = mm(o, ones[0:1, :], bs[0:1, h, :], False, True)
                ins.then_inc(sem("spatial_mm"), 1)
            pe.wait_ge(sem("ysgu_lo"), 8)
            def branch(name, first_chunk, credit):
                def step(g, i, k):
                    pe.wait_ge(sem(credit), 8 * i + (k + 1))
                    for j in range(8):
                        ins = three(ps[:, k % 4, 0:T], w(k, j * P, P), R(first_chunk + j), j == 0, j == 7)
                    return ins
                phase(name, step)
            fm_phase("gate_hy", lambda i, s: pe.wait_ge(sem("sg1_out"), 4 * i + (s + 1)))
            pe.wait_ge(sem("sg1_out"), 4 + 16)
            branch("branch_hy", 0, "bhy_out")
            pe.wait_ge(sem("bhy_out"), 4 + 16)
            fm_phase("gate_sgu", lambda i, s: pe.wait_ge(sem("sg2_out"), 4 * i + (s + 1)))
            pe.wait_ge(sem("sg2_out"), 4 + 16)
            branch("branch_sgu", 8, "merged_f")
            pe.wait_ge(sem("merged_lo"), 16)
            column_blocks("out2", 4, 4, H)
            turn("hf")
            pe.wait_ge(sem("norm_lo"), norm_count("hf", "lo", 4))
            for part in range(3):
                n0 = sum(FFN_TILES[:part])

                def pair_free(i, s, n0=n0):
                    if s % 2 == 0:
                        pe.wait_ge(sem("ffn_pair"), 2 * i + (n0 + s // 2 + 1))
                fm_phase(f"ffn_in{part}", pair_free)
                column_blocks(f"ffn_down{part}", 8 + 4 * part, FFN_TILES[part] // 4, R, n0)


def _layout(a):
    c = np.ascontiguousarray
    lay = lambda v: v.reshape(-1, P).T

    def fm(w):
        return [w[:, j:j + P].reshape(DC, P, P).transpose(1, 0, 2).reshape(P, UNIT) for j in range(0, w.shape[1], P)]

    def rows(w):
        return [w[:, j:j + P].T for j in range(0, w.shape[1], P)]

    def tm(w):
        return [w[r:r + 512, j:j + 512].reshape(4, P, 512).transpose(1, 0, 2).reshape(P, UNIT)
                for j in range(0, w.shape[1], 512) for r in range(0, w.shape[0], 512)]

    def br(w):
        return [w[:, j:j + 2 * P].reshape(8, P, 2, P).transpose(1, 2, 0, 3).reshape(P, UNIT) for j in range(0, w.shape[1], 2 * P)]

    win = a["w_in"][0]
    o = np.cumsum([0, 512, 512, 512, 512, 128, 128, 512, 512, 512, 512, 128, 128, 128, 128, 128, 128, 24])
    sec = [win[:, o[i]:o[i + 1]] for i in range(17)]
    mod_units = rows(a["ada_w"][0])
    units = mod_units[:ADA_UNITS] + fm(sec[0]) + fm(sec[1]) + tm(sec[2]) + fm(sec[6]) + fm(sec[7]) + tm(sec[8]) + fm(sec[3])
    for i in (4, 10, 11, 12, 14, 5, 13, 15):
        units += fm(sec[i])
    units += fm(sec[9]) + tm(a["w_out"][0])
    for e in range(N_EXP):
        g, u = fm(a["exp_w_gate"][0, e]), fm(a["exp_w_up"][0, e])
        units += [t for pair in zip(g, u) for t in pair] + tm(a["exp_w_down"][0, e])
    w2 = a["w_in_2"][0]
    units += fm(w2[:, 0:3072]) + fm(w2[:, 3072:4096]) + tm(w2[:, 4096:5120])
    units += fm(w2[:, 5120:7168]) + br(a["w_branch_hyena_2"][0]) + fm(w2[:, 7168:9216]) + br(a["w_branch_sgu_2"][0])
    units += tm(a["w_out_2"][0])
    fi, fo = a["w_ffn_in_2"][0], a["w_ffn_out_2"][0]
    n0 = 0
    for n in FFN_TILES:
        g, u = fm(fi[:, n0 * P:(n0 + n) * P]), fm(fi[:, DF + n0 * P:DF + (n0 + n) * P])
        units += [t for pair in zip(g, u) for t in pair] + tm(fo[n0 * P:(n0 + n) * P])
        n0 += n
    stream = np.stack(units)
    late = np.stack(mod_units[ADA_UNITS:])
    del units, mod_units

    cols = np.zeros((P, NCOLS), np.float32)

    def put(name, v):
        cols[0:v.shape[0], COLS[name]:COLS[name] + v.shape[1]] = v
    for name, key in (("norm1", "norm1_g"), ("norm2", "norm2_g"), ("mixg", "mix_norm_g"),
                      ("normmix2", "norm_mix_g_2"), ("normffn2", "norm_ffn_g_2"), ("ada_b", "ada_b"),
                      ("conv_w", "short_conv_w_2"), ("conv_b", "short_conv_b_2")):
        put(name, lay(a[key]))
    put("fb", np.stack([a["filt_b1_2"][0], a["filt_b2_2"][0], a["filt_b3_2"][0]], 1))
    put("ffreq", a["filt_freq_2"][0][:, None])
    d = dict(shape_tables(), stream=stream, mod_units=late, cols=cols, x=a["x"][0], c_row=a["c"].reshape(-1), rel_bias=a["rel_bias"])
    d["w_gate_nsa"] = sec[16].reshape(DC, P, 24).transpose(1, 0, 2)
    d["router_w"] = a["router_w"].reshape(DC, P, N_EXP).transpose(1, 0, 2)
    d["router_bias"], d["sinks"], d["final_g"], d["norm_final_g"] = a["router_bias"], a["sinks"][0], a["final_g"], a["norm_final_g_2"]
    for n in (1, 2, 3):
        d[f"filt_w{n}"] = a[f"filt_w{n}_2"][0]
    d["filt_w4"] = a["filt_w4_2"][0].reshape(64, 2, 2, 2, 512).transpose(2, 3, 0, 1, 4).reshape(4, 64, 1024)
    d["hyena_bias"] = a["hyena_bias_2"][0].reshape(4, 512)
    cmp1 = lambda v: v.reshape(16, P, P).transpose(1, 0, 2)
    d["w1k"], d["w1v"] = cmp1(a["nsa_cmp_w1_k"][0]), cmp1(a["nsa_cmp_w1_v"][0])
    d["w2kv"] = np.stack([a["nsa_cmp_w2_k"][0], a["nsa_cmp_w2_v"][0]], 1)
    d["pe"] = np.stack([a["nsa_pe_k"][0].T, a["nsa_pe_v"][0].T], 1)
    d["ln_g"], d["ln_b"] = a["sgu_ln_g_2"][0], a["sgu_ln_b_2"][0]
    d["w_s"] = a["sgu_w_s_2"][0].transpose(2, 0, 1)
    d["b_s"] = a["sgu_b_s_2"][0].reshape(1, 1024)
    return {k: c(v) for k, v in d.items()}


def kernel(**inputs):
    import concourse.bacc as bacc
    from concourse.bass_utils import run_bass_kernel_spmd as run

    nc = bacc.Bacc("TRN2", target_bir_lowering=False, num_devices=1)
    arrays = _layout({k: np.asarray(v) for k, v in inputs.items()})
    d = {k: nc.dram_tensor(f"in_{k}", v.shape, F32, kind="ExternalInput").ap() for k, v in arrays.items()}
    out = nc.dram_tensor("y", (1, T, D), F32, kind="ExternalOutput").ap()
    two_blocks(nc, d, out)
    r = run(nc, [{f"in_{k}": v for k, v in arrays.items()}], core_ids=[0])
    return r.results[0]["y"]
```
